# Optimizing a Trainium2 kernel written in Bass

```python
import math
import jax, jax.numpy as jnp
from jax import lax
import numpy as np

D_MODEL = 1024
BATCH = 1
SEQ = 1024
DEPTH = 1
DEC_BATCH = 1
DEC_SEQ = 512
PAST_LEN = 128

EPS = 1e-6
HEAD_DIM = 64
ATTN_GROUPS = ((128, 1), (512, 4), (2048, 16))
N_GROUPS = 3
HEADS_PER_GROUP = D_MODEL // 128
N_ATTN_HEADS = N_GROUPS * HEADS_PER_GROUP
ATTN_QKV_WIDTH = N_ATTN_HEADS * HEAD_DIM
ATTN_WIDTH = HEADS_PER_GROUP * HEAD_DIM
HYENA_WIDTH = D_MODEL
HYENA_ORDER = 2
SHORT_CONV = 3
FILTER_EMB = 33
N_BANDS = (FILTER_EMB - 1) // 2
FILTER_HIDDEN = 64
DECAY_TARGET = 1e-2
FAST_DECAY_PCT = 0.3
SLOW_DECAY_PCT = 1.5
NUM_BUCKETS = 32
MAX_DISTANCE = 1024
NEG_INF = -1e30
IN_SIZES = (ATTN_QKV_WIDTH, ATTN_QKV_WIDTH, ATTN_QKV_WIDTH, ATTN_WIDTH, 3 * HYENA_WIDTH, HYENA_WIDTH, 2 * D_MODEL)
IN_WIDTH = 3 * ATTN_QKV_WIDTH + ATTN_WIDTH + 4 * HYENA_WIDTH + 2 * D_MODEL

kernel_name = 'hybrid_dilated_attn_hyena_encoder'

def _split_points():
    return [int(c) for c in np.cumsum(IN_SIZES)[:-1]]

def _rms_norm(x, g):
    xf = x.astype(jnp.float32)
    y = xf * lax.rsqrt(jnp.mean(xf * xf, axis=-1, keepdims=True) + EPS)
    return (y * g.astype(jnp.float32)).astype(x.dtype)

def _t5_bucket(rel):
    half = NUM_BUCKETS // 2
    max_exact = half // 2
    n = jnp.abs(rel)
    nf = jnp.maximum(n, 1).astype(jnp.float32)
    large = max_exact + (jnp.log(nf / max_exact) / math.log(MAX_DISTANCE / max_exact) * (half - max_exact)).astype(jnp.int32)
    large = jnp.minimum(large, half - 1)
    return jnp.where(rel > 0, half, 0) + jnp.where(n < max_exact, n, large)

def _dilated_window_attention(q, k, v, bias_table, window, dilation):
    b, s, h, hd = q.shape
    r = dilation
    blk = window // (2 * dilation)
    lr = s // r
    nb = -(-lr // blk)
    lp = nb * blk

    def to_sub(t):
        t = t.reshape(b, lr, r, h, hd).transpose(0, 2, 1, 3, 4)
        return jnp.pad(t, ((0, 0), (0, 0), (0, lp - lr), (0, 0), (0, 0)))

    def neighbours(t):
        t = jnp.pad(t, ((0, 0), (0, 0), (blk, blk), (0, 0), (0, 0))).reshape(b, r, nb + 2, blk, h, hd)
        return jnp.concatenate([t[:, :, :-2], t[:, :, 1:-1], t[:, :, 2:]], axis=3)

    qb = to_sub(q).reshape(b, r, nb, blk, h, hd).astype(jnp.float32)
    kb = neighbours(to_sub(k)).astype(jnp.float32)
    vb = neighbours(to_sub(v)).astype(jnp.float32)
    qi = jnp.arange(blk)[:, None]
    kj = jnp.arange(3 * blk)[None, :] - blk
    delta = kj - qi
    bias = bias_table.astype(jnp.float32)[_t5_bucket(delta * r)].transpose(2, 0, 1)
    key_sub = jnp.arange(nb)[:, None, None] * blk + kj[None]
    valid = (jnp.abs(delta) <= blk)[None] & (key_sub >= 0) & (key_sub < lr)
    logits = jnp.einsum('brnqhd,brnkhd->brnhqk', qb, kb) * (hd ** -0.5) + bias
    logits = jnp.where(valid[:, None], logits, NEG_INF)
    m = jnp.max(logits, axis=-1, keepdims=True)
    p = jnp.exp(logits - m)
    den = jnp.sum(p, axis=-1)
    o = jnp.einsum('brnhqk,brnkhd->brnqhd', p, vb) / jnp.swapaxes(den, -1, -2)[..., None]
    lse = m[..., 0] + jnp.log(den)
    o = o.reshape(b, r, lp, h, hd)[:, :, :lr].transpose(0, 2, 1, 3, 4).reshape(b, s, h, hd)
    lse = jnp.swapaxes(lse, -1, -2).reshape(b, r, lp, h)[:, :, :lr].transpose(0, 2, 1, 3).reshape(b, s, h)
    return o, lse

def _hyena_filters(length, w1, b1, w2, b2, w3, b3, w4, freq):
    f32 = jnp.float32
    t = jnp.linspace(0.0, 1.0, length, dtype=f32)[:, None]
    ang = (2.0 * math.pi / length) * jnp.arange(length, dtype=f32)[:, None]
    bands = jnp.linspace(1e-4, N_BANDS - 1, N_BANDS, dtype=f32)[None]
    z = jnp.concatenate([t, jnp.cos(ang * bands), -jnp.sin(ang * bands)], axis=-1)
    fr = freq.astype(f32)
    hdn = jnp.sin(fr * (z @ w1.astype(f32) + b1.astype(f32)))
    hdn = jnp.sin(fr * (hdn @ w2.astype(f32) + b2.astype(f32)))
    hdn = jnp.sin(fr * (hdn @ w3.astype(f32) + b3.astype(f32)))
    filt = hdn @ w4.astype(f32)
    max_decay = math.log(DECAY_TARGET) / FAST_DECAY_PCT
    min_decay = math.log(DECAY_TARGET) / SLOW_DECAY_PCT
    deltas = jnp.abs(jnp.linspace(min_decay, max_decay, HYENA_WIDTH, dtype=f32))
    decay = jnp.exp(-t * deltas[None])
    return filt.reshape(length, HYENA_ORDER, 2, HYENA_WIDTH) * decay[:, None, None]

def _long_conv(z, h_fwd, h_bwd, skip):
    length = z.shape[1]
    c = z.shape[-1]
    kcirc = jnp.concatenate([h_fwd, jnp.zeros((1, c), jnp.float32), h_bwd[:0:-1]], axis=0)
    zf = z.astype(jnp.float32)
    spec = jnp.fft.rfft(zf, n=2 * length, axis=1) * jnp.fft.rfft(kcirc, axis=0)[None]
    y = jnp.fft.irfft(spec, n=2 * length, axis=1)[:, :length]
    return y + zf * skip.astype(jnp.float32)

def _layer(x, rel_bias, pre_g, post_g, w_in, conv_w, conv_b, fw1, fb1, fw2, fb2, fw3, fb3, fw4, ffreq, skip, w_br_a, w_br_h, w_out):
    b, s, _ = x.shape
    f32 = jnp.float32
    hn = _rms_norm(x, pre_g)
    proj = jnp.einsum('bsd,de->bse', hn, w_in)
    q, k, v, gate_a, u_hy, gate_h, merge = jnp.split(proj, _split_points(), axis=-1)
    q = q.reshape(b, s, N_GROUPS, HEADS_PER_GROUP, HEAD_DIM)
    k = k.reshape(b, s, N_GROUPS, HEADS_PER_GROUP, HEAD_DIM)
    v = v.reshape(b, s, N_GROUPS, HEADS_PER_GROUP, HEAD_DIM)

    outs, lses = [], []
    for g, (window, dilation) in enumerate(ATTN_GROUPS):
        o_g, lse_g = _dilated_window_attention(q[:, :, g], k[:, :, g], v[:, :, g], rel_bias[:, g * HEADS_PER_GROUP:(g + 1) * HEADS_PER_GROUP], window, dilation)
        outs.append(o_g)
        lses.append(lse_g)
    wts = jax.nn.softmax(jnp.stack(lses), axis=0)
    attn = jnp.einsum('gbsh,gbshd->bshd', wts, jnp.stack(outs)).reshape(b, s, ATTN_WIDTH).astype(x.dtype)
    attn_branch = jnp.einsum('bse,ed->bsd', attn * jax.nn.silu(gate_a), w_br_a)

    up = jnp.pad(u_hy, ((0, 0), (1, 1), (0, 0)))
    u_c = up[:, :-2] * conv_w[0] + up[:, 1:-1] * conv_w[1] + up[:, 2:] * conv_w[2] + conv_b
    hv, hx1, hx2 = jnp.split(u_c, 3, axis=-1)
    filt = _hyena_filters(s, fw1, fb1, fw2, fb2, fw3, fb3, fw4, ffreq)
    zz = hx1.astype(f32) * _long_conv(hv, filt[:, 0, 0], filt[:, 0, 1], skip[0])
    zz = hx2.astype(f32) * _long_conv(zz, filt[:, 1, 0], filt[:, 1, 1], skip[1])
    hy = zz.astype(x.dtype)
    hy_branch = jnp.einsum('bse,ed->bsd', hy * jax.nn.silu(gate_h), w_br_h)

    g_a, g_h = jnp.split(merge, 2, axis=-1)
    merged = jax.nn.sigmoid(g_a) * attn_branch + jax.nn.sigmoid(g_h) * hy_branch
    out = jnp.einsum('bsd,de->bse', merged, w_out)
    return x + _rms_norm(out, post_g)

def setup_inputs(seed: int = 0) -> dict:
    key = jax.random.key(seed)
    ks = jax.random.split(key, 20)

    def nrm(k, shape, scale):
        return scale * jax.random.normal(k, shape, jnp.float32)

    D, L = D_MODEL, DEPTH
    return {
        'x_prompt': nrm(ks[0], (BATCH, SEQ, D), 1.0),
        'x_sample': nrm(ks[1], (DEC_BATCH, DEC_SEQ, D), 1.0),
        'rel_bias': nrm(ks[2], (NUM_BUCKETS, N_ATTN_HEADS), 0.2),
        'pre_norm_g': 1.0 + nrm(ks[3], (L, D), 0.1),
        'post_norm_g': 1.0 + nrm(ks[4], (L, D), 0.1),
        'w_in': nrm(ks[5], (L, D, IN_WIDTH), D ** -0.5),
        'conv_w': nrm(ks[6], (L, SHORT_CONV, 3 * HYENA_WIDTH), SHORT_CONV ** -0.5),
        'conv_b': nrm(ks[7], (L, 3 * HYENA_WIDTH), 0.02),
        'filt_w1': nrm(ks[8], (L, FILTER_EMB, FILTER_HIDDEN), FILTER_EMB ** -0.5),
        'filt_b1': nrm(ks[9], (L, FILTER_HIDDEN), 0.1),
        'filt_w2': nrm(ks[10], (L, FILTER_HIDDEN, FILTER_HIDDEN), FILTER_HIDDEN ** -0.5),
        'filt_b2': nrm(ks[11], (L, FILTER_HIDDEN), 0.1),
        'filt_w3': nrm(ks[12], (L, FILTER_HIDDEN, FILTER_HIDDEN), FILTER_HIDDEN ** -0.5),
        'filt_b3': nrm(ks[13], (L, FILTER_HIDDEN), 0.1),
        'filt_w4': nrm(ks[14], (L, FILTER_HIDDEN, HYENA_ORDER * 2 * HYENA_WIDTH), 0.05 * FILTER_HIDDEN ** -0.5),
        'filt_freq': 1.0 + nrm(ks[15], (L, FILTER_HIDDEN), 0.1),
        'hyena_skip': nrm(ks[16], (L, HYENA_ORDER, HYENA_WIDTH), 1.0),
        'w_branch_a': nrm(ks[17], (L, ATTN_WIDTH, D), ATTN_WIDTH ** -0.5),
        'w_branch_h': nrm(ks[18], (L, HYENA_WIDTH, D), HYENA_WIDTH ** -0.5),
        'w_out': nrm(ks[19], (L, D, D), D ** -0.5),
    }

def reference(x_prompt, x_sample, rel_bias, pre_norm_g, post_norm_g, w_in, conv_w, conv_b, filt_w1, filt_b1, filt_w2, filt_b2, filt_w3, filt_b3, filt_w4, filt_freq, hyena_skip, w_branch_a, w_branch_h, w_out):
    def run(x):
        for l in range(DEPTH):
            x = _layer(x, rel_bias, pre_norm_g[l], post_norm_g[l], w_in[l], conv_w[l], conv_b[l], filt_w1[l], filt_b1[l], filt_w2[l], filt_b2[l], filt_w3[l], filt_b3[l], filt_w4[l], filt_freq[l], hyena_skip[l], w_branch_a[l], w_branch_h[l], w_out[l])
        return x

    y_prompt = run(x_prompt)
    y_sample = run(x_sample)
    return (y_prompt, y_sample)


_drawn_inputs = setup_inputs


def setup_inputs(seed=0):
    import zlib

    import numpy as np

    out = dict(_drawn_inputs(seed))
    spreads = {}
    factors = {'rel_bias': 2.904}
    for name, (base, spread) in spreads.items():
        noise = np.random.default_rng([zlib.crc32(name.encode()), seed]).standard_normal(out[name].shape)
        drawn = base * np.exp(spread * noise) if base else spread * noise
        out[name] = __import__('jax').numpy.asarray(drawn.astype(out[name].dtype))
    for name, factor in factors.items():
        out[name] = (out[name] * factor).astype(out[name].dtype)
    return out
```

```python
import math
from contextlib import ExitStack

import numpy as np

import concourse.bass as bass
import concourse.mybir as mybir

ALU = mybir.AluOpType
ACT = mybir.ActivationFunctionType
AX = mybir.AxisListType
F32 = mybir.dt.float32

P = 128
D = 1024
KD = D // P
SP, SS = 1024, 512
T = SP + SS
NT = T // P
BANK = 512
HD = 64
HEADS = 8
GROUPS = ((128, 1), (512, 4), (2048, 16))
QKV = len(GROUPS) * HEADS * HD
AW = HEADS * HD
BLK = 64
NEG = -1e30
NBUCK = 32
MAXDIST = 1024
FEMB, FHID = 33, 64
EPS = 1e-6
OFF_GA = 3 * QKV
OFF_U = OFF_GA + AW
OFF_GH = OFF_U + 3 * D
OFF_MG = OFF_GH + D
INW = OFF_MG + 2 * D

PADC = BLK
COL_P = PADC
COL_S = PADC + SP + PADC
HC = COL_S + SS + PADC
SPANS = (COL_P, COL_P + BANK, COL_S)

FQ = 256
NQ = D // FQ
RAD = 8

BW = 3 * P
BROW = 2 * 2 * P - 1


def bucket(rel):
    half = NBUCK // 2
    exact = half // 2
    n = np.abs(rel)
    nf = np.maximum(n, 1).astype(np.float32)
    large = exact + (np.log(nf / np.float32(exact)) / np.float32(math.log(MAXDIST / exact)) * (half - exact)).astype(np.int32)
    return np.where(rel > 0, half, 0) + np.where(n < exact, n, np.minimum(large, half - 1))


def stride(g, seq):
    return min(GROUPS[g][1], (SP, SS)[seq] // P)


def bias_tables():
    hot = np.zeros((NBUCK, 3 * BANK), np.float32)
    mask = np.zeros((HEADS, 3 * BANK), np.float32)
    for g, seq, col, reach in ((0, 0, 0, BROW // 2), (1, 0, 0, BROW // 2), (2, 0, 0, P - 1), (2, 1, 2 * P - 1, P - 1)):
        dilation, r = GROUPS[g][1], stride(g, seq)
        for i, apart in enumerate(range(-reach, reach + 1)):
            if apart * r % dilation == 0 and abs(apart * r) <= BLK * dilation:
                hot[bucket(np.array(apart * r)), g * BANK + col + i] = 1.0
            else:
                mask[:, g * BANK + col + i] = NEG
    return hot, mask


def filter_features(length):
    f = np.float32
    t = np.linspace(0.0, 1.0, length, dtype=f)[:, None]
    ang = f(2.0 * math.pi / length) * np.arange(length, dtype=f)[:, None]
    bands = np.linspace(1e-4, (FEMB - 1) // 2 - 1, (FEMB - 1) // 2, dtype=f)[None]
    return np.concatenate([t, np.cos(ang * bands), -np.sin(ang * bands)], axis=-1).astype(f).T


def decay_table(length):
    t = np.linspace(0.0, 1.0, length, dtype=np.float32)[:, None].astype(np.float64)
    deltas = np.abs(np.linspace(math.log(1e-2) / 1.5, math.log(1e-2) / 0.3, D, dtype=np.float32)).astype(np.float64)
    dec = np.exp(-t * deltas[None])
    first = dec[0:P].copy()
    first[0] = 0.0
    return np.concatenate([dec, first]).astype(np.float32)


A0, A4, A1R, A1N, A2R, A2N, A3R, A3I = range(8)


def dft(L):
    n = 2 * L
    w = n // RAD
    nc = w // P
    n2 = np.arange(w)
    fwd, inv, pairs = [], [], []
    units = [[], [], [], []]

    def add(m):
        fwd.append(m)
        return len(fwd) - 1

    def addi(m):
        inv.append(m)
        return sum(x.shape[1] for x in inv[:-1])

    def ang(c, ks):
        return 2 * np.pi * (np.outer(n2[c * P:(c + 1) * P], ks) % n) / n

    def iang(ks):
        return 2 * np.pi * (np.outer(ks, n2) % n) / n

    def weight(ks):
        return np.where((ks == 0) | (ks == L), 1.0, 2.0)[:, None] / n

    def cat(a, b):
        return np.concatenate([a, b], axis=1)

    nyq = np.cos(np.pi * (n2 % 2))
    if nc == 2:
        k0, k4 = 8 * np.arange(P), 4 + 8 * np.arange(P)
        re, im, imk, rek = [], [], [], []
        for c in range(nc):
            co, si = np.cos(ang(c, k0)), -np.sin(ang(c, k0))
            sz, cy = si.copy(), co.copy()
            sz[:, 0] = cy[:, 0] = nyq[c * P:(c + 1) * P]
            re.append((A0, c, add(co)))
            im.append((A0, c, add(sz)))
            imk.append((A0, c, add(si)))
            rek.append((A0, c, add(cy)))
        pairs.append((re, im, imk, rek))
        re = [(A4, c, add(np.cos(ang(c, k4)))) for c in range(nc)]
        im = [(A4, c, add(-np.sin(ang(c, k4)))) for c in range(nc)]
        pairs.append((re, im, im, re))
        r, s = np.cos(iang(k0)) * weight(k0), -np.sin(iang(k0)) * weight(k0)
        s[0] = nyq / n
        units[0] += [(0, 0, addi(r), 0, w), (0, 1, addi(s), 0, w)]
        units[0] += [(1, 0, addi(np.cos(iang(k4)) * weight(k4)), w, w), (1, 1, addi(-np.sin(iang(k4)) * weight(k4)), w, w)]
    else:
        h = P // 2
        k0, k4 = 8 * np.arange(h), 4 + 8 * np.arange(h)
        z, zi = np.zeros((P, h)), np.zeros((h, w))
        co, si = np.cos(ang(0, k0)), -np.sin(ang(0, k0))
        sz, cy = si.copy(), co.copy()
        sz[:, 0] = cy[:, 0] = nyq
        c4, s4 = (A4, 0, add(cat(z, np.cos(ang(0, k4))))), (A4, 0, add(cat(z, -np.sin(ang(0, k4)))))
        pairs.append(([(A0, 0, add(cat(co, z))), c4], [(A0, 0, add(cat(sz, z))), s4],
                      [(A0, 0, add(cat(si, z))), s4], [(A0, 0, add(cat(cy, z))), c4]))
        s0 = -np.sin(iang(k0)) * weight(k0)
        s0[0] = nyq / n
        r = np.concatenate([cat(np.cos(iang(k0)) * weight(k0), zi), cat(zi, np.cos(iang(k4)) * weight(k4))])
        s = np.concatenate([cat(s0, zi), cat(zi, -np.sin(iang(k4)) * weight(k4))])
        units[0] += [(0, 0, addi(r), 0, 2 * w), (0, 1, addi(s), 0, 2 * w)]
    for k1, (ar, ai, negated) in enumerate(((A1R, A1N, True), (A2R, A2N, True), (A3R, A3I, False)), 1):
        for m in range(nc):
            ks = k1 + 8 * (np.arange(P) + m * P)
            re, im = [], []
            for c in range(nc):
                co, si = np.cos(ang(c, ks)), np.sin(ang(c, ks))
                ico, ins = add(co), add(-si)
                if negated:
                    re += [(ar, c, ico), (ai, c, ins)]
                    im += [(ar, c, ins), (ai, c, add(-co))]
                else:
                    re += [(ar, c, ico), (ai, c, add(si))]
                    im += [(ar, c, ins), (ai, c, ico)]
            pairs.append((re, im, im, re))
            co, si = np.cos(iang(ks)) * weight(ks), np.sin(iang(ks)) * weight(ks)
            col = addi(np.concatenate([-si, co, si], axis=1))
            units[k1] += [(len(pairs) - 1, 0, col + w, 0, 2 * w), (len(pairs) - 1, 1, col, 0, 2 * w)]
    return {"fwd": np.stack(fwd, axis=1).astype(np.float32).reshape(P, -1),
            "inv": np.concatenate(inv, axis=1).astype(np.float32), "pairs": pairs, "units": units, "w": w, "nc": nc}


DFTS = (dft(SP), dft(SS))
LENS = (SP, SS)
TOK0 = (0, SP)
UC_W = SP + 1 + SS
UC0 = (0, SP + 1)


def constants():
    hot, mask = bias_tables()
    c = {"hot": hot, "mask": mask,
         "feat": np.concatenate([filter_features(SP), filter_features(SS)], axis=1),
         "dec0": decay_table(SP), "dec1": decay_table(SS)}
    for s in range(2):
        c[f"fwd{s}"] = DFTS[s]["fwd"]
        c[f"inv{s}"] = DFTS[s]["inv"]
    c["ident"] = np.eye(P, dtype=np.float32)
    return {k: np.ascontiguousarray(v) for k, v in c.items()}


def windows(g, t):
    if g == 0:
        u = t if t < SP // P else t - SP // P
        last = u == (SP // P if t < SP // P else SS // P) - 1
        k0 = P * t if t < SP // P else COL_S - PADC + P * u
        v0 = t if t < SP // P else SP // P + 1 + u
        return k0, 2 * P, P // 2, [v0, v0 + 1], (0, BLK) if u == 0 else (3 * BLK, 4 * BLK) if last else None
    if g == 1:
        if t < SP // P:
            r, half = t // 2, t % 2
            return 2 * P * r, 2 * P, P - P * half, [2 * r, 2 * r + 1], None
        return P * t, P, P, [t], None
    return P * t, P, (0 if t < SP // P else P), [t], None


def value_tiles(g, hn):
    out = []
    if g == 0:
        out = [(lambda k, c=P * m: hn[:, k, c:c + P]) for m in range(SP // P + 1)]
        out += [(lambda k, c=COL_S - PADC + P * m: hn[:, k, c:c + P]) for m in range(SS // P + 1)]
        return out
    for seq, c0, n in ((0, COL_P, SP), (1, COL_S, SS)):
        r = stride(g, seq)
        for m in range(n // P):
            a = c0 + m * P // (n // r) + r * (m * P % (n // r))
            out.append(lambda k, a=a, r=r: hn[:, k, a:a + r * (P - 1) + 1:r])
    return out


def build(nc, ins, cst, y_p, y_s):
    dram = {}
    for name, shape in (("uc", [3 * KD, P, UC_W]), ("og", [3, T, AW + 2 * HEADS]), ("hy", [KD, P, T]),
                        ("hn", [P, KD * HC]), ("brow", [HEADS, P, 3 * BANK])):
        dram[name] = nc.dram_tensor("s_" + name, shape, F32, kind="Internal")
    uc_d, og_d, hy_d, hn_d, brow_d = (dram[n].ap() for n in ("uc", "og", "hy", "hn", "brow"))
    w_in, w_a, w_h, w_o = ins["w_in"][0], ins["w_branch_a"][0], ins["w_branch_h"][0], ins["w_out"][0]

    with ExitStack() as ctx:
        def sem(name):
            return ctx.enter_context(nc.semaphore(name))

        ARENA = 53200
        mem = ctx.enter_context(nc.sbuf_tensor("mem", [P, ARENA], F32))
        ps = ctx.enter_context(nc.psum_tensor("ps", [P, 8, BANK], F32))

        top = [0]

        def part(n, at=None):
            if at is not None:
                top[0] = at
            a = top[0]
            top[0] += n
            assert top[0] <= ARENA, (top[0], ARENA)
            return mem[:, a:a + n]

        def grid(n, m, at=None):
            return part(n * m, at).rearrange("p (n m) -> p n m", n=n)

        ident = part(P)
        cols = part(P)
        fcol = part(8)
        small = part(96)
        BASE = top[0]
        CW, CB, CG, CS = 0, 9 * KD, 12 * KD, 13 * KD
        NCOLS = 15 * KD
        ssq, rstd = small[:, 0:NT], small[:, NT:2 * NT]
        ssq2, rstd2 = small[:, 2 * NT:3 * NT], small[:, 3 * NT:4 * NT]
        H3_AT = ARENA - T
        h3 = part(T, H3_AT)

        hn = grid(KD, HC, BASE)
        ring = [grid(KD, BANK) for _ in range(2)]
        EARLY = top[0]
        xt = grid(NT, D)
        rows = part(P)
        frows = part(FHID)
        ub = [part(UC_W + 2) for _ in range(2)]
        ut = [part(UC_W) for _ in range(3)]
        junk = [ut[i][:, 0:D] for i in range(2)]
        feat = part(T)
        fw = part(3 * FHID)
        hid = part(T)
        fk = part(BANK)
        fv = part(BANK)
        hot = part(3 * BANK)
        mask = part(3 * BANK)
        assert top[0] <= H3_AT

        qt = grid(4, T, EARLY)
        kt = grid(4, HC)
        vt = grid(14, AW)
        bw = part(HEADS * BW)
        bwt = bw.rearrange("p (h c) -> p h c", h=HEADS)
        b2t = bw[:, 0:HEADS * 2 * P].rearrange("p (h c) -> p h c", h=HEADS)
        lg = [part(2 * P) for _ in range(3)]
        pr = [part(2 * P) for _ in range(3)]
        pt = [part(2 * P) for _ in range(3)]
        ot = [part(AW + 2 * HEADS) for _ in range(2)]
        relb = small[:, 4 * NT:4 * NT + 3 * HEADS]
        assert top[0] <= H3_AT

        w4 = [part(2 * FQ, BASE), part(2 * FQ)]
        ftab = part(DFTS[0]["fwd"].shape[1])
        itab = part(DFTS[0]["inv"].shape[1])
        dec = grid(SP // P + 1, FQ)
        tge, tgo, tz = (grid(SP // P, FQ) for _ in range(3))
        fa = [grid(8, 2 * FQ) for _ in range(2)]
        kf = grid(8, 3 * FQ)
        yf = grid(8, 2 * FQ)
        hfb = [part(2 * FQ) for _ in range(2)]
        pq = [part(4 * FQ) for _ in range(2)]
        iv_u, iv_v, iv_a, iv_b = pq[0][:, 0:BANK], pq[0][:, BANK:], pq[1][:, 0:BANK], pq[1][:, BANK:]
        zc = grid(2, SP)
        hx = grid(2, SP)
        yo = part(SP)
        e01 = grid(2, 2 * FQ)
        iv0 = [part(BANK) for _ in range(2)]
        iv1 = [part(BANK) for _ in range(2)]
        assert top[0] <= H3_AT, (top[0], H3_AT)

        hm = grid(KD, HC, BASE)
        mt = grid(KD, T)
        hg = grid(KD, T)
        ga, at = hg[:, 0:4, :], hg[:, 4:8, :]
        mring = [grid(KD, BANK) for _ in range(3)]
        sg = [part(BANK) for _ in range(2)]
        gated = [part(BANK) for _ in range(2)]
        ogt = [mem[:, BASE + KD * HC + i * 3 * (AW + 2 * HEADS):BASE + KD * HC + (i + 1) * 3 * (AW + 2 * HEADS)].rearrange(
            "p (g c) -> p g c", g=3) for i in range(2)]
        GSC = BASE + KD * HC + 6 * (AW + 2 * HEADS)
        wts = [mem[:, GSC + 64 * i:GSC + 64 * i + 64] for i in range(2)]
        cmb = [mem[:, GSC + 128 + 2 * AW * i:GSC + 128 + 2 * AW * (i + 1)].rearrange("p (a c) -> p a c", a=2) for i in range(2)]
        gpost = mem[:, BASE:BASE + D]
        xres = [mem[:, BASE + D * (1 + i):BASE + D * (2 + i)] for i in range(2)]
        yout = [mem[:, BASE + D * (3 + i):BASE + D * (4 + i)] for i in range(2)]
        osq = mem[:, BASE + 5 * D:BASE + 6 * D]

        names = """ld_small ld_tabs ld_gain dve_steps ld_w0 ld_w1 w_used rows_T cols_ok fcols_ok pads_ok
            n_sq n_mean n_root n_rstd n_scaled n_T n_evA n_evD hn_saved
            u_ready u_evac u_mid u_tap u_conv h_mm h_arg h_k h_r1 h_r2 h_sin b_mm b_rows b_stored
            bw_ld0 bw_ld1 bw_ld2
            a_ready a_evac a_score a_biased a_max a_prob a_pT a_ptcopied a_ov a_oevac
            f_gen f_gen_used f_hfb f_first f_ge f_bf f_bfs f_dft f_kevac f_pq f_y f_inv0 f_ivs f_comb f_post f_zT f_tz
            f_mul ld_zc ld_hx ld_ftab ld_itab hy_out
            m_ready m_evac m_used g_cmb g_sc g_exp g_at g_T m_sig m_silu m_mul m_acc m_acc2 o_ready o_sq o_root o_r o_g o_y
            ld_hm""".split()
        S = {n: sem(n) for n in names}
        ld_x = [sem(f"ld_x{i}") for i in range(3)]
        uc_out = [sem(f"uc_out{i}") for i in range(3)]
        ot_out = [sem(f"ot_out{i}") for i in range(2)]
        ld_w4 = [sem(f"ld_w4{i}") for i in range(2)]
        ld_dec = sem("ld_dec")
        bank_ready = [sem(f"bank_ready{i}") for i in range(8)]
        bank_free = [sem(f"bank_free{i}") for i in range(8)]
        ld_m = [sem(f"ld_m{i}") for i in range(3)]
        ld_og = [sem(f"ld_og{i}") for i in range(2)]
        ld_hy = [sem(f"ld_hy{i}") for i in range(8)]
        ld_xr = [sem(f"ld_xr{i}") for i in range(2)]
        y_out = [sem(f"y_out{i}") for i in range(2)]

        NSP = len(SPANS)
        U_TILES = 3 * KD * NSP

        def group_tiles(g):
            return 8 * NSP + (14 if g == 0 else 12)

        A0T = [sum(group_tiles(x) for x in range(g)) for g in range(4)]
        UNITS = NT * HEADS

        ITEMS = [(s, q, o) for s in range(2) for q in range(NQ) for o in range(2)]
        NI = len(ITEMS)

        def npair(i):
            return len(DFTS[ITEMS[i][0]]["pairs"])

        def ntile(i):
            return LENS[ITEMS[i][0]] // P

        uk, uz, ui = [0] * NI, [0] * NI, [0] * NI
        n = 0
        uk[0], n = n, n + npair(0) + 1
        for i in range(NI):
            uz[i], n = n, n + npair(i)
            ui[i], n = n, n + 8
            if i + 1 < NI:
                uk[i + 1], n = n, n + npair(i + 1) + 1
        f_units = n
        GEN0 = [sum(ntile(x) for x in range(i)) for i in range(NI + 1)]
        TR0 = [g // 2 for g in GEN0]
        PR0 = [sum(npair(x) for x in range(i)) for i in range(NI + 1)]
        ORDER = (0, 1, 3, 2)

        def fbank(u):
            return 2 + u % 4

        def wait_ready(eng, u):
            eng.wait_ge(bank_ready[fbank(u)], u // 4 + 1)

        def wait_free(eng, u):
            eng.wait_ge(bank_free[fbank(u)], u // 4 + 1)

        MB = [("in", OFF_GA), ("a", 0), ("in", OFF_MG), ("a", BANK), ("in", OFF_MG + BANK), ("in", OFF_GH),
              ("in", OFF_GH + BANK), ("h", 0), ("in", OFF_MG + D), ("h", BANK), ("in", OFF_MG + D + BANK),
              ("o", 0), ("o", BANK)]
        B_GA, B_WA, B_MA, B_GH, B_WH, B_MH, B_WO = 0, (1, 3), (2, 4), (5, 6), (7, 9), (8, 10), (11, 12)
        MT_GA = 0
        MT_T = MT_GA + 4 * NSP
        MT_A = MT_T + NT
        MT_GH = MT_A + 2 * KD * NSP
        MT_H = MT_GH + KD * NSP
        MT_O = MT_H + 2 * KD * NSP
        MT_END = MT_O + 2 * NT
        M_DONE = [MT_T, MT_A + 24, MT_A + 24, MT_GH, MT_GH, MT_GH + 12, MT_H, MT_H + 24, MT_H + 24, MT_O, MT_O, MT_END, MT_END]

        def m_wait(eng, n):
            eng.wait_ge(m_done[n % 8], n // 8 + 1)

        def m_waitfree(eng, n):
            eng.wait_ge(m_free[n % 8], n // 8 + 1)

        def m_all(eng, n):
            for b in range(8):
                k = (n - b + 7) // 8
                if k > 0:
                    eng.wait_ge(m_done[b], k)

        def m_allfree(eng, n):
            for b in range(8):
                k = (n - b + 7) // 8
                if k > 0:
                    eng.wait_ge(m_free[b], k)

        m_done = [sem(f"m_done{i}") for i in range(8)]
        m_free = [sem(f"m_free{i}") for i in range(8)]

        GATES = [MT_A + 2 * x for x in range(KD * NSP)] + list(range(MT_GH, MT_H)) + [MT_H + 2 * x for x in range(KD * NSP)]

        def gate_used(eng, ns):
            if MT_GH <= GATES[ns] < MT_H:
                eng.wait_ge(S["m_mul"], GATES[ns] - MT_GH + 1)
            else:
                m_waitfree(eng, GATES[ns] + 1)

        def ld_w(n):
            return S["ld_w0"] if n % 2 == 0 else S["ld_w1"]

        def block_cols(n):
            if n < 6:
                return OFF_U + BANK * n
            g, kind = (n - 6) // 3, (n - 6) % 3
            return kind * QKV + g * AW

        def wait_block_used(eng, n):
            if n < 6:
                eng.wait_ge(S["u_ready"], 4 * NSP * (n + 1))
            else:
                g, kind = (n - 6) // 3, (n - 6) % 3
                eng.wait_ge(S["a_ready"], A0T[g] + (4 * NSP * (kind + 1) if kind < 2 else group_tiles(g)))

        def ot_count(g, t):
            return (g * NT + t) // 2 + 1

        block = ctx.enter_context(nc.Block())

        @block.sync
        def _(sp):
            sp.dma_start(ident, cst["ident"]).then_inc(S["ld_small"], 16)
            r0 = 0
            for src, cnt in ((ins["conv_w"][0].rearrange("j (c p) -> (j c) p", p=P), 9 * KD),
                             (ins["conv_b"][0].rearrange("(c p) -> c p", p=P), 3 * KD),
                             (ins["pre_norm_g"][0].rearrange("(c p) -> c p", p=P), KD),
                             (ins["hyena_skip"][0].rearrange("o (c p) -> (o c) p", p=P), 2 * KD)):
                sp.dma_start(rows[r0:r0 + cnt, :], src).then_inc(S["ld_small"], 16)
                r0 += cnt
            for i, name in enumerate(("filt_b1", "filt_b2", "filt_b3", "filt_freq")):
                sp.dma_start(frows[i:i + 1, :], ins[name]).then_inc(S["ld_small"], 16)
            for G in range(3):
                src = ins["x_prompt"][0, BANK * G:BANK * G + BANK, :] if G < 2 else ins["x_sample"][0]
                sp.dma_start(xt[:, 4 * G:4 * G + 4, :], src.rearrange("(t p) d -> p t d", p=P)).then_inc(ld_x[G], 16)
            sp.dma_start(feat[0:FEMB, :], cst["feat"]).then_inc(S["ld_tabs"], 16)
            sp.dma_start(fw[0:FEMB, 0:FHID], ins["filt_w1"][0]).then_inc(S["ld_tabs"], 16)
            sp.dma_start(fw[0:FHID, FHID:2 * FHID], ins["filt_w2"][0]).then_inc(S["ld_tabs"], 16)
            sp.dma_start(fw[0:FHID, 2 * FHID:3 * FHID], ins["filt_w3"][0]).then_inc(S["ld_tabs"], 16)
            sp.dma_start(hot[0:NBUCK, :], cst["hot"]).then_inc(S["ld_tabs"], 16)
            sp.dma_start(mask[0:HEADS, :], cst["mask"]).then_inc(S["ld_tabs"], 16)
            sp.dma_start(relb[0:NBUCK, :], ins["rel_bias"]).then_inc(S["ld_tabs"], 16)
            for n in range(6 + 9):
                if n >= 2:
                    wait_block_used(sp, n - 2)
                c0 = block_cols(n)
                sp.dma_start(ring[n % 2], w_in[:, c0:c0 + BANK].rearrange("(k p) c -> p k c", p=P)).then_inc(ld_w(n), 16)
            sp.wait_ge(S["a_ready"], A0T[3])
            sp.wait_ge(S["a_ov"], 3 * UNITS)
            sp.wait_ge(S["hn_saved"], 16)
            for sl in range(2):
                sp.wait_ge(ot_out[sl], 16 * ot_count(2, NT - 1))

            def load_filter(i):
                s, q, o = ITEMS[i]
                if i >= 2:
                    sp.wait_ge(S["f_gen"], GEN0[i - 1])
                sp.dma_start(w4[i % 2][0:FHID, :].rearrange("p (e c) -> p e c", e=2),
                             ins["filt_w4"][0].rearrange("k (o e c) -> k o e c", o=2, e=2)[:, o, :, FQ * q:FQ * q + FQ]
                             ).then_inc(ld_w4[i % 2], 16)
                if o == 0:
                    if i >= 1:
                        sp.wait_ge(S["f_gen_used"], GEN0[i])
                    sp.dma_start(dec[:, 0:ntile(i) + 1, :],
                                 cst[f"dec{s}"][:, FQ * q:FQ * q + FQ].rearrange("(t p) c -> p t c", p=P)
                                 ).then_inc(ld_dec, 16)

            load_filter(0)
            sp.dma_start(ftab, cst["fwd0"]).then_inc(S["ld_ftab"], 16)
            sp.dma_start(itab, cst["inv0"]).then_inc(S["ld_itab"], 16)
            for i in range(NI):
                s, q, o = ITEMS[i]
                if i + 1 < NI:
                    load_filter(i + 1)
                if o == 0:
                    if i >= 1:
                        sp.wait_ge(S["hy_out"], 16 * (i // 2))
                    sp.dma_start(zc[:, :, 0:LENS[s]], uc_d[2 * q:2 * q + 2, :, UC0[s]:UC0[s] + LENS[s]].rearrange("c p t -> p c t")
                                 ).then_inc(S["ld_zc"], 16)
                if i >= 1:
                    sp.wait_ge(S["f_post"], 2 * i)
                c0 = KD * (1 + o) + 2 * q
                sp.dma_start(hx[:, :, 0:LENS[s]], uc_d[c0:c0 + 2, :, UC0[s]:UC0[s] + LENS[s]].rearrange("c p t -> p c t")
                             ).then_inc(S["ld_hx"], 16)
                if i + 1 < NI and ITEMS[i + 1][0] != s:
                    for u in range(ui[i] + 4, ui[i] + 8):
                        wait_ready(sp, u)
                    sp.dma_start(ftab[:, 0:DFTS[1]["fwd"].shape[1]], cst["fwd1"]).then_inc(S["ld_ftab"], 16)
                    sp.dma_start(itab[:, 0:DFTS[1]["inv"].shape[1]], cst["inv1"]).then_inc(S["ld_itab"], 16)
            for u in range(f_units - 4, f_units):
                wait_ready(sp, u)
            sp.wait_ge(S["f_post"], 2 * NI)
            sp.wait_ge(S["hy_out"], 16 * (NI // 2))
            sp.dma_start(hm.rearrange("p k c -> p (k c)"), hn_d).then_inc(S["ld_hm"], 16)
            for n, (kind, c0) in enumerate(MB):
                if n >= 3:
                    m_all(sp, M_DONE[n - 3])
                w = {"in": w_in, "a": w_a, "h": w_h, "o": w_o}[kind]
                k = w.shape[0] // P
                sp.dma_start(mring[n % 3][:, 0:k, :], w[:, c0:c0 + BANK].rearrange("(k p) c -> p k c", p=P)
                             ).then_inc(ld_m[n % 3], 16)
            m_all(sp, MT_O)
            sp.dma_start(gpost, ins["post_norm_g"].to_broadcast([P, D])).then_inc(S["ld_gain"], 16)
            for t in range(NT):
                if t >= 2:
                    sp.wait_ge(S["o_y"], t - 1)
                src = ins["x_prompt"][0, P * t:P * t + P, :] if t < SP // P else ins["x_sample"][0, P * t - SP:P * t - SP + P, :]
                sp.dma_start(xres[t % 2], src).then_inc(ld_xr[t % 2], 16)

        NSMALL, NTABS = 16 * 9, 16 * 7

        @block.gpsimd
        def _(pool):
            for c in (0, COL_P + SP, COL_S + SS):
                pool.memset(hn[:, :, c:c + PADC], 0.0).then_inc(S["pads_ok"], 1)
            for b in range(2):
                for c in (0, 1 + SP, UC_W + 1):
                    pool.memset(ub[b][:, c:c + 1], 0.0).then_inc(S["pads_ok"], 1)
            pool.wait_ge(S["n_evA"], 12)
            pool.wait_ge(S["n_evD"], 12)
            pool.wait_ge(S["pads_ok"], 3)
            pool.dma_start(hn_d, hn.rearrange("p k c -> p (k c)")).then_inc(S["hn_saved"], 16)
            pool.wait_ge(S["b_rows"], 1)
            pool.dma_start(brow_d, mask[0:HEADS, :].unsqueeze(1).to_broadcast([HEADS, P, 3 * BANK])).then_inc(S["b_stored"], 16)
            for c in range(3 * KD):
                pool.wait_ge(S["u_conv"], c + 1)
                pool.dma_start(uc_d[c], ut[c % 3]).then_inc(uc_out[c % 3], 16)
            def skewed(g, q0, n, heads, width):
                return bass.AP(dram["brow"], BANK * g + q0, [[3 * BANK - 1, n], [P * 3 * BANK, heads], [1, width]])

            for i in range(3):
                pool.wait_ge(uc_out[i], 16 * KD)
            pool.wait_ge(S["b_stored"], 16)
            pool.wait_ge(S["h_sin"], 3)
            pool.wait_ge(S["n_T"], 24)
            for c in (0, COL_P + SP, COL_S + SS):
                pool.memset(kt[:, :, c:c + PADC], 0.0).then_inc(S["pads_ok"], 1)
            pool.dma_start(bwt, skewed(0, P - 1, P, HEADS, BW)).then_inc(S["bw_ld0"], 16)
            for g in range(3):
                if g == 1:
                    pool.wait_ge(S["a_biased"], UNITS)
                    pool.dma_start(bwt, skewed(1, P - 1, P, HEADS, BW)).then_inc(S["bw_ld1"], 16)
                if g == 2:
                    pool.wait_ge(S["a_biased"], 2 * UNITS)
                    for seq in range(2):
                        pool.dma_start(b2t[:, :, P * seq:P * seq + P], skewed(2, P - 1 + seq * (2 * P - 1), P, HEADS, P)
                                       ).then_inc(S["bw_ld2"], 16)
                for t in range(NT):
                    pool.wait_ge(S["a_oevac"], g * NT + t + 1)
                    sl = t % 2
                    seq = 0 if t < SP // P else 1
                    r, tt = stride(g, seq), t - TOK0[seq] // P
                    per = LENS[seq] // r
                    a = TOK0[seq] + P * tt // per + r * (P * tt % per)
                    pool.dma_start(og_d[g, a:a + r * (P - 1) + 1:r, :], ot[sl]).then_inc(ot_out[sl], 16)
            def sums(i):
                for j in range(ntile(i)):
                    n = GEN0[i] + j
                    h = hfb[n % 2]
                    pool.wait_ge(S["f_gen_used"], n + 1)
                    if i >= 1:
                        pool.wait_ge(S["f_bf"], 3 * i - 1)
                    nc.gpsimd.tensor_tensor(tge[:, j, :], h[:, 0:FQ], h[:, FQ:2 * FQ], ALU.add)
                    nc.gpsimd.tensor_tensor(tgo[:, j, :], h[:, 0:FQ], h[:, FQ:2 * FQ], ALU.subtract).then_inc(S["f_ge"], 1)

            sums(0)
            for i in range(NI):
                if i + 1 < NI:
                    sums(i + 1)
                for p in range(npair(i)):
                    n = PR0[i] + p
                    a = pq[n % 2]
                    wait_free(pool, uz[i] + p)
                    nc.gpsimd.tensor_tensor(yf[:, p, 0:FQ], a[:, 0:FQ], a[:, FQ:2 * FQ], ALU.subtract)
                    nc.gpsimd.tensor_tensor(yf[:, p, FQ:2 * FQ], a[:, 2 * FQ:3 * FQ], a[:, 3 * FQ:4 * FQ], ALU.add
                                            ).then_inc(S["f_y"], 1)
                s, q, o = ITEMS[i]
                if o == 1:
                    pool.wait_ge(S["f_post"], 2 * (i + 1))
                    pool.dma_start(hy_d[2 * q:2 * q + 2, :, TOK0[s]:TOK0[s] + LENS[s]].rearrange("c p t -> p c t"),
                                   zc[:, :, 0:LENS[s]]).then_inc(S["hy_out"], 16)
            for t in range(NT):
                if t == 0:
                    for u in range(f_units - 4, f_units):
                        wait_ready(pool, u)
                    pool.wait_ge(S["f_post"], 2 * NI)
                    pool.wait_ge(S["hy_out"], 16 * (NI // 2))
                    for sl in range(2):
                        pool.wait_ge(ot_out[sl], 16 * ot_count(2, NT - 1))
                if t >= 2:
                    pool.wait_ge(S["g_cmb"], t - 1)
                pool.dma_start(ogt[t % 2], og_d[:, P * t:P * t + P, :].rearrange("g p c -> p g c")).then_inc(ld_og[t % 2], 16)
            m_all(pool, MT_GH)
            m_allfree(pool, MT_GH)
            for j in range(KD):
                pool.dma_start(hg[:, j, :], hy_d[j]).then_inc(ld_hy[j], 16)
            for t in range(NT):
                pool.wait_ge(S["o_y"], t + 1)
                dst = y_p[0, P * t:P * t + P, :] if t < SP // P else y_s[0, P * t - SP:P * t - SP + P, :]
                pool.dma_start(dst, yout[t % 2]).then_inc(y_out[t % 2], 16)
            for sl in range(2):
                pool.wait_ge(y_out[sl], 16 * (NT // 2))

        @block.tensor
        def _(pe):
            pe.wait_ge(S["ld_small"], NSMALL)
            pe.transpose(ps[:, 0, 0:NCOLS], rows[0:NCOLS, :], ident[0:NCOLS, 0:NCOLS])
            pe.transpose(ps[0:FHID, 0, P:P + 4], frows[0:4, :], ident[0:4, 0:4]).then_inc(S["rows_T"], 1)
            pe.wait_ge(S["fcols_ok"], 1)
            for G in range(3):
                for k in range(KD):
                    n = KD * G + k
                    if k == 0:
                        pe.wait_ge(S["n_scaled"], 4 * (G + 1))
                    if n >= 4:
                        pe.wait_ge(S["n_evA"] if n % 2 == 0 else S["n_evD"], (n - 4) // 2 + 1)
                    for j in range(4):
                        mm = pe.transpose(ps[:, n % 4, P * j:P * j + P], xt[:, 4 * G + j, P * k:P * k + P], ident)
                    mm.then_inc(S["n_T"], 1)
            pe.wait_ge(S["n_evA"], 12)
            pe.wait_ge(S["n_evD"], 12)
            pe.wait_ge(S["pads_ok"], 9)
            pe.wait_ge(S["ld_tabs"], NTABS)
            for g in range(3):
                mm = pe.matmul(ps[0:HEADS, g, :], relb[0:NBUCK, HEADS * g:HEADS * g + HEADS],
                               hot[0:NBUCK, BANK * g:BANK * g + BANK], start=True, stop=True)
            mm.then_inc(S["b_mm"], 1)

            def filter_layer(l):
                if l == 0:
                    pe.wait_ge(S["b_rows"], 1)
                else:
                    pe.wait_ge(S["h_sin"], l)
                kk = FEMB if l == 0 else FHID
                for s in range(3):
                    src = feat if l == 0 else hid
                    mm = pe.matmul(ps[0:FHID, s, :], fw[0:kk, FHID * l:FHID * l + FHID],
                                   src[0:kk, BANK * s:BANK * s + BANK], start=True, stop=True)
                mm.then_inc(S["h_mm"], 1)

            for c in range(3 * KD):
                b = c // 4
                if c % 4 == 0:
                    pe.wait_ge(ld_w(b), 16 * (b // 2 + 1))
                for s in range(NSP):
                    n = NSP * c + s
                    if n >= 4:
                        pe.wait_ge(S["u_evac"], n - 3)
                    for k in range(KD):
                        mm = pe.matmul(ps[:, 4 + n % 4, :], ring[b % 2][:, k, P * (c % 4):P * (c % 4) + P],
                                       hn[:, k, SPANS[s]:SPANS[s] + BANK], start=(k == 0), stop=(k == KD - 1))
                    mm.then_inc(S["u_ready"], 1)
                if c in (2, 6, 10):
                    filter_layer((c - 2) // 4)
            pe.wait_ge(S["u_evac"], U_TILES)
            pe.wait_ge(S["h_arg"], 3)

            for g in range(3):
                base = A0T[g]
                if g >= 1:
                    pe.wait_ge(S["a_ptcopied"], g * UNITS)
                    pe.wait_ge(S["a_oevac"], g * NT)
                nl = 0
                vts = value_tiles(g, hn)
                for kind in range(3):
                    blk = 6 + 3 * g + kind
                    pe.wait_ge(ld_w(blk), 16 * (blk // 2 + 1))
                    w = ring[blk % 2]
                    for m in range(4 * NSP if kind < 2 else len(vts)):
                        if nl >= 8:
                            pe.wait_ge(S["a_evac"], base + nl - 7)
                        for k in range(KD):
                            if kind < 2:
                                j, s = m // NSP, m % NSP
                                lhs, rhs = w[:, k, P * j:P * j + P], hn[:, k, SPANS[s]:SPANS[s] + BANK]
                            else:
                                lhs, rhs = vts[m](k), w[:, k, :]
                            mm = pe.matmul(ps[:, nl % 8, :], lhs, rhs, start=(k == 0), stop=(k == KD - 1))
                        mm.then_inc(S["a_ready"], 1)
                        nl += 1
                pe.wait_ge(S["a_evac"], A0T[g + 1])
                if g == 0:
                    pe.wait_ge(S["pads_ok"], 12)

                def score(n):
                    t, h = n // HEADS, n % HEADS
                    N = g * UNITS + n
                    k0, kw = windows(g, t)[:2]
                    if N >= 3 and n >= 3:
                        pe.wait_ge(S["a_biased"], N - 2)
                    r = slice(HD * (h % 2), HD * (h % 2) + HD)
                    pe.matmul(ps[:, N % 3, 0:kw], qt[r, h // 2, P * t:P * t + P], kt[r, h // 2, k0:k0 + kw],
                              start=True, stop=True).then_inc(S["a_score"], 1)

                def turn(n):
                    N = g * UNITS + n
                    kw = windows(g, n // HEADS)[1]
                    pe.wait_ge(S["a_prob"], N + 1)
                    if N >= 3:
                        pe.wait_ge(S["a_ptcopied"], N - 2)
                    for b in range(kw // P):
                        mm = pe.transpose(ps[:, 3 + N % 3, P * b:P * b + P], pr[N % 3][:, P * b:P * b + P], ident)
                    mm.then_inc(S["a_pT"], 1)

                def value(n):
                    t, h = n // HEADS, n % HEADS
                    N = g * UNITS + n
                    vs = windows(g, t)[3]
                    pe.wait_ge(S["a_ptcopied"], N + 1)
                    if h == 0 and g * NT + t >= 2:
                        pe.wait_ge(S["a_oevac"], g * NT + t - 1)
                    for b, vi in enumerate(vs):
                        mm = pe.matmul(ps[:, 6 + t % 2, HD * h:HD * h + HD], pt[N % 3][:, P * b:P * b + P],
                                       vt[:, vi, HD * h:HD * h + HD], start=(b == 0), stop=(b == len(vs) - 1))
                    mm.then_inc(S["a_ov"], 1)

                for n in range(UNITS + 3):
                    if n < UNITS:
                        score(n)
                    if 2 <= n < UNITS + 2:
                        turn(n - 2)
                    if n >= 3:
                        value(n - 3)
            pe.wait_ge(S["a_ptcopied"], 3 * UNITS)
            pe.wait_ge(S["a_oevac"], 3 * NT)

            def gen(i):
                s = ITEMS[i][0]
                pe.wait_ge(ld_w4[i % 2], 16 * (i // 2 + 1))
                for j in range(ntile(i)):
                    n = GEN0[i] + j
                    if n >= 2:
                        pe.wait_ge(S["f_gen_used"], n - 1)
                    pe.matmul(ps[:, n % 2, :], h3[0:FHID, TOK0[s] + P * j:TOK0[s] + P * j + P], w4[i % 2][0:FHID, :],
                              start=True, stop=True).then_inc(S["f_gen"], 1)

            def spectrum(out, terms, a, nc_):
                for x, (comp, c, tab) in enumerate(terms):
                    mm = pe.matmul(out, ftab[:, P * tab:P * tab + P], a[:, comp, FQ * c:FQ * c + FQ],
                                   start=(x == 0), stop=(x == len(terms) - 1))
                return mm

            def filter_dft(i):
                s = ITEMS[i][0]
                pe.wait_ge(S["ld_ftab"], 16 * (s + 1))
                pe.wait_ge(S["f_bf"], 3 * i + 2)
                ge, go = fa[3 * i % 2], fa[(3 * i + 1) % 2]
                pairs = DFTS[s]["pairs"]
                for p in range(npair(i) + 1):
                    u = uk[i] + p
                    if u >= 4:
                        wait_free(pe, u - 4)
                    if p < npair(i):
                        spectrum(ps[:, fbank(u), 0:FQ], pairs[p][0], ge, 0)
                        mm = spectrum(ps[:, fbank(u), FQ:2 * FQ], pairs[p][2], go, 0)
                    else:
                        mm = spectrum(ps[:, fbank(u), 0:FQ], pairs[0][3], ge, 0)
                    mm.then_inc(bank_ready[fbank(u)], 1)

            def signal_dft(i):
                s = ITEMS[i][0]
                pe.wait_ge(S["f_bf"], 3 * i + 3)
                a = fa[(3 * i + 2) % 2]
                for p in range(npair(i)):
                    u = uz[i] + p
                    wait_free(pe, u - 4)
                    spectrum(ps[:, fbank(u), 0:FQ], DFTS[s]["pairs"][p][0], a, 0)
                    spectrum(ps[:, fbank(u), FQ:2 * FQ], DFTS[s]["pairs"][p][1], a, 0
                             ).then_inc(bank_ready[fbank(u)], 1)

            def inverse(i):
                s = ITEMS[i][0]
                pe.wait_ge(S["ld_itab"], 16 * (s + 1))
                pe.wait_ge(S["f_y"], PR0[i + 1])
                for ct in range(2):
                    for x, blk in enumerate(ORDER):
                        u = ui[i] + 4 * ct + x
                        wait_free(pe, u - 4)
                        terms = DFTS[s]["units"][blk]
                        for n, (p, im, col, oc, w) in enumerate(terms):
                            starts = n == 0 or terms[n - 1][3] != oc
                            stops = n == len(terms) - 1 or terms[n + 1][3] != oc
                            mm = pe.matmul(ps[:, fbank(u), oc:oc + w],
                                           yf[:, p, FQ * im + P * ct:FQ * im + P * ct + P], itab[:, col:col + w],
                                           start=starts, stop=stops)
                        mm.then_inc(bank_ready[fbank(u)], 1)

            def to_time(i):
                s, q, o = ITEMS[i]
                if o == 0:
                    pe.wait_ge(S["ld_zc"], 16 * (i // 2 + 1))
                else:
                    pe.wait_ge(S["f_post"], 2 * i)
                for j in range(ntile(i) // 2):
                    n = TR0[i] + j
                    if n >= 2:
                        pe.wait_ge(S["f_tz"], n - 1)
                    for x in range(4):
                        a = P * (2 * j + x // 2)
                        mm = pe.transpose(ps[:, 6 + n % 2, P * x:P * x + P], zc[:, x % 2, a:a + P], ident)
                    mm.then_inc(S["f_zT"], 1)

            gen(0)
            filter_dft(0)
            to_time(0)
            for i in range(NI):
                if i + 1 < NI:
                    gen(i + 1)
                signal_dft(i)
                inverse(i)
                if i + 1 < NI:
                    filter_dft(i + 1)
                    to_time(i + 1)
            for u in range(f_units - 4, f_units):
                wait_free(pe, u)
            pe.wait_ge(S["f_gen_used"], GEN0[NI])
            pe.wait_ge(S["f_tz"], TR0[NI])
            pe.wait_ge(S["ld_hm"], 16)

            def m_block(n):
                pe.wait_ge(ld_m[n % 3], 16 * (n // 3 + 1))
                return mring[n % 3]

            def m_tile(n, kc, lhs, rhs):
                if n >= 8:
                    m_waitfree(pe, n - 8)
                for k in range(kc):
                    mm = pe.matmul(ps[:, n % 8, :], lhs(k), rhs(k), start=(k == 0), stop=(k == kc - 1))
                mm.then_inc(m_done[n % 8], 1)

            w = m_block(B_GA)
            for j in range(4):
                for s in range(NSP):
                    m_tile(MT_GA + NSP * j + s, KD, lambda k: w[:, k, P * j:P * j + P],
                           lambda k: hm[:, k, SPANS[s]:SPANS[s] + BANK])
            for t in range(NT):
                n = MT_T + t
                m_waitfree(pe, n - 8)
                pe.wait_ge(S["g_cmb"], t + 1)
                for x in range(4):
                    mm = pe.transpose(ps[:, n % 8, P * x:P * x + P], cmb[t % 2][:, 0, P * x:P * x + P], ident)
                mm.then_inc(m_done[n % 8], 1)
            for n0, blocks_m, blocks_w, kc, src in ((MT_A, B_MA, B_WA, 4, at), (None, None, None, KD, hg)):
                if n0 is None:
                    for half in range(2):
                        w = m_block(B_GH[half])
                        for j in range(4):
                            for s in range(NSP):
                                m_tile(MT_GH + NSP * (4 * half + j) + s, KD, lambda k: w[:, k, P * j:P * j + P],
                                       lambda k: hm[:, k, SPANS[s]:SPANS[s] + BANK])
                    n0, blocks_m, blocks_w = MT_H, B_MH, B_WH
                if src is at:
                    m_allfree(pe, MT_A)
                else:
                    m_allfree(pe, MT_H)
                    pe.wait_ge(S["m_mul"], KD * NSP)
                for half in range(2):
                    wb, wm = m_block(blocks_w[half]), m_block(blocks_m[half])
                    for d in range(4):
                        for s in range(NSP):
                            n = n0 + 2 * (NSP * (4 * half + d) + s)
                            m_tile(n, KD, lambda k: wm[:, k, P * d:P * d + P],
                                   lambda k: hm[:, k, SPANS[s]:SPANS[s] + BANK])
                            m_tile(n + 1, kc, lambda k: wb[:, k, P * d:P * d + P],
                                   lambda k: src[:, k, BANK * s:BANK * s + BANK])
            m_allfree(pe, MT_O)
            pe.wait_ge(S["m_acc"], KD * NSP)
            wo = [m_block(B_WO[0]), m_block(B_WO[1])]
            for t in range(NT):
                for half in range(2):
                    m_tile(MT_O + 2 * t + half, KD, lambda k: mt[:, k, P * t:P * t + P], lambda k: wo[half][:, k, :])

        @block.scalar
        def _(act):
            for G in range(3):
                act.wait_ge(ld_x[G], 16)
                for t in range(4 * G, 4 * G + 4):
                    if t >= 2:
                        act.wait_ge(S["n_sq"], t - 1)
                    act.activation(junk[t % 2], xt[:, t, :], ACT.Square, accum_out=ssq[:, t:t + 1]).then_inc(S["n_sq"], 1)
                act.wait_ge(S["n_mean"], G + 1)
                act.activation(rstd[:, 4 * G:4 * G + 4], rstd[:, 4 * G:4 * G + 4], ACT.Sqrt).then_inc(S["n_root"], 1)
            act.wait_ge(S["cols_ok"], 1)
            for n in range(0, 24, 2):
                G, k = n // KD, n % KD
                act.wait_ge(S["n_T"], n + 1)
                act.activation(hn[:, k, SPANS[G]:SPANS[G] + BANK], ps[:, n % 4, :], ACT.Copy,
                               scale=cols[:, CG + k:CG + k + 1]).then_inc(S["n_evA"], 1)

            def sine(l):
                act.wait_ge(S["h_arg"], l + 1)
                dst = hid if l < 2 else h3
                act.activation(dst[0:FHID, :], xt[0:FHID, 3:5, :].rearrange("p a c -> p (a c)")[:, 0:T], ACT.Sin
                               ).then_inc(S["h_sin"], 1)

            act.wait_ge(S["pads_ok"], 9)
            for c in range(3 * KD):
                u, o = ub[c % 2], ut[c % 3]
                for s in range(NSP):
                    n = NSP * c + s
                    act.wait_ge(S["u_ready"], n + 1)
                    if s == 0 and c >= 2:
                        act.wait_ge(S["u_conv"], c - 1)
                    at0 = 1 + BANK * s + (s == 2)
                    act.activation(u[:, at0:at0 + BANK], ps[:, 4 + n % 4, :], ACT.Copy).then_inc(S["u_evac"], 1)
                act.wait_ge(S["u_evac"], NSP * (c + 1))
                if c >= 3:
                    act.wait_ge(uc_out[c % 3], 16 * (c // 3))
                act.activation(o, u[:, 1:1 + UC_W], ACT.Identity, scale=cols[:, CW + 3 * KD + c:CW + 3 * KD + c + 1],
                               bias=cols[:, CB + c:CB + c + 1]).then_inc(S["u_mid"], 1)
                if c in (4, 8, 12):
                    sine((c - 4) // 4)
            act.wait_ge(S["u_conv"], 3 * KD)
            for i in range(3):
                act.wait_ge(uc_out[i], 16 * KD)
            act.wait_ge(S["b_stored"], 16)
            for g in range(3):
                nl = 0
                for kind in range(3):
                    for m in range(4 * NSP if kind < 2 else group_tiles(g) - 8 * NSP):
                        src = ps[:, nl % 8, :]
                        act.wait_ge(S["a_ready"], A0T[g] + nl + 1)
                        if kind == 2:
                            dst = vt[:, m, :]
                        else:
                            j, s = m // NSP, m % NSP
                            seq = 0 if s < 2 else 1
                            r = stride(g, seq)
                            if g == 0 and kind == 1:
                                dst = kt[:, j, SPANS[s]:SPANS[s] + BANK]
                            else:
                                i0 = BANK * s // r if seq == 0 else 0
                                buf = (qt, kt)[kind][:, j, TOK0[seq]:TOK0[seq] + LENS[seq]]
                                dst = buf.rearrange("p (r i) -> p r i", r=r)[:, :, i0:i0 + BANK // r]
                                src = src.rearrange("p (i r) -> p r i", r=r)
                        act.activation(dst, src, ACT.Copy, scale=HD ** -0.5 if kind == 0 else 1.0).then_inc(S["a_evac"], 1)
                        nl += 1

                def prob(n):
                    N = g * UNITS + n
                    t, h = n // HEADS, n % HEADS
                    kw = windows(g, t)[1]
                    act.wait_ge(S["a_max"], N + 1)
                    if N >= 3:
                        act.wait_ge(S["a_pT"], N - 2)
                    o = ot[t % 2]
                    act.activation(pr[N % 3][:, 0:kw], lg[N % 3][:, 0:kw], ACT.Exp, bias=o[:, AW + h:AW + h + 1],
                                   accum_out=o[:, AW + HEADS + h:AW + HEADS + h + 1]).then_inc(S["a_prob"], 1)

                def copy(n):
                    N = g * UNITS + n
                    kw = windows(g, n // HEADS)[1]
                    act.wait_ge(S["a_pT"], N + 1)
                    if N >= 3:
                        act.wait_ge(S["a_ov"], N - 2)
                    act.activation(pt[N % 3][:, 0:kw], ps[:, 3 + N % 3, 0:kw], ACT.Copy).then_inc(S["a_ptcopied"], 1)

                def result(t):
                    act.wait_ge(S["a_ov"], g * UNITS + HEADS * (t + 1))
                    if g * NT + t >= 2:
                        act.wait_ge(ot_out[t % 2], 16 * ot_count(g, t - 2))
                    act.activation(ot[t % 2][:, 0:AW], ps[:, 6 + t % 2, :], ACT.Copy).then_inc(S["a_oevac"], 1)

                for n in range(UNITS + 4):
                    if n < UNITS:
                        prob(n)
                    if 1 <= n < UNITS + 1:
                        copy(n - 1)
                    if n >= 4 and (n - 4) % HEADS == HEADS - 1:
                        result((n - 4) // HEADS)
            def filter_copy(i):
                if i >= 1:
                    for u in range(uz[i - 1] + npair(i - 1) - 4, uz[i - 1] + npair(i - 1)):
                        wait_free(act, u)
                for p in range(npair(i) + 1):
                    u = uk[i] + p
                    wait_ready(act, u)
                    src = ps[:, fbank(u), :]
                    if p == npair(i):
                        act.activation(kf[:, 0, 2 * FQ:3 * FQ], src[:, 0:FQ], ACT.Copy).then_inc(bank_free[fbank(u)], 1)
                    elif p == 0:
                        act.activation(kf[:, 0, 0:2 * FQ], src, ACT.Copy).then_inc(bank_free[fbank(u)], 1)
                    else:
                        act.activation(kf[:, p, 0:2 * FQ], src, ACT.Copy)
                        act.activation(kf[:, p, 2 * FQ:3 * FQ], src[:, 0:FQ], ACT.Copy).then_inc(bank_free[fbank(u)], 1)

            def time_copy(i):
                if i >= 1:
                    act.wait_ge(S["f_bf"], 3 * i)
                for j in range(ntile(i) // 2):
                    n = TR0[i] + j
                    act.wait_ge(S["f_zT"], n + 1)
                    act.activation(tz[:, 2 * j:2 * j + 2, :], ps[:, 6 + n % 2, :].rearrange("p (a c) -> p a c", a=2),
                                   ACT.Copy).then_inc(S["f_tz"], 1)

            filter_copy(0)
            time_copy(0)
            for i in range(NI):
                w2 = 2 * DFTS[ITEMS[i][0]]["w"]
                for ct in range(2):
                    m = 2 * i + ct
                    for x, dst in ((0, iv0), (1, iv1)):
                        u = ui[i] + 4 * ct + x
                        if m >= 2:
                            act.wait_ge(S["f_post"], m - 1)
                        wait_ready(act, u)
                        act.activation(dst[m % 2][:, 0:w2], ps[:, fbank(u), 0:w2], ACT.Copy
                                       ).then_inc(bank_free[fbank(u)], 1)
                if i + 1 < NI:
                    filter_copy(i + 1)
                    time_copy(i + 1)
            act.wait_ge(S["ld_hm"], 16)

            def combine(t):
                act.wait_ge(S["g_sc"], 2 * t + 1)
                act.activation(wts[t % 2][:, 8:32], wts[t % 2][:, 8:32], ACT.Exp).then_inc(S["g_exp"], 1)

            for n in range(MT_GA, MT_T):
                if n in (4, 8):
                    combine(n // 4 - 1)
                j, s = n // NSP, n % NSP
                m_wait(act, n)
                act.activation(ga[:, j, BANK * s:BANK * s + BANK], ps[:, n % 8, :], ACT.Silu).then_inc(m_free[n % 8], 1)
            for t in range(2, NT):
                combine(t)
            for ns, n in enumerate(GATES):
                m_wait(act, n)
                if ns >= 2:
                    gate_used(act, ns - 2)
                act.activation(sg[ns % 2], ps[:, n % 8, :], ACT.Silu if MT_GH <= n < MT_H else ACT.Sigmoid
                               ).then_inc(m_free[n % 8], 1)
            for t in range(NT):
                for half in range(2):
                    n = MT_O + 2 * t + half
                    m_wait(act, n)
                    act.activation(osq[:, BANK * half:BANK * half + BANK], ps[:, n % 8, :], ACT.Square,
                                   accum_out=ssq2[:, half:half + 1] if t % 2 == 0 else ssq2[:, 2 + half:3 + half]
                                   ).then_inc(S["o_sq"], 1)
                act.wait_ge(S["o_r"], 2 * t + 1)
                act.activation(rstd2[:, t:t + 1], rstd2[:, t:t + 1], ACT.Sqrt).then_inc(S["o_root"], 1)

        @block.vector
        def _(dve):
            steps = [0]

            def chain(op):
                op.then_inc(S["dve_steps"], 1)
                steps[0] += 1

            def settle():
                dve.wait_ge(S["dve_steps"], steps[0])

            dve.wait_ge(S["rows_T"], 1)
            dve.tensor_copy(cols[:, 0:NCOLS], ps[:, 0, 0:NCOLS]).then_inc(S["cols_ok"], 1)
            dve.tensor_copy(fcol[0:FHID, 0:4], ps[0:FHID, 0, P:P + 4]).then_inc(S["fcols_ok"], 1)
            dve.wait_ge(S["cols_ok"], 1)

            def evac(n):
                G, k = n // KD, n % KD
                dve.wait_ge(S["n_T"], n + 1)
                dve.tensor_scalar(hn[:, k, SPANS[G]:SPANS[G] + BANK], ps[:, n % 4, :], cols[:, CG + k:CG + k + 1], None,
                                  ALU.mult).then_inc(S["n_evD"], 1)

            for G in range(3):
                a, b = 4 * G, 4 * G + 4
                dve.wait_ge(S["n_sq"], b)
                dve.tensor_scalar(rstd[:, a:b], ssq[:, a:b], 1.0 / D, EPS, ALU.mult, ALU.add).then_inc(S["n_mean"], 1)
                dve.wait_ge(S["n_root"], G + 1)
                dve.reciprocal(rstd[:, a:b], rstd[:, a:b]).then_inc(S["n_rstd"], 1)
                dve.wait_ge(S["n_rstd"], G + 1)
                for t in range(a, b):
                    dve.tensor_scalar(xt[:, t, :], xt[:, t, :], rstd[:, t:t + 1], None, ALU.mult).then_inc(S["n_scaled"], 1)
            for n in range(1, 24, 2):
                evac(n)
            dve.wait_ge(S["b_mm"], 1)
            m3 = mask[0:HEADS, :].rearrange("p (a c) -> p a c", a=3)
            dve.tensor_tensor(m3, ps[0:HEADS, 0:3, :], m3, ALU.add).then_inc(S["b_rows"], 1)

            TWO_PI = 2.0 * math.pi
            HI = float(np.float32(6.28125))
            LO = float(np.float32(TWO_PI - HI))
            ROUND = float(1.5 * 2 ** 23)
            LIM = float(np.float32(3.1415925))

            def argument(l):
                val = xt[0:FHID, 0:2, :].rearrange("p a c -> p (a c)")[:, 0:T]
                trn = xt[0:FHID, 6:8, :].rearrange("p a c -> p (a c)")[:, 0:T]
                arg = xt[0:FHID, 3:5, :].rearrange("p a c -> p (a c)")[:, 0:T]
                dve.wait_ge(S["h_mm"], l + 1)
                chain(dve.tensor_scalar(val.rearrange("p (a c) -> p a c", a=3), ps[0:FHID, 0:3, :], fcol[0:FHID, l:l + 1],
                                        fcol[0:FHID, 3:4], ALU.add, ALU.mult))
                settle()
                chain(dve.tensor_scalar(trn, val, 1.0 / TWO_PI, ROUND, ALU.mult, ALU.add))
                settle()
                chain(dve.tensor_scalar(trn, trn, -ROUND, None, ALU.add))
                settle()
                chain(dve.scalar_tensor_tensor(val, trn, -HI, val, ALU.mult, ALU.add))
                settle()
                chain(dve.scalar_tensor_tensor(val, trn, -LO, val, ALU.mult, ALU.add))
                settle()
                dve.tensor_scalar(arg, val, LIM, -LIM, ALU.min, ALU.max).then_inc(S["h_arg"], 1)

            for c in range(3 * KD):
                u, o = ub[c % 2], ut[c % 3]
                dve.wait_ge(S["u_mid"], c + 1)
                dve.scalar_tensor_tensor(o, u[:, 0:UC_W], cols[:, CW + c:CW + c + 1], o, ALU.mult, ALU.add
                                         ).then_inc(S["u_tap"], 1)
                dve.wait_ge(S["u_tap"], c + 1)
                dve.scalar_tensor_tensor(o, u[:, 2:2 + UC_W], cols[:, CW + 6 * KD + c:CW + 6 * KD + c + 1], o,
                                         ALU.mult, ALU.add).then_inc(S["u_conv"], 1)
                if c in (3, 7, 11):
                    argument((c - 3) // 4)
            for g in range(3):
                dve.wait_ge(S[f"bw_ld{g}"], 16 if g < 2 else 32)
                for n in range(UNITS):
                    N = g * UNITS + n
                    t, h = n // HEADS, n % HEADS
                    _, kw, b0, _, edge = windows(g, t)
                    l = lg[N % 3]
                    c0, c1 = 0, kw
                    if edge is not None:
                        c0, c1 = (edge[1], kw) if edge[0] == 0 else (0, edge[0])
                    dve.wait_ge(S["a_score"], N + 1)
                    if N >= 3:
                        dve.wait_ge(S["a_prob"], N - 2)
                    if edge is not None:
                        chain(dve.memset(l[:, edge[0]:edge[1]], NEG))
                        settle()
                    bias = (bwt if g < 2 else b2t)[:, h, b0 + c0:b0 + c1]
                    dve.tensor_tensor(l[:, c0:c1], ps[:, N % 3, c0:c1], bias, ALU.add).then_inc(S["a_biased"], 1)
                    dve.wait_ge(S["a_biased"], N + 1)
                    if h == 0 and g * NT + t >= 2:
                        dve.wait_ge(ot_out[t % 2], 16 * ot_count(g, t - 2))
                    dve.tensor_reduce(ot[t % 2][:, AW + h:AW + h + 1], l[:, 0:kw], AX.X, ALU.max, negate=True
                                      ).then_inc(S["a_max"], 1)
            RT = math.sqrt(0.5)

            def filt(i):
                if ITEMS[i][2] == 0:
                    dve.wait_ge(ld_dec, 16 * (i // 2 + 1))
                for j in range(ntile(i)):
                    n = GEN0[i] + j
                    h = hfb[n % 2]
                    dve.wait_ge(S["f_gen"], n + 1)
                    if n >= 2:
                        dve.wait_ge(S["f_ge"], n - 1)
                    if j == 0:
                        chain(dve.tensor_tensor(h[:, 0:FQ], ps[:, n % 2, 0:FQ], dec[:, 0, :], ALU.mult))
                        dve.tensor_tensor(h[:, FQ:2 * FQ], ps[:, n % 2, FQ:2 * FQ], dec[:, ntile(i), :], ALU.mult
                                          ).then_inc(S["f_gen_used"], 1)
                    else:
                        dve.tensor_tensor(h.rearrange("p (e c) -> p e c", e=2),
                                          ps[:, n % 2, :].rearrange("p (e c) -> p e c", e=2),
                                          dec[:, j:j + 1, :].to_broadcast([P, 2, FQ]), ALU.mult).then_inc(S["f_gen_used"], 1)

            def butterfly(i, x, src):
                m = 3 * i + x
                if m >= 2:
                    if x == 0:
                        u = uk[i - 1] + npair(i - 1)
                    elif x == 1:
                        u = uz[i - 1] + npair(i - 1) - 1
                    else:
                        u = uk[i] + npair(i)
                    wait_ready(dve, u)
                a = fa[m % 2]
                nc_ = DFTS[ITEMS[i][0]]["nc"]
                w = nc_ * FQ
                f = src.rearrange("p t c -> p (t c)")
                e = e01.rearrange("p a c -> p (a c)")

                def A(c):
                    return a[:, c, 0:w]

                settle()
                if m >= 1:
                    dve.wait_ge(S["f_bf"], m)
                chain(dve.tensor_tensor(e[:, 0:2 * w], f[:, 0:2 * w], f[:, 2 * w:4 * w], ALU.add))
                chain(dve.tensor_tensor(a[:, A2R:A2N + 1, 0:w], f[:, 0:2 * w].rearrange("p (a c) -> p a c", a=2),
                                        f[:, 2 * w:4 * w].rearrange("p (a c) -> p a c", a=2), ALU.subtract))
                settle()
                e0, e1 = e[:, 0:w], e[:, w:2 * w]
                chain(dve.tensor_tensor(A(A0), e0, e1, ALU.add))
                chain(dve.tensor_tensor(A(A4), e0, e1, ALU.subtract))
                chain(dve.scalar_tensor_tensor(A(A1R), A(A2N), RT, f[:, 0:w], ALU.mult, ALU.add))
                chain(dve.scalar_tensor_tensor(A(A3R), A(A2N), -RT, f[:, 0:w], ALU.mult, ALU.add))
                chain(dve.scalar_tensor_tensor(A(A1N), e1, RT, f[:, 2 * w:3 * w], ALU.mult, ALU.add))
                dve.scalar_tensor_tensor(A(A3I), e1, -RT, f[:, 2 * w:3 * w], ALU.mult, ALU.add).then_inc(S["f_bf"], 1)

            def filter_butterflies(i):
                dve.wait_ge(S["f_ge"], GEN0[i + 1])
                butterfly(i, 0, tge)
                butterfly(i, 1, tgo)

            def product(i):
                for u in range(uk[i] + npair(i) - 3, uk[i] + npair(i) + 1):
                    wait_free(dve, u)
                for p in range(npair(i)):
                    u = uz[i] + p
                    n = PR0[i] + p
                    a = pq[n % 2]
                    wait_ready(dve, u)
                    if n >= 2:
                        dve.wait_ge(S["f_y"], n - 1)
                    src = ps[:, fbank(u), :]
                    chain(dve.tensor_tensor(a[:, 0:2 * FQ], src, kf[:, p, 0:2 * FQ], ALU.mult))
                    dve.tensor_tensor(a[:, 2 * FQ:4 * FQ], src, kf[:, p, FQ:3 * FQ], ALU.mult
                                      ).then_inc(bank_free[fbank(u)], 1)

            def recombine(i, ct):
                s, q, o = ITEMS[i]
                L, w = LENS[s], DFTS[s]["w"]
                m = 2 * i + ct
                b0, b1 = iv0[m % 2], iv1[m % 2]
                u0, u1, u3, u2 = (ui[i] + 4 * ct + x for x in range(4))
                U, V, E, X = iv_u[:, 0:2 * w], iv_v[:, 0:2 * w], iv_a[:, 0:2 * w], iv_b[:, 0:2 * w]
                G = e01.rearrange("p a c -> p (a c)")[:, 0:2 * w]
                settle()
                if m >= 1:
                    dve.wait_ge(S["f_post"], m)
                dve.wait_ge(S["f_bf"], 3 * i + (5 if i + 1 < NI else 3))
                wait_free(dve, u0)
                chain(dve.tensor_tensor(E[:, 0:w], b0[:, 0:w], b0[:, w:2 * w], ALU.add))
                chain(dve.tensor_tensor(E[:, w:2 * w], b0[:, 0:w], b0[:, w:2 * w], ALU.subtract))
                wait_free(dve, u1)
                wait_ready(dve, u3)
                chain(dve.tensor_tensor(U, ps[:, fbank(u3), 0:2 * w], b1[:, 0:2 * w], ALU.add))
                dve.scalar_tensor_tensor(V, ps[:, fbank(u3), 0:2 * w], -1.0, b1[:, 0:2 * w], ALU.mult, ALU.add
                                         ).then_inc(bank_free[fbank(u3)], 1)
                settle()
                wait_ready(dve, u2)
                chain(dve.tensor_tensor(X, ps[:, fbank(u2), 0:2 * w], E, ALU.add))
                settle()
                dve.scalar_tensor_tensor(E, ps[:, fbank(u2), 0:2 * w], -1.0, E, ALU.mult, ALU.add
                                         ).then_inc(bank_free[fbank(u2)], 1)
                wait_free(dve, u3)
                chain(dve.tensor_tensor(G[:, 0:w], V[:, 0:w], U[:, w:2 * w], ALU.subtract))
                chain(dve.tensor_tensor(G[:, w:2 * w], V[:, 0:w], U[:, w:2 * w], ALU.add))
                wait_free(dve, u2)
                settle()
                chain(dve.tensor_tensor(yo[:, 0:w], X[:, 0:w], U[:, 0:w], ALU.add))
                chain(dve.tensor_tensor(yo[:, 2 * w:3 * w], E[:, 0:w], V[:, w:2 * w], ALU.subtract))
                chain(dve.scalar_tensor_tensor(yo[:, w:2 * w], G[:, 0:w], RT, E[:, w:2 * w], ALU.mult, ALU.add))
                chain(dve.scalar_tensor_tensor(yo[:, 3 * w:4 * w], G[:, w:2 * w], -RT, X[:, w:2 * w], ALU.mult, ALU.add))
                settle()
                z = zc[:, ct, 0:L]
                sk = CS + KD * o + 2 * q + ct
                chain(dve.scalar_tensor_tensor(yo[:, 0:L], z, cols[:, sk:sk + 1], yo[:, 0:L], ALU.mult, ALU.add))
                settle()
                dve.wait_ge(S["ld_hx"], 16 * (i + 1))
                dve.tensor_tensor(z, yo[:, 0:L], hx[:, ct, 0:L], ALU.mult).then_inc(S["f_post"], 1)

            filt(0)
            filter_butterflies(0)
            for i in range(NI):
                dve.wait_ge(S["f_tz"], TR0[i + 1])
                butterfly(i, 2, tz)
                if i + 1 < NI:
                    filt(i + 1)
                product(i)
                if i + 1 < NI:
                    filter_butterflies(i + 1)
                recombine(i, 0)
                recombine(i, 1)
            dve.wait_ge(S["ld_hm"], 16)

            def gate(t):
                n = MT_T + t
                if t == 0:
                    m_allfree(dve, MT_T)
                m_wait(dve, n)
                c = slice(P * t, P * t + P)
                dve.tensor_tensor(at[:, :, c], ps[:, n % 8, :].rearrange("p (j c) -> p j c", j=4), ga[:, :, c], ALU.mult
                                  ).then_inc(m_free[n % 8], 1)

            for t in range(NT):
                o, w = ogt[t % 2], wts[t % 2]
                acc, tmp = cmb[t % 2][:, 0, :], cmb[t % 2][:, 1, :]
                nm, den = o[:, :, AW:AW + HEADS], o[:, :, AW + HEADS:AW + 2 * HEADS]
                e = w[:, 8:32].rearrange("p (g c) -> p g c", g=3)
                ed = w[:, 32:56].rearrange("p (g c) -> p g c", g=3)
                dve.wait_ge(ld_og[t % 2], 16 * (t // 2 + 1))
                chain(dve.tensor_tensor(w[:, 0:8], nm[:, 0, :], nm[:, 1, :], ALU.min))
                settle()
                chain(dve.tensor_tensor(w[:, 0:8], w[:, 0:8], nm[:, 2, :], ALU.min))
                settle()
                dve.tensor_tensor(e, w[:, 0:8].unsqueeze(1).to_broadcast([P, 3, 8]), nm, ALU.subtract).then_inc(S["g_sc"], 1)
                dve.wait_ge(S["g_exp"], t + 1)
                chain(dve.tensor_tensor(ed, e, den, ALU.mult))
                settle()
                chain(dve.tensor_tensor(w[:, 56:64], ed[:, 0, :], ed[:, 1, :], ALU.add))
                settle()
                chain(dve.tensor_tensor(w[:, 56:64], w[:, 56:64], ed[:, 2, :], ALU.add))
                settle()
                chain(dve.reciprocal(w[:, 56:64], w[:, 56:64]))
                settle()
                dve.tensor_tensor(e, e, w[:, 56:64].unsqueeze(1).to_broadcast([P, 3, 8]), ALU.mult).then_inc(S["g_sc"], 1)
                dve.wait_ge(S["g_sc"], 2 * t + 2)
                if t >= 2:
                    m_wait(dve, MT_T + t - 2)

                def weighted(dst, g):
                    chain(dve.tensor_tensor(dst.rearrange("p (h c) -> p h c", h=HEADS),
                                            o[:, g, 0:AW].rearrange("p (h c) -> p h c", h=HEADS),
                                            e[:, g, :].unsqueeze(2).to_broadcast([P, HEADS, HD]), ALU.mult))

                weighted(acc, 0)
                weighted(tmp, 1)
                settle()
                chain(dve.tensor_tensor(acc, acc, tmp, ALU.add))
                settle()
                weighted(tmp, 2)
                settle()
                dve.tensor_tensor(acc, acc, tmp, ALU.add).then_inc(S["g_cmb"], 1)
                if t >= 1:
                    gate(t - 1)
            gate(NT - 1)

            ns = 0
            for x in range(KD * NSP):
                n = MT_A + 2 * x
                d, s = x // NSP, x % NSP
                m_waitfree(dve, n)
                m_wait(dve, n + 1)
                if x == 0:
                    dve.wait_ge(S["g_cmb"], NT)
                dve.tensor_tensor(mt[:, d, BANK * s:BANK * s + BANK], ps[:, (n + 1) % 8, :], sg[ns % 2], ALU.mult
                                  ).then_inc(m_free[(n + 1) % 8], 1)
                ns += 1
            for x in range(KD * NSP):
                n = MT_GH + x
                j, s = x // NSP, x % NSP
                m_waitfree(dve, n)
                dve.wait_ge(ld_hy[j], 16)
                h = hg[:, j, BANK * s:BANK * s + BANK]
                dve.tensor_tensor(h, h, sg[ns % 2], ALU.mult).then_inc(S["m_mul"], 1)
                ns += 1
            for x in range(KD * NSP):
                n = MT_H + 2 * x
                d, s = x // NSP, x % NSP
                m_waitfree(dve, n)
                m_wait(dve, n + 1)
                m = mt[:, d, BANK * s:BANK * s + BANK]
                tmp = gated[x % 2]
                dve.tensor_tensor(tmp, ps[:, (n + 1) % 8, :], sg[ns % 2], ALU.mult).then_inc(m_free[(n + 1) % 8], 1)
                m_waitfree(dve, n + 1)
                dve.tensor_tensor(m, m, tmp, ALU.add).then_inc(S["m_acc"], 1)
                ns += 1
            dve.wait_ge(S["ld_gain"], 16)
            for t in range(NT):
                a = 2 * (t % 2)
                r = rstd2[:, t:t + 1]
                dve.wait_ge(S["o_sq"], 2 * t + 2)
                chain(dve.tensor_tensor(r, ssq2[:, a:a + 1], ssq2[:, a + 1:a + 2], ALU.add))
                settle()
                dve.tensor_scalar(r, r, 1.0 / D, EPS, ALU.mult, ALU.add).then_inc(S["o_r"], 1)
                dve.wait_ge(S["o_root"], t + 1)
                dve.reciprocal(r, r).then_inc(S["o_r"], 1)
                dve.wait_ge(S["o_r"], 2 * t + 2)
                if t >= 2:
                    dve.wait_ge(y_out[t % 2], 16 * (t // 2))
                y = yout[t % 2]
                for half in range(2):
                    n = MT_O + 2 * t + half
                    c = slice(BANK * half, BANK * half + BANK)
                    dve.scalar_tensor_tensor(y[:, c], ps[:, n % 8, :], r, gpost[:, c], ALU.mult, ALU.mult
                                             ).then_inc(m_free[n % 8], 1)
                    m_waitfree(dve, n)
                dve.wait_ge(ld_xr[t % 2], 16 * (t // 2 + 1))
                dve.tensor_tensor(y, y, xres[t % 2], ALU.add).then_inc(S["o_y"], 1)


INPUTS = ("x_prompt", "x_sample", "rel_bias", "pre_norm_g", "post_norm_g", "w_in", "conv_w", "conv_b", "filt_w1", "filt_b1",
          "filt_w2", "filt_b2", "filt_w3", "filt_b3", "filt_w4", "filt_freq", "hyena_skip", "w_branch_a", "w_branch_h", "w_out")


def kernel(**inputs):
    import concourse.bacc as bacc
    from concourse.bass_utils import run_bass_kernel_spmd

    nc = bacc.Bacc("TRN2", target_bir_lowering=False, num_devices=1)
    arrays, ins, cst = {}, {}, {}
    for name in INPUTS:
        arrays["in_" + name] = np.ascontiguousarray(inputs[name])
        ins[name] = nc.dram_tensor("in_" + name, arrays["in_" + name].shape, F32, kind="ExternalInput").ap()
    for name, a in constants().items():
        arrays["c_" + name] = a
        cst[name] = nc.dram_tensor("c_" + name, a.shape, F32, kind="ExternalInput").ap()
    y_p = nc.dram_tensor("y_prompt", (1, SP, D), F32, kind="ExternalOutput").ap()
    y_s = nc.dram_tensor("y_sample", (1, SS, D), F32, kind="ExternalOutput").ap()
    build(nc, ins, cst, y_p, y_s)
    r = run_bass_kernel_spmd(nc, [arrays], core_ids=[0])
    return r.results[0]["y_prompt"], r.results[0]["y_sample"]
```

```python
import math
from contextlib import ExitStack

import numpy as np

import concourse.bass as bass
import concourse.mybir as mybir

ALU = mybir.AluOpType
ACT = mybir.ActivationFunctionType
AX = mybir.AxisListType
F32, FP16, I32 = mybir.dt.float32, mybir.dt.float16, mybir.dt.int32

P = 128
D = 1024
KD = D // P
SP, SS = 1024, 512
T = SP + SS
NT = T // P
BANK = 512
HD = 64
HEADS = 8
GROUPS = ((128, 1), (512, 4), (2048, 16))
QKV = len(GROUPS) * HEADS * HD
AW = HEADS * HD
HW = AW // 2
HH = HEADS // 2
WC = 256
BLK = 64
NEG = -1e30
NBUCK = 32
MAXDIST = 1024
FEMB, FHID = 33, 64
EPS = 1e-6
OFF_GA = 3 * QKV
OFF_U = OFF_GA + AW
OFF_GH = OFF_U + 3 * D
OFF_MG = OFF_GH + D
INW = OFF_MG + 2 * D

PADC = BLK
COL_P = PADC
COL_S = PADC + SP + PADC
HC = COL_S + SS + PADC
SPANS = (COL_P, COL_P + BANK, COL_S)

FQ = 256
NQ = D // FQ
RAD = 8

BW = 3 * P
BROW = 2 * 2 * P - 1
OW = HW + 2 * HH


def bucket(rel):
    half = NBUCK // 2
    exact = half // 2
    n = np.abs(rel)
    nf = np.maximum(n, 1).astype(np.float32)
    large = exact + (np.log(nf / np.float32(exact)) / np.float32(math.log(MAXDIST / exact)) * (half - exact)).astype(np.int32)
    return np.where(rel > 0, half, 0) + np.where(n < exact, n, np.minimum(large, half - 1))


def stride(g, seq):
    return min(GROUPS[g][1], (SP, SS)[seq] // P)


def bias_tables():
    hot = np.zeros((NBUCK, 3 * BANK), np.float32)
    mask = np.zeros((HEADS, 3 * BANK), np.float32)
    for g, seq, col, reach in ((0, 0, 0, BROW // 2), (1, 0, 0, BROW // 2), (2, 0, 0, P - 1), (2, 1, 2 * P - 1, P - 1)):
        dilation, r = GROUPS[g][1], stride(g, seq)
        for i, apart in enumerate(range(-reach, reach + 1)):
            if apart * r % dilation == 0 and abs(apart * r) <= BLK * dilation:
                hot[bucket(np.array(apart * r)), g * BANK + col + i] = 1.0
            else:
                mask[:, g * BANK + col + i] = NEG
    return hot, mask


def filter_features(length):
    f = np.float32
    t = np.linspace(0.0, 1.0, length, dtype=f)[:, None]
    ang = f(2.0 * math.pi / length) * np.arange(length, dtype=f)[:, None]
    bands = np.linspace(1e-4, (FEMB - 1) // 2 - 1, (FEMB - 1) // 2, dtype=f)[None]
    return np.concatenate([t, np.cos(ang * bands), -np.sin(ang * bands)], axis=-1).astype(f).T


def decay_table(length):
    t = np.linspace(0.0, 1.0, length, dtype=np.float32)[:, None].astype(np.float64)
    deltas = np.abs(np.linspace(math.log(1e-2) / 1.5, math.log(1e-2) / 0.3, D, dtype=np.float32)).astype(np.float64)
    dec = np.exp(-t * deltas[None])
    first = dec[0:P].copy()
    first[0] = 0.0
    return np.concatenate([dec, first]).astype(np.float32)


A0, A4, A1R, A1N, A2R, A2N, A3R, A3I = range(8)


def dft(L):
    n = 2 * L
    w = n // RAD
    nc = w // P
    n2 = np.arange(w)
    fwd, inv, pairs = [], [], []
    units = [[], [], [], []]

    def add(m):
        fwd.append(m)
        return len(fwd) - 1

    def addi(m):
        inv.append(m)
        return sum(x.shape[1] for x in inv[:-1])

    def ang(c, ks):
        return 2 * np.pi * (np.outer(n2[c * P:(c + 1) * P], ks) % n) / n

    def iang(ks):
        return 2 * np.pi * (np.outer(ks, n2) % n) / n

    def weight(ks):
        return np.where((ks == 0) | (ks == L), 1.0, 2.0)[:, None] / n

    def cat(a, b):
        return np.concatenate([a, b], axis=1)

    nyq = np.cos(np.pi * (n2 % 2))
    if nc == 2:
        k0, k4 = 8 * np.arange(P), 4 + 8 * np.arange(P)
        re, im, imk, rek = [], [], [], []
        for c in range(nc):
            co, si = np.cos(ang(c, k0)), -np.sin(ang(c, k0))
            sz, cy = si.copy(), co.copy()
            sz[:, 0] = cy[:, 0] = nyq[c * P:(c + 1) * P]
            re.append((A0, c, add(co)))
            im.append((A0, c, add(sz)))
            imk.append((A0, c, add(si)))
            rek.append((A0, c, add(cy)))
        pairs.append((re, im, imk, rek))
        re = [(A4, c, add(np.cos(ang(c, k4)))) for c in range(nc)]
        im = [(A4, c, add(-np.sin(ang(c, k4)))) for c in range(nc)]
        pairs.append((re, im, im, re))
        r, s = np.cos(iang(k0)) * weight(k0), -np.sin(iang(k0)) * weight(k0)
        s[0] = nyq / n
        units[0] += [(0, 0, addi(r), 0, w), (0, 1, addi(s), 0, w)]
        units[0] += [(1, 0, addi(np.cos(iang(k4)) * weight(k4)), w, w), (1, 1, addi(-np.sin(iang(k4)) * weight(k4)), w, w)]
    else:
        h = P // 2
        k0, k4 = 8 * np.arange(h), 4 + 8 * np.arange(h)
        z, zi = np.zeros((P, h)), np.zeros((h, w))
        co, si = np.cos(ang(0, k0)), -np.sin(ang(0, k0))
        sz, cy = si.copy(), co.copy()
        sz[:, 0] = cy[:, 0] = nyq
        c4, s4 = (A4, 0, add(cat(z, np.cos(ang(0, k4))))), (A4, 0, add(cat(z, -np.sin(ang(0, k4)))))
        pairs.append(([(A0, 0, add(cat(co, z))), c4], [(A0, 0, add(cat(sz, z))), s4],
                      [(A0, 0, add(cat(si, z))), s4], [(A0, 0, add(cat(cy, z))), c4]))
        s0 = -np.sin(iang(k0)) * weight(k0)
        s0[0] = nyq / n
        r = np.concatenate([cat(np.cos(iang(k0)) * weight(k0), zi), cat(zi, np.cos(iang(k4)) * weight(k4))])
        s = np.concatenate([cat(s0, zi), cat(zi, -np.sin(iang(k4)) * weight(k4))])
        units[0] += [(0, 0, addi(r), 0, 2 * w), (0, 1, addi(s), 0, 2 * w)]
    for k1, (ar, ai, negated) in enumerate(((A1R, A1N, True), (A2R, A2N, True), (A3R, A3I, False)), 1):
        for m in range(nc):
            ks = k1 + 8 * (np.arange(P) + m * P)
            re, im = [], []
            for c in range(nc):
                co, si = np.cos(ang(c, ks)), np.sin(ang(c, ks))
                ico, ins = add(co), add(-si)
                if negated:
                    re += [(ar, c, ico), (ai, c, ins)]
                    im += [(ar, c, ins), (ai, c, add(-co))]
                else:
                    re += [(ar, c, ico), (ai, c, add(si))]
                    im += [(ar, c, ins), (ai, c, ico)]
            pairs.append((re, im, im, re))
            co, si = np.cos(iang(ks)) * weight(ks), np.sin(iang(ks)) * weight(ks)
            col = addi(np.concatenate([-si, co, si], axis=1))
            units[k1] += [(len(pairs) - 1, 0, col + w, 0, 2 * w), (len(pairs) - 1, 1, col, 0, 2 * w)]
    return {"fwd": np.stack(fwd, axis=1).astype(np.float32).reshape(P, -1),
            "inv": np.concatenate(inv, axis=1).astype(np.float32), "pairs": pairs, "units": units, "w": w, "nc": nc}


DFTS = (dft(SP), dft(SS))
LENS = (SP, SS)
TOK0 = (0, SP)
UC_W = SP + 1 + SS
UC0 = (0, SP + 1)


def constants():
    hot, mask = bias_tables()
    c = {"hot": hot, "mask": mask,
         "feat": np.concatenate([filter_features(SP), filter_features(SS)], axis=1),
         "dec0": decay_table(SP), "dec1": decay_table(SS)}
    for s in range(2):
        c[f"fwd{s}"] = DFTS[s]["fwd"]
        c[f"inv{s}"] = DFTS[s]["inv"]
    c["ident"] = np.eye(P, dtype=np.float32)
    return {k: np.ascontiguousarray(v) for k, v in c.items()}


def windows(g, t):
    if g == 0:
        u = t if t < SP // P else t - SP // P
        last = u == (SP // P if t < SP // P else SS // P) - 1
        k0 = P * t if t < SP // P else COL_S - PADC + P * u
        v0 = t if t < SP // P else SP // P + 1 + u
        return k0, 2 * P, P // 2, [v0, v0 + 1], (0, BLK) if u == 0 else (3 * BLK, 4 * BLK) if last else None
    if g == 1:
        if t < SP // P:
            r, half = t // 2, t % 2
            return 2 * P * r, 2 * P, P - P * half, [2 * r, 2 * r + 1], None
        return P * t, P, P, [t], None
    return P * t, P, (0 if t < SP // P else P), [t], None


def value_tiles(g):
    if g == 0:
        return [(P * m, 1) for m in range(SP // P + 1)] + [(COL_S - PADC + P * m, 1) for m in range(SS // P + 1)]
    out = []
    for seq, c0, n in ((0, COL_P, SP), (1, COL_S, SS)):
        r = stride(g, seq)
        for m in range(n // P):
            out.append((c0 + m * P // (n // r) + r * (m * P % (n // r)), r))
    return out


def build(nc, ins, cst, y_p, y_s):
    dram = {}
    for name, shape in (("uc", [3 * KD, P, UC_W]), ("og", [3, T, 2, OW]), ("hy", [KD, P, T]),
                        ("hn", [P, KD * HC]), ("brow", [HEADS, P, 3 * BANK])):
        dram[name] = nc.dram_tensor("s_" + name, shape, F32, kind="Internal")
    uc_d, og_d, hy_d, hn_d, brow_d = (dram[n].ap() for n in ("uc", "og", "hy", "hn", "brow"))
    w_in, w_a, w_h, w_o = ins["w_in"][0], ins["w_branch_a"][0], ins["w_branch_h"][0], ins["w_out"][0]

    with ExitStack() as ctx:
        def sem(name):
            return ctx.enter_context(nc.semaphore(name))

        ARENA = 53200
        mem = ctx.enter_context(nc.sbuf_tensor("mem", [P, ARENA], F32))
        ps = ctx.enter_context(nc.psum_tensor("ps", [P, 8, BANK], F32))

        top = [0]

        def part(n, at=None):
            if at is not None:
                top[0] = at
            a = top[0]
            top[0] += n
            assert top[0] <= ARENA, (top[0], ARENA)
            return mem[:, a:a + n]

        def grid(n, m, at=None):
            return part(n * m, at).rearrange("p (n m) -> p n m", n=n)

        ident = part(P)
        cols = part(P)
        fcol = part(8)
        small = part(72)
        wsc = part(72)
        BASE = top[0]
        CW, CB, CG, CS = 0, 9 * KD, 12 * KD, 13 * KD
        NCOLS = 15 * KD
        ssq, rstd = small[:, 0:NT], small[:, NT:2 * NT]
        ssq2, rstd2 = small[:, 2 * NT:3 * NT], small[:, 3 * NT:4 * NT]
        H3_AT = ARENA - T
        h3 = part(T, H3_AT)

        def halves(a, n, m):
            return a.bitcast(FP16).rearrange("p (h n m) -> p h n m", h=2, n=n)

        hn_words = part(KD * HC, BASE)
        hn = halves(hn_words, KD, HC)
        raw = [grid(KD, WC) for _ in range(2)]
        ring = [halves(part(KD * WC), KD, WC) for _ in range(3)]
        EARLY = top[0]
        NB_U, NB_A, NB_M = 3 * D // WC, 6 * 3, 14
        NB = NB_U + NB_A + NB_M
        descale = [wsc[:, b:b + 1] for b in range(NB)]
        amax, amax_all, wexp, wscale = ([wsc[:, NB + 3 * x + i:NB + 3 * x + i + 1] for i in range(3)] for x in range(4))
        XC = NB + 12
        gscaled = wsc[:, XC:XC + KD]
        gmax, gmax_all, xscale, xdescale = (wsc[:, XC + KD + i:XC + KD + i + 1] for i in range(4))
        assert XC + KD + 4 <= 72
        xt = grid(NT, D)
        rows = part(P)
        frows = part(FHID)
        ub = [part(UC_W + 2) for _ in range(2)]
        ut = [part(UC_W) for _ in range(3)]
        junk = [ut[i][:, 0:D] for i in range(2)]
        feat = part(T)
        fw = part(3 * FHID)
        hid = part(T)
        hot = part(3 * BANK)
        mask = part(3 * BANK)
        assert top[0] <= H3_AT

        qt = [grid(2, T, EARLY), grid(2, T)]
        kt = [grid(2, HC) for _ in range(2)]
        vt = [grid(14, HW) for _ in range(2)]
        bwt = [grid(HH, BW) for _ in range(2)]
        b2t = [b.rearrange("p h c -> p (h c)")[:, 0:HH * 2 * P].rearrange("p (h c) -> p h c", h=HH) for b in bwt]
        lg = [grid(2, 2 * P) for _ in range(2)]
        pr = [grid(2, 2 * P) for _ in range(2)]
        pt = [grid(2, 2 * P) for _ in range(2)]
        ot = [part(OW) for _ in range(3)]
        relb = small[:, 4 * NT:4 * NT + 3 * HEADS]
        assert top[0] <= H3_AT

        w4 = [part(2 * FQ, BASE), part(2 * FQ)]
        ftab = part(DFTS[0]["fwd"].shape[1])
        itab = part(DFTS[0]["inv"].shape[1])
        dec = grid(SP // P + 1, FQ)
        tge, tgo, tz = (grid(SP // P, FQ) for _ in range(3))
        fa = [grid(8, 2 * FQ) for _ in range(2)]
        kf = grid(8, 2 * FQ)
        kfl = part(FQ)
        yf = grid(8, 2 * FQ)
        hfb = [part(2 * FQ) for _ in range(2)]
        pq = [part(4 * FQ) for _ in range(2)]
        iv_u, iv_v, iv_a, iv_b = pq[0][:, 0:BANK], pq[0][:, BANK:], pq[1][:, 0:BANK], pq[1][:, BANK:]
        zc = [grid(2, SP) for _ in range(2)]
        hx = grid(2, SP)
        yo = part(SP)
        e01 = grid(2, 2 * FQ)
        iv0 = [part(BANK) for _ in range(2)]
        iv1 = [part(BANK) for _ in range(2)]
        assert top[0] <= H3_AT, (top[0], H3_AT)

        mt = grid(KD, T, BASE + KD * HC)
        hg = grid(KD, T)
        ga, at = hg[:, 0:4, :], hg[:, 4:8, :]
        mraw = [grid(KD, WC) for _ in range(2)]
        wo = mem[:, top[0] - 2 * KD * WC:top[0] + 2 * KD * WC].rearrange("p (k c) -> p k c", k=KD)
        LAST = (NB - 1) % 3
        mring = [None] * 3
        for i in (LAST + 1, LAST + 2, LAST):
            mring[i % 3] = halves(part(KD * WC), KD, WC)
        wb = grid(KD, WC)
        sg = [part(BANK) for _ in range(3)]
        gated = part(BANK)
        ogt = [mem[:, BASE + KD * HC + i * 6 * OW:BASE + KD * HC + (i + 1) * 6 * OW].rearrange(
            "p (g a c) -> p g a c", g=3, a=2) for i in range(2)]
        GSC = BASE + KD * HC + 12 * OW
        wts = [mem[:, GSC + 64 * i:GSC + 64 * i + 64] for i in range(2)]
        cmb = [mem[:, GSC + 128 + 2 * AW * i:GSC + 128 + 2 * AW * (i + 1)].rearrange("p (a c) -> p a c", a=2) for i in range(2)]
        gpost = mem[:, BASE:BASE + D]
        xres = [mem[:, BASE + D * (1 + i):BASE + D * (2 + i)] for i in range(2)]
        yout = [mem[:, BASE + D * (3 + i):BASE + D * (4 + i)] for i in range(2)]
        osq = mem[:, BASE + 5 * D:BASE + 6 * D]

        names = """ld_small ld_tabs ld_gain dve_steps ld_w0 ld_w1 w_amax w_all w_scale w_hi w_lo g_amax g_all
            g_scale ld_wb rows_T cols_ok fcols_ok pads_ok n_sq n_mean n_root n_rstd n_scaled n_T n_evA n_evD
            hn_saved u_ready u_evac u_mid u_tap u_conv h_mm h_arg h_sin b_mm b_rows b_stored a_ready a_evac
            a_score a_biased a_max a_prob a_pT a_ptcopied a_ov a_oevac f_gen f_gen_used f_ge f_bf f_y f_post
            f_zT f_tz ld_hx ld_ftab ld_itab g_cmb g_sc g_exp m_mul m_acc o_sq o_root o_r o_y ld_hm""".split()
        S = {n: sem(n) for n in names}
        ld_x = [sem(f"ld_x{i}") for i in range(3)]
        uc_out = [sem(f"uc_out{i}") for i in range(3)]
        ot_out = [sem(f"ot_out{i}") for i in range(3)]
        ld_w4 = [sem(f"ld_w4{i}") for i in range(2)]
        ld_dec = sem("ld_dec")
        ld_zc = [sem(f"ld_zc{i}") for i in range(2)]
        hy_out = [sem(f"hy_out{i}") for i in range(2)]
        bank_ready = [sem(f"bank_ready{i}") for i in range(8)]
        bank_free = [sem(f"bank_free{i}") for i in range(8)]
        ld_wo = sem("ld_wo")
        ld_og = [sem(f"ld_og{i}") for i in range(2)]
        ld_hy = [sem(f"ld_hy{i}") for i in range(8)]
        ld_xr = [sem(f"ld_xr{i}") for i in range(2)]
        y_out = [sem(f"y_out{i}") for i in range(2)]

        NSP = len(SPANS)
        U_TILES = 3 * KD * NSP

        NPT = [2 * 2 * NSP + len(value_tiles(H // 2)) // 2 for H in range(6)]
        PT0 = [sum(NPT[:H]) for H in range(7)]
        STEPS = NT * 2
        NSTEP = 6 * STEPS
        MIX = [[(H, m) for m in range(n * NPT[H] // STEPS, (n + 1) * NPT[H] // STEPS)] if H < 6 else []
               for H in range(1, 7) for n in range(STEPS)]

        def unit(N):
            H, n = N // STEPS, N % STEPS
            return H, H // 2, n // 2, n % 2

        def ptile(H, m):
            kind = min(m // (2 * NSP), 2)
            return kind, m - 2 * NSP * kind, NB_U + 3 * H + kind, m == 2 * NSP * kind

        ITEMS = [(s, q, o) for s in range(2) for q0 in range(0, NQ, 2) for o in range(2) for q in (q0, q0 + 1)]
        NI = len(ITEMS)

        def npair(i):
            return len(DFTS[ITEMS[i][0]]["pairs"])

        def ntile(i):
            return LENS[ITEMS[i][0]] // P

        def zc_uses(i):
            return len([x for x in ITEMS[:i + 1] if x[1] % 2 == ITEMS[i][1] % 2 and x[2] == ITEMS[i][2]])

        uk, uz, ui = [0] * NI, [0] * NI, [0] * NI
        n = 0
        uk[0], n = n, n + npair(0) + 1
        for i in range(NI):
            uz[i], n = n, n + npair(i)
            ui[i], n = n, n + 8
            if i + 1 < NI:
                uk[i + 1], n = n, n + npair(i + 1) + 1
        f_units = n
        GEN0 = [sum(ntile(x) for x in range(i)) for i in range(NI + 1)]
        TR0 = [g // 2 for g in GEN0]
        PR0 = [sum(npair(x) for x in range(i)) for i in range(NI + 1)]
        ORDER = (0, 1, 3, 2)

        def fbank(u):
            return 2 + u % 4

        def wait_ready(eng, u):
            eng.wait_ge(bank_ready[fbank(u)], u // 4 + 1)

        def wait_free(eng, u):
            eng.wait_ge(bank_free[fbank(u)], u // 4 + 1)

        MB = [OFF_GA + WC * i for i in range(2)] + [OFF_MG + WC * i for i in range(4)] + [OFF_GH + WC * i for i in range(4)]
        MB += [OFF_MG + D + WC * i for i in range(4)]
        assert len(MB) == NB_M
        MT_GA = 0
        MT_T = MT_GA + 4 * NSP
        MT_A = MT_T + NT
        MT_GH = MT_A + 2 * KD * NSP
        MT_H = MT_GH + KD * NSP
        MT_O = MT_H + 2 * KD * NSP
        MT_END = MT_O + 2 * NT
        M_DONE = [MT_GA + 2 * NSP * (i + 1) for i in range(2)] + [MT_A + 4 * NSP * i + 3 * NSP for i in range(4)]
        M_DONE += [MT_GH + 2 * NSP * (i + 1) for i in range(4)] + [MT_H + 4 * NSP * i + 3 * NSP for i in range(4)]

        def m_wait(eng, n):
            eng.wait_ge(m_done[n % 8], n // 8 + 1)

        def m_waitfree(eng, n):
            eng.wait_ge(m_free[n % 8], n // 8 + 1)

        def m_all(eng, n):
            for b in range(8):
                k = (n - b + 7) // 8
                if k > 0:
                    eng.wait_ge(m_done[b], k)

        def m_allfree(eng, n):
            for b in range(8):
                k = (n - b + 7) // 8
                if k > 0:
                    eng.wait_ge(m_free[b], k)

        m_done = [sem(f"m_done{i}") for i in range(8)]
        m_free = [sem(f"m_free{i}") for i in range(8)]

        PAIRED = [2 * NSP * (x // NSP) + x % NSP for x in range(KD * NSP)]
        GATES = [MT_A + x for x in PAIRED] + list(range(MT_GH, MT_H)) + [MT_H + x for x in PAIRED]

        def gate_used(eng, ns):
            if MT_GH <= GATES[ns] < MT_H:
                eng.wait_ge(S["m_mul"], GATES[ns] - MT_GH + 1)
            else:
                m_waitfree(eng, GATES[ns] + NSP)

        def ld_w(n):
            return S["ld_w0"] if n % 2 == 0 else S["ld_w1"]

        def block_cols(b):
            if b < NB_U:
                return OFF_U + WC * b
            if b < NB_U + NB_A:
                H, kind = (b - NB_U) // 3, (b - NB_U) % 3
                return kind * QKV + HW * H
            return MB[b - NB_U - NB_A]

        def wait_block_used(eng, b):
            if b < NB_U:
                eng.wait_ge(S["u_ready"], 2 * NSP * (b + 1))
            elif b < NB_U + NB_A:
                H, kind = (b - NB_U) // 3, (b - NB_U) % 3
                eng.wait_ge(S["a_ready"], PT0[H] + (2 * NSP * (kind + 1) if kind < 2 else NPT[H]))
            else:
                m_all(eng, M_DONE[b - NB_U - NB_A])

        def ot_count(n):
            return n // 3 + 1

        def w_load(sp, b):
            if b >= 2:
                sp.wait_ge(S["w_lo"], b - 1)
            sp.dma_start((raw if b < NB_U + NB_A else mraw)[b % 2],
                         w_in[:, block_cols(b):block_cols(b) + WC].rearrange("(k p) c -> p k c", p=P)).then_inc(ld_w(b), 16)

        def w_max(dve, b):
            dve.wait_ge(ld_w(b), 16 * (b // 2 + 1))
            if b >= 3:
                dve.wait_ge(S["w_all"], b - 2)
            dve.tensor_reduce(amax[b % 3], (raw if b < NB_U + NB_A else mraw)[b % 2].rearrange("p k c -> p (k c)"), AX.X,
                              ALU.max, apply_absolute_value=True).then_inc(S["w_amax"], 1)

        def w_allmax(pool, b):
            pool.wait_ge(S["w_amax"], b + 1)
            if b >= 3:
                pool.wait_ge(S["w_scale"], b - 2)
            pool.partition_all_reduce(amax_all[b % 3], amax[b % 3], P, bass.bass_isa.ReduceOp.max).then_inc(S["w_all"], 1)

        def w_hi(act, b):
            act.wait_ge(S["w_scale"], b + 1)
            if b >= 3:
                wait_block_used(act, b - 3)
            early = b < NB_U + NB_A
            act.activation((ring if early else mring)[b % 3][:, 0], (raw if early else mraw)[b % 2], ACT.Copy,
                           scale=wscale[b % 3]).then_inc(S["w_hi"], 1)

        def power_of_two(dve, chain, settle, out, mx, low):
            chain(dve.tensor_scalar(out.bitcast(I32), mx.bitcast(I32), 0x7F800000, None, ALU.bitwise_and))
            settle()
            chain(dve.tensor_scalar(out, out, 2.0 ** -86, low, ALU.max, ALU.mult))
            settle()

        def w_split(dve, chain, settle, b):
            i = b % 3
            dve.wait_ge(S["w_all"], b + 1)
            if b >= 3:
                dve.wait_ge(S["w_lo"], b - 2)
            power_of_two(dve, chain, settle, wexp[i], amax_all[i], 2.0 ** -14)
            chain(dve.reciprocal(wscale[i], wexp[i]))
            query = NB_U <= b < NB_U + NB_A and (b - NB_U) % 3 == 0
            dve.tensor_scalar(descale[b], wexp[i], xdescale, HD ** -0.5 if query else 1.0, ALU.mult, ALU.mult
                              ).then_inc(S["w_scale"], 1)
            settle()
            dve.wait_ge(S["w_hi"], b + 1)
            early = b < NB_U + NB_A
            w = (ring if early else mring)[i]
            dve.scalar_tensor_tensor(w[:, 1], (raw if early else mraw)[b % 2], wscale[i], w[:, 0], ALU.mult, ALU.subtract
                                     ).then_inc(S["w_lo"], 1)

        PREPARED = NB_U + NB_A

        def prepare(H, m, split, largest):
            _, _, b, first = ptile(H, m)
            if first and b + 2 < PREPARED:
                split(b + 2)
            if first and b + 3 < PREPARED:
                largest(b + 3)

        ld_bias = [sem(f"ld_bias{i}") for i in range(2)]
        block = ctx.enter_context(nc.Block())

        @block.sync
        def _(sp):
            sp.dma_start(ident, cst["ident"]).then_inc(S["ld_small"], 16)
            r0 = 0
            for src, cnt in ((ins["conv_w"][0].rearrange("j (c p) -> (j c) p", p=P), 9 * KD),
                             (ins["conv_b"][0].rearrange("(c p) -> c p", p=P), 3 * KD),
                             (ins["pre_norm_g"][0].rearrange("(c p) -> c p", p=P), KD),
                             (ins["hyena_skip"][0].rearrange("o (c p) -> (o c) p", p=P), 2 * KD)):
                sp.dma_start(rows[r0:r0 + cnt, :], src).then_inc(S["ld_small"], 16)
                r0 += cnt
            for i, name in enumerate(("filt_b1", "filt_b2", "filt_b3", "filt_freq")):
                sp.dma_start(frows[i:i + 1, :], ins[name]).then_inc(S["ld_small"], 16)
            for G in range(3):
                src = ins["x_prompt"][0, BANK * G:BANK * G + BANK, :] if G < 2 else ins["x_sample"][0]
                sp.dma_start(xt[:, 4 * G:4 * G + 4, :], src.rearrange("(t p) d -> p t d", p=P)).then_inc(ld_x[G], 16)
            sp.dma_start(feat[0:FEMB, :], cst["feat"]).then_inc(S["ld_tabs"], 16)
            sp.dma_start(fw[0:FEMB, 0:FHID], ins["filt_w1"][0]).then_inc(S["ld_tabs"], 16)
            sp.dma_start(fw[0:FHID, FHID:2 * FHID], ins["filt_w2"][0]).then_inc(S["ld_tabs"], 16)
            sp.dma_start(fw[0:FHID, 2 * FHID:3 * FHID], ins["filt_w3"][0]).then_inc(S["ld_tabs"], 16)
            sp.dma_start(hot[0:NBUCK, :], cst["hot"]).then_inc(S["ld_tabs"], 16)
            sp.dma_start(mask[0:HEADS, :], cst["mask"]).then_inc(S["ld_tabs"], 16)
            sp.dma_start(relb[0:NBUCK, :], ins["rel_bias"]).then_inc(S["ld_tabs"], 16)
            for b in range(NB_U + NB_A):
                w_load(sp, b)
            sp.wait_ge(S["a_ready"], PT0[6])
            sp.wait_ge(S["a_ov"], NSTEP)
            sp.wait_ge(S["hn_saved"], 16)
            for sl in range(3):
                sp.wait_ge(ot_out[sl], 16 * ot_count(6 * NT - 1))

            def load_filter(i):
                s, q, o = ITEMS[i]
                if i >= 2:
                    sp.wait_ge(S["f_gen"], GEN0[i - 1])
                sp.dma_start(w4[i % 2][0:FHID, :].rearrange("p (e c) -> p e c", e=2),
                             ins["filt_w4"][0].rearrange("k (o e c) -> k o e c", o=2, e=2)[:, o, :, FQ * q:FQ * q + FQ]
                             ).then_inc(ld_w4[i % 2], 16)
                if i >= 1:
                    sp.wait_ge(S["f_gen_used"], GEN0[i])
                sp.dma_start(dec[:, 0:ntile(i) + 1, :],
                             cst[f"dec{s}"][:, FQ * q:FQ * q + FQ].rearrange("(t p) c -> p t c", p=P)
                             ).then_inc(ld_dec, 16)

            def load_signal(i):
                s, q, o = ITEMS[i]
                if o == 0:
                    if i >= 2:
                        sp.wait_ge(hy_out[q % 2], 16 * zc_uses(i - 2))
                    sp.dma_start(zc[q % 2][:, :, 0:LENS[s]],
                                 uc_d[2 * q:2 * q + 2, :, UC0[s]:UC0[s] + LENS[s]].rearrange("c p t -> p c t")
                                 ).then_inc(ld_zc[q % 2], 16)

            load_filter(0)
            load_signal(0)
            sp.dma_start(ftab, cst["fwd0"]).then_inc(S["ld_ftab"], 16)
            sp.dma_start(itab, cst["inv0"]).then_inc(S["ld_itab"], 16)
            for i in range(NI):
                s, q, o = ITEMS[i]
                if i + 1 < NI:
                    load_filter(i + 1)
                    load_signal(i + 1)
                if i >= 1:
                    sp.wait_ge(S["f_post"], 2 * i)
                c0 = KD * (1 + o) + 2 * q
                sp.dma_start(hx[:, :, 0:LENS[s]], uc_d[c0:c0 + 2, :, UC0[s]:UC0[s] + LENS[s]].rearrange("c p t -> p c t")
                             ).then_inc(S["ld_hx"], 16)
                if i + 1 < NI and ITEMS[i + 1][0] != s:
                    for u in range(uz[i] + npair(i) - 4, uz[i] + npair(i)):
                        wait_ready(sp, u)
                    sp.dma_start(ftab[:, 0:DFTS[1]["fwd"].shape[1]], cst["fwd1"]).then_inc(S["ld_ftab"], 16)
                    for u in range(ui[i] + 4, ui[i] + 8):
                        wait_ready(sp, u)
                    sp.dma_start(itab[:, 0:DFTS[1]["inv"].shape[1]], cst["inv1"]).then_inc(S["ld_itab"], 16)
            for u in range(f_units - 4, f_units):
                wait_ready(sp, u)
            sp.wait_ge(S["f_post"], 2 * NI)
            for sl in range(2):
                sp.wait_ge(hy_out[sl], 16 * zc_uses(NI - 1))
            M0 = NB_U + NB_A
            w_load(sp, M0)
            w_load(sp, M0 + 1)
            sp.dma_start(hn_words, hn_d).then_inc(S["ld_hm"], 16)
            w_load(sp, M0 + 2)
            w_load(sp, M0 + 3)
            ahead = iter(((4, 5, 6), (7,), (8,), (9,), (10, 11, 12, 13), (), (), ()))
            for kind in range(2):
                for q in range(4):
                    if kind or q:
                        m_all(sp, (MT_A, MT_H)[kind] + 4 * NSP * q if q else MT_GH)
                    w = (w_a, w_h)[kind]
                    sp.dma_start(wb[:, 0:w.shape[0] // P, :], w[:, WC * q:WC * q + WC].rearrange("(k p) c -> p k c", p=P)
                                 ).then_inc(S["ld_wb"], 16)
                    for b in next(ahead):
                        w_load(sp, M0 + b)
            sp.wait_ge(S["w_lo"], NB)
            m_all(sp, M_DONE[NB_M - 2])
            sp.dma_start(wo, w_o.rearrange("(k p) c -> p k c", p=P)).then_inc(ld_wo, 16)
            m_all(sp, MT_O)
            sp.dma_start(gpost, ins["post_norm_g"].to_broadcast([P, D])).then_inc(S["ld_gain"], 16)
            for t in range(NT):
                if t >= 2:
                    sp.wait_ge(S["o_y"], t - 1)
                src = ins["x_prompt"][0, P * t:P * t + P, :] if t < SP // P else ins["x_sample"][0, P * t - SP:P * t - SP + P, :]
                sp.dma_start(xres[t % 2], src).then_inc(ld_xr[t % 2], 16)

        NSMALL, NTABS = 16 * 9, 16 * 7

        @block.gpsimd
        def _(pool):
            for c in (0, COL_P + SP, COL_S + SS):
                pool.memset(hn_words.rearrange("p (k c) -> p k c", k=2 * KD)[:, :, c // 2:(c + PADC) // 2], 0.0
                            ).then_inc(S["pads_ok"], 1)
            for b in range(2):
                for c in (0, 1 + SP, UC_W + 1):
                    pool.memset(ub[b][:, c:c + 1], 0.0).then_inc(S["pads_ok"], 1)
            pool.wait_ge(S["g_amax"], 1)
            pool.partition_all_reduce(gmax_all, gmax, P, bass.bass_isa.ReduceOp.max).then_inc(S["g_all"], 1)
            for b in range(3):
                w_allmax(pool, b)
            pool.wait_ge(S["n_evD"], 24)
            pool.wait_ge(S["pads_ok"], 3)
            pool.dma_start(hn_d, hn_words).then_inc(S["hn_saved"], 16)
            pool.wait_ge(S["b_rows"], 1)
            pool.dma_start(brow_d, mask[0:HEADS, :].unsqueeze(1).to_broadcast([HEADS, P, 3 * BANK])).then_inc(S["b_stored"], 16)
            for c in range(3 * KD):
                if c % 2 == 0 and c // 2 + 3 < PREPARED:
                    w_allmax(pool, c // 2 + 3)
                pool.wait_ge(S["u_conv"], c + 1)
                pool.dma_start(uc_d[c], ut[c % 3]).then_inc(uc_out[c % 3], 16)
            def skewed(g, q0, n, h0, width):
                return bass.AP(dram["brow"], BANK * g + q0 + h0 * P * 3 * BANK, [[3 * BANK - 1, n], [P * 3 * BANK, HH], [1, width]])

            for i in range(3):
                pool.wait_ge(uc_out[i], 16 * KD)
            pool.wait_ge(S["b_stored"], 16)
            pool.wait_ge(S["h_sin"], 3)
            pool.wait_ge(S["n_T"], 24)
            for b in range(2):
                for c in (0, COL_P + SP, COL_S + SS):
                    pool.memset(kt[b][:, :, c:c + PADC], 0.0).then_inc(S["pads_ok"], 1)

            def load_bias(H):
                g, h0 = H // 2, HH * (H % 2)
                if H >= 2:
                    pool.wait_ge(S["a_biased"], STEPS * (H - 1))
                if g < 2:
                    pool.dma_start(bwt[H % 2], skewed(g, P - 1, P, h0, BW)).then_inc(ld_bias[H % 2], 16)
                else:
                    for seq in range(2):
                        pool.dma_start(b2t[H % 2][:, :, P * seq:P * seq + P],
                                       skewed(2, P - 1 + seq * (2 * P - 1), P, h0, P)).then_inc(ld_bias[H % 2], 16)

            load_bias(0)
            load_bias(1)
            for m in range(NPT[0]):
                prepare(0, m, lambda b: None, lambda b: w_allmax(pool, b))
            for N in range(NSTEP + 2):
                if N % STEPS == 0 and 0 < N < NSTEP - STEPS:
                    load_bias(N // STEPS + 1)
                if 1 <= N <= NSTEP:
                    for H, m in MIX[N - 1]:
                        prepare(H, m, lambda b: None, lambda b: w_allmax(pool, b))
                if N >= 3 and N % 2 == 1:
                    H, g, t, _ = unit(N - 2)
                    n = (N - 3) // 2
                    pool.wait_ge(S["a_oevac"], n + 1)
                    seq = 0 if t < SP // P else 1
                    r, tt = stride(g, seq), t - TOK0[seq] // P
                    per = LENS[seq] // r
                    a = TOK0[seq] + P * tt // per + r * (P * tt % per)
                    pool.dma_start(og_d[g, a:a + r * (P - 1) + 1:r, H % 2, :], ot[n % 3]).then_inc(ot_out[n % 3], 16)
            def sums(i, j):
                n = GEN0[i] + j
                h = hfb[n % 2]
                pool.wait_ge(S["f_gen_used"], n + 1)
                if i >= 1:
                    pool.wait_ge(S["f_bf"], 3 * i - 1)
                nc.gpsimd.tensor_tensor(tge[:, j, :], h[:, 0:FQ], h[:, FQ:2 * FQ], ALU.add)
                nc.gpsimd.tensor_tensor(tgo[:, j, :], h[:, 0:FQ], h[:, FQ:2 * FQ], ALU.subtract).then_inc(S["f_ge"], 1)

            for j in range(ntile(0)):
                sums(0, j)
            for i in range(NI):
                for p in range(npair(i)):
                    n = PR0[i] + p
                    a = pq[n % 2]
                    wait_free(pool, uz[i] + p)
                    nc.gpsimd.tensor_tensor(yf[:, p, 0:FQ], a[:, 0:FQ], a[:, 3 * FQ:4 * FQ], ALU.subtract)
                    nc.gpsimd.tensor_tensor(yf[:, p, FQ:2 * FQ], a[:, FQ:2 * FQ], a[:, 2 * FQ:3 * FQ], ALU.add
                                            ).then_inc(S["f_y"], 1)
                    if i + 1 < NI and p < ntile(i + 1):
                        sums(i + 1, p)
                s, q, o = ITEMS[i]
                if o == 1:
                    pool.wait_ge(S["f_post"], 2 * (i + 1))
                    pool.dma_start(hy_d[2 * q:2 * q + 2, :, TOK0[s]:TOK0[s] + LENS[s]].rearrange("c p t -> p c t"),
                                   zc[q % 2][:, :, 0:LENS[s]]).then_inc(hy_out[q % 2], 16)
            M0 = NB_U + NB_A
            for b in range(3):
                w_allmax(pool, M0 + b)
            for t in range(NT):
                if t == 0:
                    w_allmax(pool, M0 + 3)
                if t == 1:
                    w_allmax(pool, M0 + 4)
                if t == 0:
                    for u in range(f_units - 4, f_units):
                        wait_ready(pool, u)
                    pool.wait_ge(S["f_post"], 2 * NI)
                    for sl in range(2):
                        pool.wait_ge(hy_out[sl], 16 * zc_uses(NI - 1))
                    for sl in range(3):
                        pool.wait_ge(ot_out[sl], 16 * ot_count(6 * NT - 1))
                if t >= 2:
                    pool.wait_ge(S["g_cmb"], t - 1)
                pool.dma_start(ogt[t % 2], og_d[:, P * t:P * t + P, :, :].rearrange("g p a c -> p g a c")).then_inc(ld_og[t % 2], 16)
            for b in range(5, 9):
                w_allmax(pool, M0 + b)
            m_all(pool, MT_GH)
            m_allfree(pool, MT_GH)
            for j in range(KD):
                pool.dma_start(hg[:, j, :], hy_d[j]).then_inc(ld_hy[j], 16)
            for b in range(9, NB_M):
                w_allmax(pool, M0 + b)
            for t in range(NT):
                pool.wait_ge(S["o_y"], t + 1)
                dst = y_p[0, P * t:P * t + P, :] if t < SP // P else y_s[0, P * t - SP:P * t - SP + P, :]
                pool.dma_start(dst, yout[t % 2]).then_inc(y_out[t % 2], 16)
            for sl in range(2):
                pool.wait_ge(y_out[sl], 16 * (NT // 2))

        @block.tensor
        def _(pe):
            def split_product(out, n, lhs, rhs):
                for k in range(n):
                    for x, (a, b) in enumerate(((0, 0), (0, 1), (1, 0))):
                        mm = pe.matmul(out, lhs(a, k), rhs(b, k), start=(k == 0 and x == 0), stop=(k == n - 1 and x == 2))
                return mm

            pe.wait_ge(S["ld_small"], NSMALL)
            pe.transpose(ps[:, 0, 0:NCOLS], rows[0:NCOLS, :], ident[0:NCOLS, 0:NCOLS])
            pe.transpose(ps[0:FHID, 0, P:P + 4], frows[0:4, :], ident[0:4, 0:4]).then_inc(S["rows_T"], 1)
            pe.wait_ge(S["fcols_ok"], 1)
            for G in range(3):
                for k in range(KD):
                    n = KD * G + k
                    if k == 0:
                        pe.wait_ge(S["n_scaled"], 4 * (G + 1))
                    if n >= 4:
                        pe.wait_ge(S["n_evD"], n - 3)
                    for j in range(4):
                        mm = pe.transpose(ps[:, n % 4, P * j:P * j + P], xt[:, 4 * G + j, P * k:P * k + P], ident)
                    mm.then_inc(S["n_T"], 1)
            pe.wait_ge(S["n_evD"], 24)
            pe.wait_ge(S["pads_ok"], 9)
            pe.wait_ge(S["ld_tabs"], NTABS)
            for g in range(3):
                mm = pe.matmul(ps[0:HEADS, g, :], relb[0:NBUCK, HEADS * g:HEADS * g + HEADS],
                               hot[0:NBUCK, BANK * g:BANK * g + BANK], start=True, stop=True)
            mm.then_inc(S["b_mm"], 1)

            def filter_layer(l):
                if l == 0:
                    pe.wait_ge(S["b_rows"], 1)
                else:
                    pe.wait_ge(S["h_sin"], l)
                kk = FEMB if l == 0 else FHID
                for s in range(3):
                    src = feat if l == 0 else hid
                    mm = pe.matmul(ps[0:FHID, s, :], fw[0:kk, FHID * l:FHID * l + FHID],
                                   src[0:kk, BANK * s:BANK * s + BANK], start=True, stop=True)
                mm.then_inc(S["h_mm"], 1)

            for c in range(3 * KD):
                b = c // 2
                if c % 2 == 0:
                    pe.wait_ge(S["w_lo"], b + 1)
                for s in range(NSP):
                    n = NSP * c + s
                    if n >= 4:
                        pe.wait_ge(S["u_evac"], n - 3)
                    split_product(ps[:, 4 + n % 4, :], KD,
                                  lambda a, k: ring[b % 3][:, a, k, P * (c % 2):P * (c % 2) + P],
                                  lambda a, k: hn[:, a, k, SPANS[s]:SPANS[s] + BANK]).then_inc(S["u_ready"], 1)
                if c in (2, 6, 10):
                    filter_layer((c - 2) // 4)
            pe.wait_ge(S["u_evac"], U_TILES)
            pe.wait_ge(S["h_arg"], 3)

            def project(H, m):
                kind, i, b, first = ptile(H, m)
                n = PT0[H] + m
                if first:
                    pe.wait_ge(S["w_lo"], b + 1)
                if n >= 2:
                    pe.wait_ge(S["a_evac"], n - 1)
                w = ring[b % 3]
                if kind < 2:
                    j, s = i // NSP, i % NSP
                    mm = split_product(ps[:, n % 2, :], KD, lambda a, k: w[:, a, k, P * j:P * j + P],
                                       lambda a, k: hn[:, a, k, SPANS[s]:SPANS[s] + BANK])
                else:
                    for x in range(2):
                        c, r = value_tiles(H // 2)[2 * i + x]
                        mm = split_product(ps[:, n % 2, HW * x:HW * x + HW], KD,
                                           lambda a, k: hn[:, a, k, c:c + r * (P - 1) + 1:r], lambda a, k: w[:, a, k, :])
                mm.then_inc(S["a_ready"], 1)

            def score(N):
                H, g, t, h = unit(N)
                if N % STEPS == 0:
                    pe.wait_ge(S["a_evac"], PT0[H] + 4 * NSP)
                    if N == 0:
                        pe.wait_ge(S["pads_ok"], 15)
                k0, kw = windows(g, t)[:2]
                if N >= 2:
                    pe.wait_ge(S["a_biased"], N - 1)
                for x in range(2):
                    r = slice(HD * h, HD * h + HD)
                    mm = pe.matmul(ps[:, 2 + N % 2, 2 * P * x:2 * P * x + kw], qt[H % 2][r, x, P * t:P * t + P],
                                   kt[H % 2][r, x, k0:k0 + kw], start=True, stop=True)
                mm.then_inc(S["a_score"], 1)

            def turn(N):
                H, g, t, h = unit(N)
                kw = windows(g, t)[1]
                pe.wait_ge(S["a_prob"], 2 * N + 2)
                if N >= 2:
                    pe.wait_ge(S["a_ptcopied"], N - 1)
                for x in range(2):
                    for b in range(kw // P):
                        mm = pe.transpose(ps[:, 4 + N % 2, 2 * P * x + P * b:2 * P * x + P * b + P],
                                          pr[N % 2][:, x, P * b:P * b + P], ident)
                mm.then_inc(S["a_pT"], 1)

            def value(N):
                H, g, t, h = unit(N)
                vs = windows(g, t)[3]
                if N % STEPS == 0:
                    pe.wait_ge(S["a_evac"], PT0[H + 1])
                pe.wait_ge(S["a_ptcopied"], N + 1)
                if h == 0 and N >= 4:
                    pe.wait_ge(S["a_oevac"], N // 2 - 1)
                for x in range(2):
                    for b, vi in enumerate(vs):
                        c = slice(HD * (h + 2 * x), HD * (h + 2 * x) + HD)
                        mm = pe.matmul(ps[:, 6 + t % 2, c], pt[N % 2][:, x, P * b:P * b + P], vt[H % 2][:, vi, c],
                                       start=(b == 0), stop=(b == len(vs) - 1))
                mm.then_inc(S["a_ov"], 1)

            for m in range(NPT[0]):
                project(0, m)
            score(0)
            for N in range(NSTEP + 1):
                if N + 1 < NSTEP:
                    score(N + 1)
                if N < NSTEP:
                    turn(N)
                if N >= 1:
                    value(N - 1)
                if N < NSTEP:
                    for H, m in MIX[N]:
                        project(H, m)
            pe.wait_ge(S["a_ptcopied"], NSTEP)
            pe.wait_ge(S["a_oevac"], 6 * NT)

            def gen(i, j):
                s = ITEMS[i][0]
                if j == 0:
                    pe.wait_ge(ld_w4[i % 2], 16 * (i // 2 + 1))
                n = GEN0[i] + j
                if n >= 2:
                    pe.wait_ge(S["f_gen_used"], n - 1)
                pe.matmul(ps[:, n % 2, :], h3[0:FHID, TOK0[s] + P * j:TOK0[s] + P * j + P], w4[i % 2][0:FHID, :],
                          start=True, stop=True).then_inc(S["f_gen"], 1)

            def spectrum(out, terms, a):
                for x, (comp, c, tab) in enumerate(terms):
                    mm = pe.matmul(out, ftab[:, P * tab:P * tab + P], a[:, comp, FQ * c:FQ * c + FQ],
                                   start=(x == 0), stop=(x == len(terms) - 1))
                return mm

            def filter_dft(i):
                s = ITEMS[i][0]
                pe.wait_ge(S["ld_ftab"], 16 * (s + 1))
                pe.wait_ge(S["f_bf"], 3 * i + 1)
                ge, go = fa[3 * i % 2], fa[(3 * i + 1) % 2]
                pairs, half = DFTS[s]["pairs"], npair(i) // 2
                for n in range(npair(i) + 1):
                    u = uk[i] + n
                    if u >= 4:
                        wait_free(pe, u - 4)
                    if n == half + 1:
                        pe.wait_ge(S["f_bf"], 3 * i + 2)
                    if n == half:
                        mm = spectrum(ps[:, fbank(u), 0:FQ], pairs[0][3], ge)
                    else:
                        for x in range(2):
                            terms = pairs[2 * n + x][0] if n < half else pairs[2 * (n - half - 1) + x][2]
                            mm = spectrum(ps[:, fbank(u), FQ * x:FQ * x + FQ], terms, ge if n < half else go)
                    mm.then_inc(bank_ready[fbank(u)], 1)

            def signal_dft(i):
                s = ITEMS[i][0]
                pe.wait_ge(S["f_bf"], 3 * i + 3)
                a = fa[(3 * i + 2) % 2]
                for p in range(npair(i)):
                    u = uz[i] + p
                    wait_free(pe, u - 4)
                    spectrum(ps[:, fbank(u), 0:FQ], DFTS[s]["pairs"][p][0], a)
                    spectrum(ps[:, fbank(u), FQ:2 * FQ], DFTS[s]["pairs"][p][1], a
                             ).then_inc(bank_ready[fbank(u)], 1)
                    if i + 1 < NI and p < ntile(i + 1):
                        gen(i + 1, p)

            def inverse(i):
                s = ITEMS[i][0]
                pe.wait_ge(S["ld_itab"], 16 * (s + 1))
                for ct in range(2):
                    for x, blk in enumerate(ORDER):
                        u = ui[i] + 4 * ct + x
                        wait_free(pe, u - 4)
                        terms = DFTS[s]["units"][blk]
                        if ct == 0:
                            pe.wait_ge(S["f_y"], PR0[i] + max(term[0] for term in terms) + 1)
                        for n, (p, im, col, oc, w) in enumerate(terms):
                            starts = n == 0 or terms[n - 1][3] != oc
                            stops = n == len(terms) - 1 or terms[n + 1][3] != oc
                            mm = pe.matmul(ps[:, fbank(u), oc:oc + w],
                                           yf[:, p, FQ * im + P * ct:FQ * im + P * ct + P], itab[:, col:col + w],
                                           start=starts, stop=stops)
                        mm.then_inc(bank_ready[fbank(u)], 1)

            def to_time(i):
                s, q, o = ITEMS[i]
                if o == 0:
                    pe.wait_ge(ld_zc[q % 2], 16 * zc_uses(i))
                else:
                    pe.wait_ge(S["f_post"], 2 * (i - 1))
                for j in range(ntile(i) // 2):
                    n = TR0[i] + j
                    if n >= 2:
                        pe.wait_ge(S["f_tz"], n - 1)
                    for x in range(4):
                        a = P * (2 * j + x // 2)
                        mm = pe.transpose(ps[:, 6 + n % 2, P * x:P * x + P], zc[q % 2][:, x % 2, a:a + P], ident)
                    mm.then_inc(S["f_zT"], 1)

            for j in range(ntile(0)):
                gen(0, j)
            to_time(0)
            filter_dft(0)
            for i in range(NI):
                signal_dft(i)
                if i + 1 < NI:
                    to_time(i + 1)
                inverse(i)
                if i + 1 < NI:
                    filter_dft(i + 1)
            for u in range(f_units - 4, f_units):
                wait_free(pe, u)
            pe.wait_ge(S["f_gen_used"], GEN0[NI])
            pe.wait_ge(S["f_tz"], TR0[NI])
            pe.wait_ge(S["ld_hm"], 16)

            def m_tile(n, kc, lhs, rhs):
                if n >= 8:
                    m_waitfree(pe, n - 8)
                for k in range(kc):
                    mm = pe.matmul(ps[:, n % 8, :], lhs(k), rhs(k), start=(k == 0), stop=(k == kc - 1))
                mm.then_inc(m_done[n % 8], 1)

            def gate_tiles(n0, i, d):
                b = NB_U + NB_A + i
                pe.wait_ge(S["w_lo"], b + 1)
                for s in range(NSP):
                    if n0 + s >= 8:
                        m_waitfree(pe, n0 + s - 8)
                    split_product(ps[:, (n0 + s) % 8, :], KD, lambda a, k: mring[b % 3][:, a, k, P * (d % 2):P * (d % 2) + P],
                                  lambda a, k: hn[:, a, k, SPANS[s]:SPANS[s] + BANK]).then_inc(m_done[(n0 + s) % 8], 1)

            for j in range(4):
                gate_tiles(MT_GA + NSP * j, j // 2, j)
            for t in range(NT):
                n = MT_T + t
                m_waitfree(pe, n - 8)
                pe.wait_ge(S["g_cmb"], t + 1)
                for x in range(4):
                    mm = pe.transpose(ps[:, n % 8, P * x:P * x + P], cmb[t % 2][:, 0, P * x:P * x + P], ident)
                mm.then_inc(m_done[n % 8], 1)
            for kind, n0, i0, kc, src in ((0, MT_A, 2, 4, at), (1, MT_H, 10, KD, hg)):
                if kind == 1:
                    for j in range(KD):
                        gate_tiles(MT_GH + NSP * j, 6 + j // 2, j)
                for d in range(KD):
                    gate_tiles(n0 + 2 * NSP * d, i0 + d // 2, d)
                    if d == 0:
                        if kind == 0:
                            m_allfree(pe, MT_A)
                        else:
                            pe.wait_ge(S["m_mul"], KD * NSP)
                    pe.wait_ge(S["ld_wb"], 16 * (4 * kind + d // 2 + 1))
                    for s in range(NSP):
                        m_tile(n0 + 2 * NSP * d + NSP + s, kc, lambda k: wb[:, k, P * (d % 2):P * (d % 2) + P],
                               lambda k: src[:, k, BANK * s:BANK * s + BANK])
            m_allfree(pe, MT_O)
            pe.wait_ge(S["m_acc"], KD * NSP)
            pe.wait_ge(ld_wo, 16)
            for t in range(NT):
                for half in range(2):
                    m_tile(MT_O + 2 * t + half, KD, lambda k: mt[:, k, P * t:P * t + P],
                           lambda k: wo[:, k, BANK * half:BANK * half + BANK])

        @block.scalar
        def _(act):
            for G in range(3):
                act.wait_ge(ld_x[G], 16)
                for t in range(4 * G, 4 * G + 4):
                    if t >= 2:
                        act.wait_ge(S["n_sq"], t - 1)
                    act.activation(junk[t % 2], xt[:, t, :], ACT.Square, accum_out=ssq[:, t:t + 1]).then_inc(S["n_sq"], 1)
                act.wait_ge(S["n_mean"], G + 1)
                act.activation(rstd[:, 4 * G:4 * G + 4], rstd[:, 4 * G:4 * G + 4], ACT.Sqrt).then_inc(S["n_root"], 1)
            for b in range(2):
                w_hi(act, b)
            act.wait_ge(S["g_scale"], 1)
            for n in range(24):
                G, k = n // KD, n % KD
                act.wait_ge(S["n_T"], n + 1)
                act.activation(hn[:, 0, k, SPANS[G]:SPANS[G] + BANK], ps[:, n % 4, :], ACT.Copy, scale=gscaled[:, k:k + 1]
                               ).then_inc(S["n_evA"], 1)

            def sine(l):
                act.wait_ge(S["h_arg"], l + 1)
                dst = hid if l < 2 else h3
                act.activation(dst[0:FHID, :], xt[0:FHID, 3:5, :].rearrange("p a c -> p (a c)")[:, 0:T], ACT.Sin
                               ).then_inc(S["h_sin"], 1)

            act.wait_ge(S["pads_ok"], 9)
            for c in range(3 * KD):
                u, o = ub[c % 2], ut[c % 3]
                if c % 2 == 0 and c // 2 + 2 < PREPARED:
                    w_hi(act, c // 2 + 2)
                for s in range(NSP):
                    n = NSP * c + s
                    act.wait_ge(S["u_ready"], n + 1)
                    if s == 0 and c >= 2:
                        act.wait_ge(S["u_conv"], c - 1)
                    at0 = 1 + BANK * s + (s == 2)
                    act.activation(u[:, at0:at0 + BANK], ps[:, 4 + n % 4, :], ACT.Copy, scale=descale[c // 2]
                                   ).then_inc(S["u_evac"], 1)
                act.wait_ge(S["u_evac"], NSP * (c + 1))
                if c >= 3:
                    act.wait_ge(uc_out[c % 3], 16 * (c // 3))
                act.activation(o, u[:, 1:1 + UC_W], ACT.Identity, scale=cols[:, CW + 3 * KD + c:CW + 3 * KD + c + 1],
                               bias=cols[:, CB + c:CB + c + 1]).then_inc(S["u_mid"], 1)
                if c in (4, 8, 12):
                    sine((c - 4) // 4)
            act.wait_ge(S["u_conv"], 3 * KD)
            for i in range(3):
                act.wait_ge(uc_out[i], 16 * KD)
            act.wait_ge(S["b_stored"], 16)

            def evacuate(H, m):
                prepare(H, m, lambda b: w_hi(act, b), lambda b: None)
                kind, i, b, _ = ptile(H, m)
                n, g = PT0[H] + m, H // 2
                src = ps[:, n % 2, :]
                act.wait_ge(S["a_ready"], n + 1)
                if kind == 2:
                    dst = vt[H % 2][:, 2 * i:2 * i + 2, :]
                    src = src.rearrange("p (a c) -> p a c", a=2)
                else:
                    j, s = i // NSP, i % NSP
                    seq = 0 if s < 2 else 1
                    r = stride(g, seq)
                    if g == 0 and kind == 1:
                        dst = kt[H % 2][:, j, SPANS[s]:SPANS[s] + BANK]
                    else:
                        i0 = BANK * s // r if seq == 0 else 0
                        buf = (qt, kt)[kind][H % 2][:, j, TOK0[seq]:TOK0[seq] + LENS[seq]]
                        dst = buf.rearrange("p (r i) -> p r i", r=r)[:, :, i0:i0 + BANK // r]
                        src = src.rearrange("p (i r) -> p r i", r=r)
                act.activation(dst, src, ACT.Copy, scale=descale[b]).then_inc(S["a_evac"], 1)

            def prob(N):
                H, g, t, h = unit(N)
                kw = windows(g, t)[1]
                o = ot[N // 2 % 3]
                act.wait_ge(S["a_max"], N + 1)
                if N >= 2:
                    act.wait_ge(S["a_pT"], N - 1)
                for x in range(2):
                    c = HW + h + 2 * x
                    act.activation(pr[N % 2][:, x, 0:kw], lg[N % 2][:, x, 0:kw], ACT.Exp, bias=o[:, c:c + 1],
                                   accum_out=o[:, c + HH:c + HH + 1]).then_inc(S["a_prob"], 1)

            def copy(N):
                kw = windows(unit(N)[1], unit(N)[2])[1]
                act.wait_ge(S["a_pT"], N + 1)
                if N >= 2:
                    act.wait_ge(S["a_ov"], N - 1)
                act.activation(pt[N % 2][:, :, 0:kw], ps[:, 4 + N % 2, :].rearrange("p (x c) -> p x c", x=2)[:, :, 0:kw],
                               ACT.Copy).then_inc(S["a_ptcopied"], 1)

            def result(n):
                act.wait_ge(S["a_ov"], 2 * n + 2)
                if n >= 3:
                    act.wait_ge(ot_out[n % 3], 16 * ot_count(n - 3))
                act.activation(ot[n % 3][:, 0:HW], ps[:, 6 + n % 2, 0:HW], ACT.Copy).then_inc(S["a_oevac"], 1)

            for m in range(NPT[0]):
                evacuate(0, m)
            prob(0)
            for N in range(NSTEP + 2):
                if N < NSTEP:
                    copy(N)
                if 1 <= N <= NSTEP:
                    for H, m in MIX[N - 1]:
                        evacuate(H, m)
                if N + 1 < NSTEP:
                    prob(N + 1)
                if N >= 3 and N % 2 == 1:
                    result((N - 3) // 2)
            def filter_copy(i):
                if i >= 1:
                    for u in range(uz[i - 1] + npair(i - 1) - 4, uz[i - 1] + npair(i - 1)):
                        wait_free(act, u)
                half = npair(i) // 2
                for n in range(npair(i) + 1):
                    u = uk[i] + n
                    wait_ready(act, u)
                    src = ps[:, fbank(u), :].rearrange("p (a c) -> p a c", a=2)
                    if n == half:
                        src, dst = ps[:, fbank(u), 0:FQ], kfl
                    elif n < half:
                        dst = kf[:, 2 * n:2 * n + 2, 0:FQ]
                    else:
                        dst = kf[:, 2 * (n - half - 1):2 * (n - half), FQ:2 * FQ]
                    act.activation(dst, src, ACT.Copy).then_inc(bank_free[fbank(u)], 1)

            def time_copy(i):
                if i >= 1:
                    act.wait_ge(S["f_bf"], 3 * i)
                for j in range(ntile(i) // 2):
                    n = TR0[i] + j
                    act.wait_ge(S["f_zT"], n + 1)
                    act.activation(tz[:, 2 * j:2 * j + 2, :], ps[:, 6 + n % 2, :].rearrange("p (a c) -> p a c", a=2),
                                   ACT.Copy).then_inc(S["f_tz"], 1)

            time_copy(0)
            filter_copy(0)
            for i in range(NI):
                w2 = 2 * DFTS[ITEMS[i][0]]["w"]
                if i + 1 < NI:
                    time_copy(i + 1)
                for ct in range(2):
                    m = 2 * i + ct
                    for x, dst in ((0, iv0), (1, iv1)):
                        u = ui[i] + 4 * ct + x
                        if m >= 2:
                            act.wait_ge(S["f_post"], m - 1)
                        wait_ready(act, u)
                        act.activation(dst[m % 2][:, 0:w2], ps[:, fbank(u), 0:w2], ACT.Copy
                                       ).then_inc(bank_free[fbank(u)], 1)
                if i + 1 < NI:
                    filter_copy(i + 1)
            act.wait_ge(S["ld_hm"], 16)

            def combine(t):
                act.wait_ge(S["g_sc"], 2 * t + 1)
                act.activation(wts[t % 2][:, 8:32], wts[t % 2][:, 8:32], ACT.Exp).then_inc(S["g_exp"], 1)

            M0 = NB_U + NB_A
            w_hi(act, M0)
            w_hi(act, M0 + 1)
            for n in range(MT_GA, MT_T):
                if n % 6 == 0:
                    w_hi(act, M0 + 2 + n // 6)
                if n in (4, 8):
                    combine(n // 4 - 1)
                j, s = n // NSP, n % NSP
                m_wait(act, n)
                act.activation(ga[:, j, BANK * s:BANK * s + BANK], ps[:, n % 8, :], ACT.Silu, scale=descale[M0 + j // 2]
                               ).then_inc(m_free[n % 8], 1)
            for t in range(2, NT):
                combine(t)
            for ns, n in enumerate(GATES):
                i = 2 + ns // 6
                if ns % 6 == 0 and i + 2 < NB_M:
                    w_hi(act, M0 + i + 2)
                m_wait(act, n)
                if ns >= 3:
                    gate_used(act, ns - 3)
                act.activation(sg[ns % 3], ps[:, n % 8, :], ACT.Silu if MT_GH <= n < MT_H else ACT.Sigmoid,
                               scale=descale[M0 + i]).then_inc(m_free[n % 8], 1)
            for t in range(NT):
                for half in range(2):
                    n = MT_O + 2 * t + half
                    m_wait(act, n)
                    act.activation(osq[:, BANK * half:BANK * half + BANK], ps[:, n % 8, :], ACT.Square,
                                   accum_out=ssq2[:, half:half + 1] if t % 2 == 0 else ssq2[:, 2 + half:3 + half]
                                   ).then_inc(S["o_sq"], 1)
                act.wait_ge(S["o_r"], 2 * t + 1)
                act.activation(rstd2[:, t:t + 1], rstd2[:, t:t + 1], ACT.Sqrt).then_inc(S["o_root"], 1)

        @block.vector
        def _(dve):
            steps = [0]

            def chain(op):
                op.then_inc(S["dve_steps"], 1)
                steps[0] += 1

            def settle():
                dve.wait_ge(S["dve_steps"], steps[0])

            dve.wait_ge(S["rows_T"], 1)
            dve.tensor_copy(cols[:, 0:NCOLS], ps[:, 0, 0:NCOLS]).then_inc(S["cols_ok"], 1)
            dve.tensor_copy(fcol[0:FHID, 0:4], ps[0:FHID, 0, P:P + 4]).then_inc(S["fcols_ok"], 1)
            dve.wait_ge(S["cols_ok"], 1)

            def evac(n):
                G, k = n // KD, n % KD
                dve.wait_ge(S["n_evA"], n + 1)
                dst = hn[:, :, k, SPANS[G]:SPANS[G] + BANK]
                dve.scalar_tensor_tensor(dst[:, 1], ps[:, n % 4, :], gscaled[:, k:k + 1], dst[:, 0], ALU.mult, ALU.subtract
                                         ).then_inc(S["n_evD"], 1)

            dve.tensor_reduce(gmax, cols[:, CG:CG + KD], AX.X, ALU.max, apply_absolute_value=True).then_inc(S["g_amax"], 1)
            for G in range(3):
                a, b = 4 * G, 4 * G + 4
                dve.wait_ge(S["n_sq"], b)
                dve.tensor_scalar(rstd[:, a:b], ssq[:, a:b], 1.0 / D, EPS, ALU.mult, ALU.add).then_inc(S["n_mean"], 1)
                dve.wait_ge(S["n_root"], G + 1)
                dve.reciprocal(rstd[:, a:b], rstd[:, a:b]).then_inc(S["n_rstd"], 1)
                dve.wait_ge(S["n_rstd"], G + 1)
                for t in range(a, b):
                    dve.tensor_scalar(xt[:, t, :], xt[:, t, :], rstd[:, t:t + 1], None, ALU.mult).then_inc(S["n_scaled"], 1)
            dve.wait_ge(S["g_all"], 1)
            power_of_two(dve, chain, settle, xdescale, gmax_all, 2.0 ** -15 * 2.0 ** math.ceil(math.log2(2 * math.sqrt(D))))
            chain(dve.reciprocal(xscale, xdescale))
            settle()
            dve.tensor_scalar(gscaled, cols[:, CG:CG + KD], xscale, None, ALU.mult).then_inc(S["g_scale"], 1)
            w_max(dve, 0)
            w_max(dve, 1)
            w_split(dve, chain, settle, 0)
            w_split(dve, chain, settle, 1)
            w_max(dve, 2)
            for n in range(24):
                evac(n)
            dve.wait_ge(S["b_mm"], 1)
            m3 = mask[0:HEADS, :].rearrange("p (a c) -> p a c", a=3)
            dve.tensor_tensor(m3, ps[0:HEADS, 0:3, :], m3, ALU.add).then_inc(S["b_rows"], 1)

            TWO_PI = 2.0 * math.pi
            HI = float(np.float32(6.28125))
            LO = float(np.float32(TWO_PI - HI))
            ROUND = float(1.5 * 2 ** 23)
            LIM = float(np.float32(3.1415925))

            def argument(l):
                val = xt[0:FHID, 0:2, :].rearrange("p a c -> p (a c)")[:, 0:T]
                trn = xt[0:FHID, 6:8, :].rearrange("p a c -> p (a c)")[:, 0:T]
                arg = xt[0:FHID, 3:5, :].rearrange("p a c -> p (a c)")[:, 0:T]
                dve.wait_ge(S["h_mm"], l + 1)
                chain(dve.tensor_scalar(val.rearrange("p (a c) -> p a c", a=3), ps[0:FHID, 0:3, :], fcol[0:FHID, l:l + 1],
                                        fcol[0:FHID, 3:4], ALU.add, ALU.mult))
                settle()
                chain(dve.tensor_scalar(trn, val, 1.0 / TWO_PI, ROUND, ALU.mult, ALU.add))
                settle()
                chain(dve.tensor_scalar(trn, trn, -ROUND, None, ALU.add))
                settle()
                chain(dve.scalar_tensor_tensor(val, trn, -HI, val, ALU.mult, ALU.add))
                settle()
                chain(dve.scalar_tensor_tensor(val, trn, -LO, val, ALU.mult, ALU.add))
                settle()
                dve.tensor_scalar(arg, val, LIM, -LIM, ALU.min, ALU.max).then_inc(S["h_arg"], 1)

            for c in range(3 * KD):
                u, o = ub[c % 2], ut[c % 3]
                if c % 2 == 0 and c // 2 + 2 < PREPARED:
                    w_split(dve, chain, settle, c // 2 + 2)
                if c % 2 == 0 and c // 2 + 3 < PREPARED:
                    w_max(dve, c // 2 + 3)
                dve.wait_ge(S["u_mid"], c + 1)
                dve.scalar_tensor_tensor(o, u[:, 0:UC_W], cols[:, CW + c:CW + c + 1], o, ALU.mult, ALU.add
                                         ).then_inc(S["u_tap"], 1)
                dve.wait_ge(S["u_tap"], c + 1)
                dve.scalar_tensor_tensor(o, u[:, 2:2 + UC_W], cols[:, CW + 6 * KD + c:CW + 6 * KD + c + 1], o,
                                         ALU.mult, ALU.add).then_inc(S["u_conv"], 1)
                if c in (3, 7, 11):
                    argument((c - 3) // 4)
            def scored(N):
                H, g, t, h = unit(N)
                _, kw, b0, _, edge = windows(g, t)
                l = lg[N % 2]
                c0, c1 = 0, kw
                if edge is not None:
                    c0, c1 = (edge[1], kw) if edge[0] == 0 else (0, edge[0])
                if N % STEPS == 0:
                    dve.wait_ge(ld_bias[H % 2], 16 * (H // 2 + 1 if H < 4 else 4))
                dve.wait_ge(S["a_score"], N + 1)
                if N >= 2:
                    dve.wait_ge(S["a_prob"], 2 * N - 2)
                if edge is not None:
                    chain(dve.memset(l[:, :, edge[0]:edge[1]], NEG))
                    settle()
                bias = (bwt if g < 2 else b2t)[H % 2][:, h:h + 3:2, b0 + c0:b0 + c1]
                dve.tensor_tensor(l[:, :, c0:c1], ps[:, 2 + N % 2, :].rearrange("p (x c) -> p x c", x=2)[:, :, c0:c1], bias,
                                  ALU.add).then_inc(S["a_biased"], 1)
                dve.wait_ge(S["a_biased"], N + 1)
                n = N // 2
                if h == 0 and n >= 3:
                    dve.wait_ge(ot_out[n % 3], 16 * ot_count(n - 3))
                dve.tensor_reduce(ot[n % 3][:, HW + h:HW + h + 3:2], l[:, :, 0:kw], AX.X, ALU.max, negate=True
                                  ).then_inc(S["a_max"], 1)

            def look_ahead(H, m):
                prepare(H, m, lambda b: w_split(dve, chain, settle, b), lambda b: w_max(dve, b))

            for m in range(NPT[0]):
                look_ahead(0, m)
            scored(0)
            for N in range(NSTEP):
                if N + 1 < NSTEP:
                    scored(N + 1)
                if N >= 1:
                    for H, m in MIX[N - 1]:
                        look_ahead(H, m)
            RT = math.sqrt(0.5)

            def filt(i, j):
                if j == 0:
                    dve.wait_ge(ld_dec, 16 * (i + 1))
                n = GEN0[i] + j
                h = hfb[n % 2]
                dve.wait_ge(S["f_gen"], n + 1)
                if n >= 2:
                    dve.wait_ge(S["f_ge"], n - 1)
                if j == 0:
                    chain(dve.tensor_tensor(h[:, 0:FQ], ps[:, n % 2, 0:FQ], dec[:, 0, :], ALU.mult))
                    dve.tensor_tensor(h[:, FQ:2 * FQ], ps[:, n % 2, FQ:2 * FQ], dec[:, ntile(i), :], ALU.mult
                                      ).then_inc(S["f_gen_used"], 1)
                else:
                    dve.tensor_tensor(h.rearrange("p (e c) -> p e c", e=2),
                                      ps[:, n % 2, :].rearrange("p (e c) -> p e c", e=2),
                                      dec[:, j:j + 1, :].to_broadcast([P, 2, FQ]), ALU.mult).then_inc(S["f_gen_used"], 1)

            def butterfly(i, x, src):
                m = 3 * i + x
                if m >= 2:
                    if x == 0:
                        u = uk[i - 1] + npair(i - 1)
                    elif x == 1:
                        u = uz[i - 1] + npair(i - 1) - 1
                    else:
                        u = uk[i] + npair(i) // 2
                    wait_ready(dve, u)
                a = fa[m % 2]
                nc_ = DFTS[ITEMS[i][0]]["nc"]
                w = nc_ * FQ
                f = src.rearrange("p t c -> p (t c)")
                e = e01.rearrange("p a c -> p (a c)")

                def A(c):
                    return a[:, c, 0:w]

                settle()
                if m >= 1:
                    dve.wait_ge(S["f_bf"], m)
                chain(dve.tensor_tensor(e[:, 0:2 * w], f[:, 0:2 * w], f[:, 2 * w:4 * w], ALU.add))
                chain(dve.tensor_tensor(a[:, A2R:A2N + 1, 0:w], f[:, 0:2 * w].rearrange("p (a c) -> p a c", a=2),
                                        f[:, 2 * w:4 * w].rearrange("p (a c) -> p a c", a=2), ALU.subtract))
                settle()
                e0, e1 = e[:, 0:w], e[:, w:2 * w]
                chain(dve.tensor_tensor(A(A0), e0, e1, ALU.add))
                chain(dve.tensor_tensor(A(A4), e0, e1, ALU.subtract))
                chain(dve.scalar_tensor_tensor(A(A1R), A(A2N), RT, f[:, 0:w], ALU.mult, ALU.add))
                chain(dve.scalar_tensor_tensor(A(A3R), A(A2N), -RT, f[:, 0:w], ALU.mult, ALU.add))
                chain(dve.scalar_tensor_tensor(A(A1N), e1, RT, f[:, 2 * w:3 * w], ALU.mult, ALU.add))
                dve.scalar_tensor_tensor(A(A3I), e1, -RT, f[:, 2 * w:3 * w], ALU.mult, ALU.add).then_inc(S["f_bf"], 1)

            def filter_butterflies(i):
                dve.wait_ge(S["f_ge"], GEN0[i + 1])
                butterfly(i, 0, tge)
                butterfly(i, 1, tgo)

            def product(i):
                settle()
                for u in range(uk[i] + npair(i) - 3, uk[i] + npair(i) + 1):
                    wait_free(dve, u)
                for p in range(npair(i)):
                    u = uz[i] + p
                    n = PR0[i] + p
                    a = pq[n % 2]
                    wait_ready(dve, u)
                    if n >= 2:
                        dve.wait_ge(S["f_y"], n - 1)
                    re, im = ps[:, fbank(u), 0:FQ], ps[:, fbank(u), FQ:2 * FQ]
                    k = kf[:, p, :].rearrange("p (a c) -> p a c", a=2)
                    chain(dve.tensor_tensor(a[:, 0:2 * FQ].rearrange("p (a c) -> p a c", a=2),
                                            re.unsqueeze(1).to_broadcast([P, 2, FQ]), k, ALU.mult))
                    if p == 0:
                        chain(dve.tensor_tensor(a[:, 2 * FQ:3 * FQ], im, kfl, ALU.mult))
                        dve.tensor_tensor(a[:, 3 * FQ:4 * FQ], im, kf[:, 0, FQ:2 * FQ], ALU.mult
                                          ).then_inc(bank_free[fbank(u)], 1)
                    else:
                        dve.tensor_tensor(a[:, 2 * FQ:4 * FQ].rearrange("p (a c) -> p a c", a=2),
                                          im.unsqueeze(1).to_broadcast([P, 2, FQ]), k, ALU.mult
                                          ).then_inc(bank_free[fbank(u)], 1)
                    if i + 1 < NI and p < ntile(i + 1):
                        filt(i + 1, p)

            def recombine(i, ct):
                s, q, o = ITEMS[i]
                L, w = LENS[s], DFTS[s]["w"]
                m = 2 * i + ct
                b0, b1 = iv0[m % 2], iv1[m % 2]
                u0, u1, u3, u2 = (ui[i] + 4 * ct + x for x in range(4))
                U, V, E, X = iv_u[:, 0:2 * w], iv_v[:, 0:2 * w], iv_a[:, 0:2 * w], iv_b[:, 0:2 * w]
                G = e01.rearrange("p a c -> p (a c)")[:, 0:2 * w]
                settle()
                dve.wait_ge(S["f_y"], PR0[i + 1])
                if m >= 1:
                    dve.wait_ge(S["f_post"], m)
                dve.wait_ge(S["f_bf"], 3 * i + (5 if i + 1 < NI else 3))
                wait_free(dve, u0)
                chain(dve.tensor_tensor(E[:, 0:w], b0[:, 0:w], b0[:, w:2 * w], ALU.add))
                chain(dve.tensor_tensor(E[:, w:2 * w], b0[:, 0:w], b0[:, w:2 * w], ALU.subtract))
                wait_free(dve, u1)
                wait_ready(dve, u3)
                chain(dve.tensor_tensor(U, ps[:, fbank(u3), 0:2 * w], b1[:, 0:2 * w], ALU.add))
                dve.scalar_tensor_tensor(V, ps[:, fbank(u3), 0:2 * w], -1.0, b1[:, 0:2 * w], ALU.mult, ALU.add
                                         ).then_inc(bank_free[fbank(u3)], 1)
                settle()
                wait_ready(dve, u2)
                chain(dve.tensor_tensor(X, ps[:, fbank(u2), 0:2 * w], E, ALU.add))
                settle()
                dve.scalar_tensor_tensor(E, ps[:, fbank(u2), 0:2 * w], -1.0, E, ALU.mult, ALU.add
                                         ).then_inc(bank_free[fbank(u2)], 1)
                wait_free(dve, u3)
                chain(dve.tensor_tensor(G[:, 0:w], V[:, 0:w], U[:, w:2 * w], ALU.subtract))
                chain(dve.tensor_tensor(G[:, w:2 * w], V[:, 0:w], U[:, w:2 * w], ALU.add))
                wait_free(dve, u2)
                settle()
                chain(dve.tensor_tensor(yo[:, 0:w], X[:, 0:w], U[:, 0:w], ALU.add))
                chain(dve.tensor_tensor(yo[:, 2 * w:3 * w], E[:, 0:w], V[:, w:2 * w], ALU.subtract))
                chain(dve.scalar_tensor_tensor(yo[:, w:2 * w], G[:, 0:w], RT, E[:, w:2 * w], ALU.mult, ALU.add))
                chain(dve.scalar_tensor_tensor(yo[:, 3 * w:4 * w], G[:, w:2 * w], -RT, X[:, w:2 * w], ALU.mult, ALU.add))
                settle()
                z = zc[q % 2][:, ct, 0:L]
                sk = CS + KD * o + 2 * q + ct
                chain(dve.scalar_tensor_tensor(yo[:, 0:L], z, cols[:, sk:sk + 1], yo[:, 0:L], ALU.mult, ALU.add))
                settle()
                dve.wait_ge(S["ld_hx"], 16 * (i + 1))
                dve.tensor_tensor(z, yo[:, 0:L], hx[:, ct, 0:L], ALU.mult).then_inc(S["f_post"], 1)

            for j in range(ntile(0)):
                filt(0, j)
            filter_butterflies(0)
            dve.wait_ge(S["f_tz"], TR0[1])
            butterfly(0, 2, tz)
            for i in range(NI):
                product(i)
                if i + 1 < NI:
                    filter_butterflies(i + 1)
                recombine(i, 0)
                recombine(i, 1)
                if i + 1 < NI:
                    dve.wait_ge(S["f_tz"], TR0[i + 2])
                    butterfly(i + 1, 2, tz)
            M0 = NB_U + NB_A
            w_max(dve, M0)
            w_max(dve, M0 + 1)
            w_split(dve, chain, settle, M0)
            w_split(dve, chain, settle, M0 + 1)
            w_max(dve, M0 + 2)
            w_split(dve, chain, settle, M0 + 2)
            w_max(dve, M0 + 3)
            dve.wait_ge(S["ld_hm"], 16)

            def gate(t):
                n = MT_T + t
                if t == 0:
                    m_allfree(dve, MT_T)
                m_wait(dve, n)
                c = slice(P * t, P * t + P)
                dve.tensor_tensor(at[:, :, c], ps[:, n % 8, :].rearrange("p (j c) -> p j c", j=4), ga[:, :, c], ALU.mult
                                  ).then_inc(m_free[n % 8], 1)

            for t in range(NT):
                o, w = ogt[t % 2], wts[t % 2]
                acc, tmp = cmb[t % 2][:, 0, :], cmb[t % 2][:, 1, :]
                nm, den = o[:, :, :, HW:HW + HH], o[:, :, :, HW + HH:OW]
                low, total = (w[:, c:c + 8].rearrange("p (a h) -> p a h", a=2) for c in (0, 56))
                e, ed = (w[:, c:c + 24].rearrange("p (g a h) -> p g a h", g=3, a=2) for c in (8, 32))
                dve.wait_ge(ld_og[t % 2], 16 * (t // 2 + 1))
                chain(dve.tensor_tensor(low, nm[:, 0], nm[:, 1], ALU.min))
                settle()
                chain(dve.tensor_tensor(low, low, nm[:, 2], ALU.min))
                settle()
                dve.tensor_tensor(e, low.unsqueeze(1).to_broadcast([P, 3, 2, HH]), nm, ALU.subtract).then_inc(S["g_sc"], 1)
                dve.wait_ge(S["g_exp"], t + 1)
                chain(dve.tensor_tensor(ed, e, den, ALU.mult))
                settle()
                chain(dve.tensor_tensor(total, ed[:, 0], ed[:, 1], ALU.add))
                settle()
                chain(dve.tensor_tensor(total, total, ed[:, 2], ALU.add))
                settle()
                chain(dve.reciprocal(total, total))
                settle()
                dve.tensor_tensor(e, e, total.unsqueeze(1).to_broadcast([P, 3, 2, HH]), ALU.mult).then_inc(S["g_sc"], 1)
                dve.wait_ge(S["g_sc"], 2 * t + 2)
                if t >= 2:
                    m_wait(dve, MT_T + t - 2)

                def weighted(dst, g):
                    chain(dve.tensor_tensor(dst.rearrange("p (a h c) -> p a h c", a=2, h=HH),
                                            o[:, g, :, 0:HW].rearrange("p a (h c) -> p a h c", h=HH),
                                            e[:, g].unsqueeze(3).to_broadcast([P, 2, HH, HD]), ALU.mult))

                weighted(acc, 0)
                weighted(tmp, 1)
                settle()
                chain(dve.tensor_tensor(acc, acc, tmp, ALU.add))
                settle()
                weighted(tmp, 2)
                settle()
                dve.tensor_tensor(acc, acc, tmp, ALU.add).then_inc(S["g_cmb"], 1)
                if t == 0:
                    w_split(dve, chain, settle, M0 + 3)
                    w_max(dve, M0 + 4)
                if t >= 1:
                    gate(t - 1)
            gate(NT - 1)

            def m_prepare(i):
                if i + 2 < NB_M:
                    w_split(dve, chain, settle, M0 + i + 2)
                if i + 3 < NB_M:
                    w_max(dve, M0 + i + 3)

            for ns, n in enumerate(GATES):
                x = ns % (KD * NSP)
                d, s = x // NSP, x % NSP
                c = slice(BANK * s, BANK * s + BANK)
                if x % 6 == 0:
                    m_prepare(2 + ns // 6)
                m_waitfree(dve, n)
                if MT_GH <= n < MT_H:
                    dve.wait_ge(ld_hy[d], 16)
                    dve.tensor_tensor(hg[:, d, c], hg[:, d, c], sg[ns % 3], ALU.mult).then_inc(S["m_mul"], 1)
                    continue
                b = n + NSP
                m_wait(dve, b)
                if n < MT_GH:
                    if x == 0:
                        dve.wait_ge(S["g_cmb"], NT)
                    dve.tensor_tensor(mt[:, d, c], ps[:, b % 8, :], sg[ns % 3], ALU.mult).then_inc(m_free[b % 8], 1)
                else:
                    if x >= 1:
                        dve.wait_ge(S["m_acc"], x)
                    dve.tensor_tensor(gated, ps[:, b % 8, :], sg[ns % 3], ALU.mult).then_inc(m_free[b % 8], 1)
                    m_waitfree(dve, b)
                    dve.tensor_tensor(mt[:, d, c], mt[:, d, c], gated, ALU.add).then_inc(S["m_acc"], 1)
            dve.wait_ge(S["ld_gain"], 16)
            for t in range(NT):
                a = 2 * (t % 2)
                r = rstd2[:, t:t + 1]
                dve.wait_ge(S["o_sq"], 2 * t + 2)
                chain(dve.tensor_tensor(r, ssq2[:, a:a + 1], ssq2[:, a + 1:a + 2], ALU.add))
                settle()
                dve.tensor_scalar(r, r, 1.0 / D, EPS, ALU.mult, ALU.add).then_inc(S["o_r"], 1)
                dve.wait_ge(S["o_root"], t + 1)
                dve.reciprocal(r, r).then_inc(S["o_r"], 1)
                dve.wait_ge(S["o_r"], 2 * t + 2)
                if t >= 2:
                    dve.wait_ge(y_out[t % 2], 16 * (t // 2))
                y = yout[t % 2]
                for half in range(2):
                    n = MT_O + 2 * t + half
                    c = slice(BANK * half, BANK * half + BANK)
                    dve.scalar_tensor_tensor(y[:, c], ps[:, n % 8, :], r, gpost[:, c], ALU.mult, ALU.mult
                                             ).then_inc(m_free[n % 8], 1)
                    m_waitfree(dve, n)
                dve.wait_ge(ld_xr[t % 2], 16 * (t // 2 + 1))
                dve.tensor_tensor(y, y, xres[t % 2], ALU.add).then_inc(S["o_y"], 1)


INPUTS = ("x_prompt", "x_sample", "rel_bias", "pre_norm_g", "post_norm_g", "w_in", "conv_w", "conv_b", "filt_w1", "filt_b1",
          "filt_w2", "filt_b2", "filt_w3", "filt_b3", "filt_w4", "filt_freq", "hyena_skip", "w_branch_a", "w_branch_h", "w_out")


def kernel(**inputs):
    import concourse.bacc as bacc
    from concourse.bass_utils import run_bass_kernel_spmd

    nc = bacc.Bacc("TRN2", target_bir_lowering=False, num_devices=1)
    arrays, ins, cst = {}, {}, {}
    for name in INPUTS:
        arrays["in_" + name] = np.ascontiguousarray(inputs[name])
        ins[name] = nc.dram_tensor("in_" + name, arrays["in_" + name].shape, F32, kind="ExternalInput").ap()
    for name, a in constants().items():
        arrays["c_" + name] = a
        cst[name] = nc.dram_tensor("c_" + name, a.shape, F32, kind="ExternalInput").ap()
    y_p = nc.dram_tensor("y_prompt", (1, SP, D), F32, kind="ExternalOutput").ap()
    y_s = nc.dram_tensor("y_sample", (1, SS, D), F32, kind="ExternalOutput").ap()
    build(nc, ins, cst, y_p, y_s)
    r = run_bass_kernel_spmd(nc, [arrays], core_ids=[0])
    return r.results[0]["y_prompt"], r.results[0]["y_sample"]
```

```python
import math
from contextlib import ExitStack

import numpy as np

import concourse.bass as bass
import concourse.mybir as mybir

ALU = mybir.AluOpType
ACT = mybir.ActivationFunctionType
AX = mybir.AxisListType
F32, FP16, I32 = mybir.dt.float32, mybir.dt.float16, mybir.dt.int32

P = 128
D = 1024
KD = D // P
SP, SS = 1024, 512
T = SP + SS
NT = T // P
BANK = 512
HD = 64
HEADS = 8
GROUPS = ((128, 1), (512, 4), (2048, 16))
QKV = len(GROUPS) * HEADS * HD
AW = HEADS * HD
HW = AW // 2
HH = HEADS // 2
WC = 256
BLK = 64
NEG = -1e30
NBUCK = 32
MAXDIST = 1024
FEMB, FHID = 33, 64
EPS = 1e-6
OFF_GA = 3 * QKV
OFF_U = OFF_GA + AW
OFF_GH = OFF_U + 3 * D
OFF_MG = OFF_GH + D
INW = OFF_MG + 2 * D

PADC = BLK
COL_P = PADC
COL_S = PADC + SP + PADC
HC = COL_S + SS + PADC
SPANS = (COL_P, COL_P + BANK, COL_S)

FQ = 256
NQ = D // FQ
RAD = 8

BW = 3 * P
BROW = 2 * 2 * P - 1
OW = HW + 2 * HH


def bucket(rel):
    half = NBUCK // 2
    exact = half // 2
    n = np.abs(rel)
    nf = np.maximum(n, 1).astype(np.float32)
    large = exact + (np.log(nf / np.float32(exact)) / np.float32(math.log(MAXDIST / exact)) * (half - exact)).astype(np.int32)
    return np.where(rel > 0, half, 0) + np.where(n < exact, n, np.minimum(large, half - 1))


def stride(g, seq):
    return min(GROUPS[g][1], (SP, SS)[seq] // P)


def bias_tables():
    hot = np.zeros((NBUCK, 3 * BANK), np.float32)
    mask = np.zeros((HEADS, 3 * BANK), np.float32)
    for g, seq, col, reach in ((0, 0, 0, BROW // 2), (1, 0, 0, BROW // 2), (2, 0, 0, P - 1), (2, 1, 2 * P - 1, P - 1)):
        dilation, r = GROUPS[g][1], stride(g, seq)
        for i, apart in enumerate(range(-reach, reach + 1)):
            if apart * r % dilation == 0 and abs(apart * r) <= BLK * dilation:
                hot[bucket(np.array(apart * r)), g * BANK + col + i] = 1.0
            else:
                mask[:, g * BANK + col + i] = NEG
    return hot, mask


def filter_features(length):
    f = np.float32
    t = np.linspace(0.0, 1.0, length, dtype=f)[:, None]
    ang = f(2.0 * math.pi / length) * np.arange(length, dtype=f)[:, None]
    bands = np.linspace(1e-4, (FEMB - 1) // 2 - 1, (FEMB - 1) // 2, dtype=f)[None]
    return np.concatenate([t, np.cos(ang * bands), -np.sin(ang * bands)], axis=-1).astype(f).T


def decay_table(length):
    t = np.linspace(0.0, 1.0, length, dtype=np.float32)[:, None].astype(np.float64)
    deltas = np.abs(np.linspace(math.log(1e-2) / 1.5, math.log(1e-2) / 0.3, D, dtype=np.float32)).astype(np.float64)
    dec = np.exp(-t * deltas[None])
    first = dec[0:P].copy()
    first[0] = 0.0
    return np.concatenate([dec, first]).astype(np.float32)


A0, A4, A1R, A1N, A2R, A2N, A3R, A3I = range(8)


def dft(L):
    n = 2 * L
    w = n // RAD
    nc = w // P
    n2 = np.arange(w)
    fwd, inv, pairs = [], [], []
    units = [[], [], [], []]

    def add(m):
        fwd.append(m)
        return len(fwd) - 1

    def addi(m):
        inv.append(m)
        return sum(x.shape[1] for x in inv[:-1])

    def ang(c, ks):
        return 2 * np.pi * (np.outer(n2[c * P:(c + 1) * P], ks) % n) / n

    def iang(ks):
        return 2 * np.pi * (np.outer(ks, n2) % n) / n

    def weight(ks):
        return np.where((ks == 0) | (ks == L), 1.0, 2.0)[:, None] / n

    def cat(a, b):
        return np.concatenate([a, b], axis=1)

    nyq = np.cos(np.pi * (n2 % 2))
    if nc == 2:
        k0, k4 = 8 * np.arange(P), 4 + 8 * np.arange(P)
        re, im, imk, rek = [], [], [], []
        for c in range(nc):
            co, si = np.cos(ang(c, k0)), -np.sin(ang(c, k0))
            sz, cy = si.copy(), co.copy()
            sz[:, 0] = cy[:, 0] = nyq[c * P:(c + 1) * P]
            re.append((A0, c, add(co)))
            im.append((A0, c, add(sz)))
            imk.append((A0, c, add(si)))
            rek.append((A0, c, add(cy)))
        pairs.append((re, im, imk, rek))
        re = [(A4, c, add(np.cos(ang(c, k4)))) for c in range(nc)]
        im = [(A4, c, add(-np.sin(ang(c, k4)))) for c in range(nc)]
        pairs.append((re, im, im, re))
        r, s = np.cos(iang(k0)) * weight(k0), -np.sin(iang(k0)) * weight(k0)
        s[0] = nyq / n
        units[0] += [(0, 0, addi(r), 0, w), (0, 1, addi(s), 0, w)]
        units[0] += [(1, 0, addi(np.cos(iang(k4)) * weight(k4)), w, w), (1, 1, addi(-np.sin(iang(k4)) * weight(k4)), w, w)]
    else:
        h = P // 2
        k0, k4 = 8 * np.arange(h), 4 + 8 * np.arange(h)
        z, zi = np.zeros((P, h)), np.zeros((h, w))
        co, si = np.cos(ang(0, k0)), -np.sin(ang(0, k0))
        sz, cy = si.copy(), co.copy()
        sz[:, 0] = cy[:, 0] = nyq
        c4, s4 = (A4, 0, add(cat(z, np.cos(ang(0, k4))))), (A4, 0, add(cat(z, -np.sin(ang(0, k4)))))
        pairs.append(([(A0, 0, add(cat(co, z))), c4], [(A0, 0, add(cat(sz, z))), s4],
                      [(A0, 0, add(cat(si, z))), s4], [(A0, 0, add(cat(cy, z))), c4]))
        s0 = -np.sin(iang(k0)) * weight(k0)
        s0[0] = nyq / n
        r = np.concatenate([cat(np.cos(iang(k0)) * weight(k0), zi), cat(zi, np.cos(iang(k4)) * weight(k4))])
        s = np.concatenate([cat(s0, zi), cat(zi, -np.sin(iang(k4)) * weight(k4))])
        units[0] += [(0, 0, addi(r), 0, 2 * w), (0, 1, addi(s), 0, 2 * w)]
    for k1, (ar, ai, negated) in enumerate(((A1R, A1N, True), (A2R, A2N, True), (A3R, A3I, False)), 1):
        for m in range(nc):
            ks = k1 + 8 * (np.arange(P) + m * P)
            re, im = [], []
            for c in range(nc):
                co, si = np.cos(ang(c, ks)), np.sin(ang(c, ks))
                ico, ins = add(co), add(-si)
                if negated:
                    re += [(ar, c, ico), (ai, c, ins)]
                    im += [(ar, c, ins), (ai, c, add(-co))]
                else:
                    re += [(ar, c, ico), (ai, c, add(si))]
                    im += [(ar, c, ins), (ai, c, ico)]
            pairs.append((re, im, im, re))
            co, si = np.cos(iang(ks)) * weight(ks), np.sin(iang(ks)) * weight(ks)
            col = addi(np.concatenate([-si, co, si], axis=1))
            units[k1] += [(len(pairs) - 1, 0, col + w, 0, 2 * w), (len(pairs) - 1, 1, col, 0, 2 * w)]
    return {"fwd": np.stack(fwd, axis=1).astype(np.float32).reshape(P, -1),
            "inv": np.concatenate(inv, axis=1).astype(np.float32), "pairs": pairs, "units": units, "w": w, "nc": nc}


DFTS = (dft(SP), dft(SS))
LENS = (SP, SS)
TOK0 = (0, SP)
UC_W = SP + 1 + SS
UC0 = (0, SP + 1)


def constants():
    hot, mask = bias_tables()
    c = {"hot": hot, "mask": mask,
         "feat": np.concatenate([filter_features(SP), filter_features(SS)], axis=1),
         "dec0": decay_table(SP), "dec1": decay_table(SS)}
    for s in range(2):
        c[f"fwd{s}"] = DFTS[s]["fwd"]
        c[f"inv{s}"] = DFTS[s]["inv"]
    c["ident"] = np.eye(P, dtype=np.float32)
    return {k: np.ascontiguousarray(v) for k, v in c.items()}


def windows(g, t):
    if g == 0:
        u = t if t < SP // P else t - SP // P
        last = u == (SP // P if t < SP // P else SS // P) - 1
        k0 = P * t if t < SP // P else COL_S - PADC + P * u
        v0 = t if t < SP // P else SP // P + 1 + u
        return k0, 2 * P, P // 2, [v0, v0 + 1], (0, BLK) if u == 0 else (3 * BLK, 4 * BLK) if last else None
    if g == 1:
        if t < SP // P:
            r, half = t // 2, t % 2
            return 2 * P * r, 2 * P, P - P * half, [2 * r, 2 * r + 1], None
        return P * t, P, P, [t], None
    return P * t, P, (0 if t < SP // P else P), [t], None


def value_tiles(g):
    if g == 0:
        return [(P * m, 1) for m in range(SP // P + 1)] + [(COL_S - PADC + P * m, 1) for m in range(SS // P + 1)]
    out = []
    for seq, c0, n in ((0, COL_P, SP), (1, COL_S, SS)):
        r = stride(g, seq)
        for m in range(n // P):
            out.append((c0 + m * P // (n // r) + r * (m * P % (n // r)), r))
    return out


def build(nc, ins, cst, y_p, y_s):
    dram = {}
    for name, shape in (("uc", [3 * KD, P, UC_W]), ("og", [3, T, 2, OW]), ("hy", [KD, P, T]),
                        ("hn", [P, KD * HC]), ("brow", [HEADS, P, 3 * BANK])):
        dram[name] = nc.dram_tensor("s_" + name, shape, F32, kind="Internal")
    uc_d, og_d, hy_d, hn_d, brow_d = (dram[n].ap() for n in ("uc", "og", "hy", "hn", "brow"))
    w_in, w_a, w_h, w_o = ins["w_in"][0], ins["w_branch_a"][0], ins["w_branch_h"][0], ins["w_out"][0]

    with ExitStack() as ctx:
        def sem(name):
            return ctx.enter_context(nc.semaphore(name))

        ARENA = 53200
        mem = ctx.enter_context(nc.sbuf_tensor("mem", [P, ARENA], F32))
        ps = ctx.enter_context(nc.psum_tensor("ps", [P, 8, BANK], F32))

        top = [0]

        def part(n, at=None):
            if at is not None:
                top[0] = at
            a = top[0]
            top[0] += n
            assert top[0] <= ARENA, (top[0], ARENA)
            return mem[:, a:a + n]

        def grid(n, m, at=None):
            return part(n * m, at).rearrange("p (n m) -> p n m", n=n)

        ident = part(P)
        cols = part(P)
        fcol = part(8)
        small = part(72)
        wsc = part(72)
        BASE = top[0]
        CW, CB, CG, CS = 0, 9 * KD, 12 * KD, 13 * KD
        NCOLS = 15 * KD
        ssq, rstd = small[:, 0:NT], small[:, NT:2 * NT]
        ssq2, rstd2 = small[:, 2 * NT:3 * NT], small[:, 3 * NT:4 * NT]
        H3_AT = ARENA - T
        h3 = part(T, H3_AT)

        def halves(a, n, m):
            return a.bitcast(FP16).rearrange("p (h n m) -> p h n m", h=2, n=n)

        hn_words = part(KD * HC, BASE)
        hn = halves(hn_words, KD, HC)
        raw = [grid(KD, WC) for _ in range(2)]
        ring = [halves(part(KD * WC), KD, WC) for _ in range(3)]
        EARLY = top[0]
        NB_U, NB_A, NB_M = 3 * D // WC, 6 * 3, 14 + 4
        NB = NB_U + NB_A + NB_M
        descale = [wsc[:, b:b + 1] for b in range(NB)]
        amax, amax_all, wexp, wscale = ([wsc[:, NB + 3 * x + i:NB + 3 * x + i + 1] for i in range(3)] for x in range(4))
        XC = NB + 12
        gscaled = wsc[:, XC:XC + KD]
        gmax, gmax_all, xscale, xdescale = (wsc[:, XC + KD + i:XC + KD + i + 1] for i in range(4))
        assert XC + KD + 4 <= 72
        xt = grid(NT, D)
        rows = part(P)
        frows = part(FHID)
        ub = [part(UC_W + 2) for _ in range(2)]
        ut = [part(UC_W) for _ in range(3)]
        junk = [ut[i][:, 0:D] for i in range(2)]
        feat = part(T)
        fw = part(3 * FHID)
        hid = part(T)
        hot = part(3 * BANK)
        mask = part(3 * BANK)
        assert top[0] <= H3_AT

        qt = [grid(2, T, EARLY), grid(2, T)]
        kt = [grid(2, HC) for _ in range(2)]
        vt = [grid(14, HW) for _ in range(2)]
        bwt = [grid(HH, BW) for _ in range(2)]
        b2t = [b.rearrange("p h c -> p (h c)")[:, 0:HH * 2 * P].rearrange("p (h c) -> p h c", h=HH) for b in bwt]
        lg = [grid(2, 2 * P) for _ in range(2)]
        pr = [grid(2, 2 * P) for _ in range(2)]
        pt = [grid(2, 2 * P) for _ in range(2)]
        ot = [part(OW) for _ in range(3)]
        relb = small[:, 4 * NT:4 * NT + 3 * HEADS]
        assert top[0] <= H3_AT

        w4 = [part(2 * FQ, BASE), part(2 * FQ)]
        ftab = part(DFTS[0]["fwd"].shape[1])
        itab = part(DFTS[0]["inv"].shape[1])
        dec = grid(SP // P + 1, FQ)
        tge, tgo, tz = (grid(SP // P, FQ) for _ in range(3))
        fa = [grid(8, 2 * FQ) for _ in range(2)]
        kf = grid(8, 2 * FQ)
        kfl = part(FQ)
        yf = grid(8, 2 * FQ)
        hfb = [part(2 * FQ) for _ in range(2)]
        pq = [part(4 * FQ) for _ in range(2)]
        iv_u, iv_v, iv_a, iv_b = pq[0][:, 0:BANK], pq[0][:, BANK:], pq[1][:, 0:BANK], pq[1][:, BANK:]
        zc = [grid(2, SP) for _ in range(2)]
        hx = grid(2, SP)
        yo = part(SP)
        e01 = grid(2, 2 * FQ)
        iv0 = [part(BANK) for _ in range(2)]
        iv1 = [part(BANK) for _ in range(2)]
        assert top[0] <= H3_AT, (top[0], H3_AT)

        mt = grid(KD, T, BASE + KD * HC)
        hg = grid(KD, T)
        ga, at = hg[:, 0:4, :], hg[:, 4:8, :]
        mraw = [grid(KD, WC) for _ in range(2)]
        mring = [halves(part(KD * WC), KD, WC) for _ in range(3)]
        wb_words = part(KD * WC)
        wb = wb_words.rearrange("p (k c) -> p k c", k=KD)
        wb_split = halves(wb_words, KD, WC)
        sg = [part(BANK) for _ in range(3)]
        gated = part(BANK)
        ogt = [mem[:, BASE + KD * HC + i * 6 * OW:BASE + KD * HC + (i + 1) * 6 * OW].rearrange(
            "p (g a c) -> p g a c", g=3, a=2) for i in range(2)]
        GSC = BASE + KD * HC + 12 * OW
        wts = [mem[:, GSC + 64 * i:GSC + 64 * i + 64] for i in range(2)]
        cmb = [mem[:, GSC + 128 + 2 * AW * i:GSC + 128 + 2 * AW * (i + 1)].rearrange("p (a c) -> p a c", a=2) for i in range(2)]
        m16 = halves(mem[:, BASE:BASE + KD * T], KD, T)
        OUT = BASE + KD * HC + KD * T
        gpost = mem[:, OUT:OUT + D]
        xres = [mem[:, OUT + D * (1 + i):OUT + D * (2 + i)] for i in range(2)]
        yout = [mem[:, OUT + D * (3 + i):OUT + D * (4 + i)] for i in range(2)]
        osq = mem[:, OUT + 5 * D:OUT + 6 * D]
        mt_max = small[:, 4 * NT:4 * NT + KD * len(SPANS)]
        m_max, m_all_max, m_descale, m_scale = (wsc[:, i:i + 1] for i in range(4))
        o_descale, o_scale = wsc[:, 4:8], wsc[:, 8:12]

        names = """ld_small ld_tabs ld_gain dve_steps ld_w0 ld_w1 w_amax w_all w_scale w_hi w_lo g_amax g_all
            g_scale ld_wb rows_T cols_ok fcols_ok pads_ok n_sq n_mean n_root n_rstd n_scaled n_T n_evA n_evD
            hn_saved u_ready u_evac u_mid u_tap u_conv h_mm h_arg h_sin b_mm b_rows b_stored a_ready a_evac
            a_score a_biased a_max a_prob a_pT a_ptcopied a_ov a_oevac f_gen f_gen_used f_ge f_bf f_y f_post
            f_zT f_tz ld_hx ld_ftab ld_itab g_cmb g_sc g_exp m_mul m_acc o_sq o_root o_r o_y""".split()
        S = {n: sem(n) for n in names}
        ld_x = [sem(f"ld_x{i}") for i in range(3)]
        uc_out = [sem(f"uc_out{i}") for i in range(3)]
        ot_out = [sem(f"ot_out{i}") for i in range(3)]
        ld_w4 = [sem(f"ld_w4{i}") for i in range(2)]
        ld_dec = sem("ld_dec")
        ld_zc = [sem(f"ld_zc{i}") for i in range(2)]
        hy_out = [sem(f"hy_out{i}") for i in range(2)]
        bank_ready = [sem(f"bank_ready{i}") for i in range(8)]
        bank_free = [sem(f"bank_free{i}") for i in range(8)]
        ld_hm = [sem(f"ld_hm{s}") for s in range(len(SPANS))]
        ld_og = [sem(f"ld_og{i}") for i in range(2)]
        ld_hy = [sem(f"ld_hy{i}") for i in range(8)]
        ld_xr = [sem(f"ld_xr{i}") for i in range(2)]
        y_out = [sem(f"y_out{i}") for i in range(2)]

        NSP = len(SPANS)
        U_TILES = 3 * KD * NSP

        NPT = [2 * 2 * NSP + len(value_tiles(H // 2)) // 2 for H in range(6)]
        PT0 = [sum(NPT[:H]) for H in range(7)]
        STEPS = NT * 2
        NSTEP = 6 * STEPS
        MIX = [[(H, m) for m in range(n * NPT[H] // STEPS, (n + 1) * NPT[H] // STEPS)] if H < 6 else []
               for H in range(1, 7) for n in range(STEPS)]
        PARTS = [[(H, u // KD, u % KD) for u in range(n * KD * NPT[H] // STEPS, (n + 1) * KD * NPT[H] // STEPS)] if H < 6 else []
                 for H in range(1, 7) for n in range(STEPS)]

        def unit(N):
            H, n = N // STEPS, N % STEPS
            return H, H // 2, n // 2, n % 2

        def ptile(H, m):
            kind = min(m // (2 * NSP), 2)
            return kind, m - 2 * NSP * kind, NB_U + 3 * H + kind

        ITEMS = [(s, q, o) for s in range(2) for q0 in range(0, NQ, 2) for o in range(2) for q in (q0, q0 + 1)]
        NI = len(ITEMS)

        def npair(i):
            return len(DFTS[ITEMS[i][0]]["pairs"])

        def ntile(i):
            return LENS[ITEMS[i][0]] // P

        def zc_uses(i):
            return len([x for x in ITEMS[:i + 1] if x[1] % 2 == ITEMS[i][1] % 2 and x[2] == ITEMS[i][2]])

        uk, uz, ui = [0] * NI, [0] * NI, [0] * NI
        n = 0
        uk[0], n = n, n + npair(0) + 1
        for i in range(NI):
            uz[i], n = n, n + npair(i)
            ui[i], n = n, n + 8
            if i + 1 < NI:
                uk[i + 1], n = n, n + npair(i + 1) + 1
        f_units = n
        GEN0 = [sum(ntile(x) for x in range(i)) for i in range(NI + 1)]
        TR0 = [g // 2 for g in GEN0]
        PR0 = [sum(npair(x) for x in range(i)) for i in range(NI + 1)]
        ORDER = (0, 1, 3, 2)

        def fbank(u):
            return 2 + u % 4

        def wait_ready(eng, u):
            eng.wait_ge(bank_ready[fbank(u)], u // 4 + 1)

        def wait_free(eng, u):
            eng.wait_ge(bank_free[fbank(u)], u // 4 + 1)

        MB = [OFF_GA + WC * i for i in range(2)] + [OFF_MG + WC * i for i in range(4)] + [OFF_GH + WC * i for i in range(4)]
        MB += [OFF_MG + D + WC * i for i in range(4)]
        assert len(MB) + 4 == NB_M
        others = [("ga", j, s) for s in range(1, NSP) for j in range(4)] + [("ma", 0, s) for s in range(NSP)]
        MSEQ = [("ga", j, 0) for j in range(4)]
        for x in range(NT):
            MSEQ += [("T", x, 0)] + others[x:x + 1]
        POS = {e: n for n, e in enumerate(MSEQ)}
        MT_A = 4 * NSP + NT
        MT_GH = MT_A + 2 * KD * NSP
        MT_H = MT_GH + KD * NSP
        MT_O = MT_H + 2 * KD * NSP
        MT_END = MT_O + 2 * NT
        M_DONE = [POS["ga", 2 * i + 1, NSP - 1] + 1 for i in range(2)] + [MT_A + 4 * NSP * i + 3 * NSP for i in range(4)]
        M_DONE += [MT_GH + 2 * NSP * (i + 1) for i in range(4)] + [MT_H + 4 * NSP * i + 3 * NSP for i in range(4)]

        def m_wait(eng, n):
            eng.wait_ge(m_done[n % 8], n // 8 + 1)

        def m_waitfree(eng, n):
            eng.wait_ge(m_free[n % 8], n // 8 + 1)

        def m_all(eng, n):
            for b in range(8):
                k = (n - b + 7) // 8
                if k > 0:
                    eng.wait_ge(m_done[b], k)

        def m_allfree(eng, n):
            for b in range(8):
                k = (n - b + 7) // 8
                if k > 0:
                    eng.wait_ge(m_free[b], k)

        m_done = [sem(f"m_done{i}") for i in range(8)]
        m_free = [sem(f"m_free{i}") for i in range(8)]

        PAIRED = [2 * NSP * (x // NSP) + x % NSP for x in range(KD * NSP)]
        GATES = [POS["ma", 0, s] for s in range(NSP)] + [MT_A + x for x in PAIRED[NSP:]] + list(range(MT_GH, MT_H)) + [MT_H + x for x in PAIRED]
        BRANCH = [MT_A + NSP + x for x in PAIRED] + [None] * (KD * NSP) + [MT_H + NSP + x for x in PAIRED]

        SPLITS = [NSP] + list(range(6, len(GATES), 6))

        def gate_used(eng, ns):
            if MT_GH <= GATES[ns] < MT_H:
                eng.wait_ge(S["m_mul"], GATES[ns] - MT_GH + 1)
            else:
                m_waitfree(eng, BRANCH[ns])

        def ld_w(n):
            return S["ld_w0"] if n % 2 == 0 else S["ld_w1"]

        def block_cols(b):
            if b < NB_U:
                return OFF_U + WC * b
            if b < NB_U + NB_A:
                H, kind = (b - NB_U) // 3, (b - NB_U) % 3
                return kind * QKV + HW * H
            return MB[b - NB_U - NB_A]

        def wait_block_used(eng, b):
            if b < NB_U:
                eng.wait_ge(S["u_ready"], 2 * NSP * (b + 1))
            elif b < NB_U + NB_A:
                H, kind = (b - NB_U) // 3, (b - NB_U) % 3
                eng.wait_ge(S["a_ready"], PT0[H] + (2 * NSP * (kind + 1) if kind < 2 else NPT[H]))
            else:
                m_all(eng, M_DONE[b - NB_U - NB_A])

        def ot_count(n):
            return n // 3 + 1

        def w_load(sp, b):
            if b >= 2:
                sp.wait_ge(S["w_lo"], b - 1)
            w, c = (w_in, block_cols(b)) if b < NB - 4 else (w_o, WC * (b - NB + 4))
            sp.dma_start((raw if b < NB_U + NB_A else mraw)[b % 2], w[:, c:c + WC].rearrange("(k p) c -> p k c", p=P)
                         ).then_inc(ld_w(b), 16)

        def w_max(dve, b):
            dve.wait_ge(ld_w(b), 16 * (b // 2 + 1))
            if b >= 3:
                dve.wait_ge(S["w_all"], b - 2)
            dve.tensor_reduce(amax[b % 3], (raw if b < NB_U + NB_A else mraw)[b % 2].rearrange("p k c -> p (k c)"), AX.X,
                              ALU.max, apply_absolute_value=True).then_inc(S["w_amax"], 1)

        def w_allmax(pool, b):
            pool.wait_ge(S["w_amax"], b + 1)
            if b >= 3:
                pool.wait_ge(S["w_scale"], b - 2)
            pool.partition_all_reduce(amax_all[b % 3], amax[b % 3], P, bass.bass_isa.ReduceOp.max).then_inc(S["w_all"], 1)

        def w_place(b):
            return ring[b % 3] if b < NB_U + NB_A else mring[b % 3] if b < NB - 1 else wb_split

        def w_hi(act, b):
            act.wait_ge(S["w_scale"], b + 1)
            if b == NB - 1:
                m_all(act, MT_O)
            elif b >= 3:
                wait_block_used(act, b - 3)
            act.activation(w_place(b)[:, 0], (raw if b < NB_U + NB_A else mraw)[b % 2], ACT.Copy, scale=wscale[b % 3]
                           ).then_inc(S["w_hi"], 1)

        def power_of_two(dve, chain, settle, out, mx, low):
            chain(dve.tensor_scalar(out.bitcast(I32), mx.bitcast(I32), 0x7F800000, None, ALU.bitwise_and))
            settle()
            chain(dve.tensor_scalar(out, out, 2.0 ** -86, low, ALU.max, ALU.mult))
            settle()

        def w_power(dve, chain, settle, b):
            i = b % 3
            dve.wait_ge(S["w_all"], b + 1)
            if b >= 3:
                dve.wait_ge(S["w_lo"], b - 2)
            power_of_two(dve, chain, settle, wexp[i], amax_all[i], 2.0 ** -14)
            chain(dve.reciprocal(wscale[i], wexp[i]))
            query = NB_U <= b < NB_U + NB_A and (b - NB_U) % 3 == 0
            dve.tensor_scalar(descale[b], wexp[i], xdescale if b < NB - 4 else 1.0, HD ** -0.5 if query else 1.0, ALU.mult, ALU.mult
                              ).then_inc(S["w_scale"], 1)
            settle()

        def w_low(dve, b):
            dve.wait_ge(S["w_hi"], b + 1)
            w = w_place(b)
            dve.scalar_tensor_tensor(w[:, 1], (raw if b < NB_U + NB_A else mraw)[b % 2], wscale[b % 3], w[:, 0], ALU.mult,
                                     ALU.subtract).then_inc(S["w_lo"], 1)

        def w_split(dve, chain, settle, b):
            w_power(dve, chain, settle, b)
            w_low(dve, b)

        PREPARED = NB_U + NB_A

        def prepare(H, m, scale=None, low=None, largest=None):
            _, i, b = ptile(H, m)
            if i == 0 and scale and b + 2 < PREPARED:
                scale(b + 2)
            if i == 1 and low and b + 2 < PREPARED:
                low(b + 2)
            if i == 2 and largest and b + 3 < PREPARED:
                largest(b + 3)

        mt_maxed, mt_all, mt_scaled, mt_hi, mt_lo = (sem(n) for n in ("mt_maxed", "mt_all", "mt_scaled", "mt_hi", "mt_lo"))
        ld_bias = [sem(f"ld_bias{i}") for i in range(2)]
        block = ctx.enter_context(nc.Block())

        @block.sync
        def _(sp):
            sp.dma_start(ident, cst["ident"]).then_inc(S["ld_small"], 16)
            r0 = 0
            for src, cnt in ((ins["conv_w"][0].rearrange("j (c p) -> (j c) p", p=P), 9 * KD),
                             (ins["conv_b"][0].rearrange("(c p) -> c p", p=P), 3 * KD),
                             (ins["pre_norm_g"][0].rearrange("(c p) -> c p", p=P), KD),
                             (ins["hyena_skip"][0].rearrange("o (c p) -> (o c) p", p=P), 2 * KD)):
                sp.dma_start(rows[r0:r0 + cnt, :], src).then_inc(S["ld_small"], 16)
                r0 += cnt
            for i, name in enumerate(("filt_b1", "filt_b2", "filt_b3", "filt_freq")):
                sp.dma_start(frows[i:i + 1, :], ins[name]).then_inc(S["ld_small"], 16)
            for G in range(3):
                src = ins["x_prompt"][0, BANK * G:BANK * G + BANK, :] if G < 2 else ins["x_sample"][0]
                sp.dma_start(xt[:, 4 * G:4 * G + 4, :], src.rearrange("(t p) d -> p t d", p=P)).then_inc(ld_x[G], 16)
                if G == 1:
                    w_load(sp, 0)
            sp.dma_start(feat[0:FEMB, :], cst["feat"]).then_inc(S["ld_tabs"], 16)
            sp.dma_start(fw[0:FEMB, 0:FHID], ins["filt_w1"][0]).then_inc(S["ld_tabs"], 16)
            sp.dma_start(fw[0:FHID, FHID:2 * FHID], ins["filt_w2"][0]).then_inc(S["ld_tabs"], 16)
            sp.dma_start(fw[0:FHID, 2 * FHID:3 * FHID], ins["filt_w3"][0]).then_inc(S["ld_tabs"], 16)
            sp.dma_start(hot[0:NBUCK, :], cst["hot"]).then_inc(S["ld_tabs"], 16)
            sp.dma_start(mask[0:HEADS, :], cst["mask"]).then_inc(S["ld_tabs"], 16)
            sp.dma_start(relb[0:NBUCK, :], ins["rel_bias"]).then_inc(S["ld_tabs"], 16)
            for b in range(1, NB_U + NB_A):
                w_load(sp, b)
            sp.wait_ge(S["a_ready"], PT0[6])
            sp.wait_ge(S["a_ov"], NSTEP)
            sp.wait_ge(S["hn_saved"], 16)
            for sl in range(3):
                sp.wait_ge(ot_out[sl], 16 * ot_count(6 * NT - 1))

            def load_filter(i):
                s, q, o = ITEMS[i]
                if i >= 2:
                    sp.wait_ge(S["f_gen"], GEN0[i - 1])
                sp.dma_start(w4[i % 2][0:FHID, :].rearrange("p (e c) -> p e c", e=2),
                             ins["filt_w4"][0].rearrange("k (o e c) -> k o e c", o=2, e=2)[:, o, :, FQ * q:FQ * q + FQ]
                             ).then_inc(ld_w4[i % 2], 16)
                if i >= 1:
                    sp.wait_ge(S["f_gen_used"], GEN0[i])
                sp.dma_start(dec[:, 0:ntile(i) + 1, :],
                             cst[f"dec{s}"][:, FQ * q:FQ * q + FQ].rearrange("(t p) c -> p t c", p=P)
                             ).then_inc(ld_dec, 16)

            def load_signal(i):
                s, q, o = ITEMS[i]
                if o == 0:
                    if i >= 2:
                        sp.wait_ge(hy_out[q % 2], 16 * zc_uses(i - 2))
                    sp.dma_start(zc[q % 2][:, :, 0:LENS[s]],
                                 uc_d[2 * q:2 * q + 2, :, UC0[s]:UC0[s] + LENS[s]].rearrange("c p t -> p c t")
                                 ).then_inc(ld_zc[q % 2], 16)

            load_filter(0)
            load_signal(0)
            sp.dma_start(ftab, cst["fwd0"]).then_inc(S["ld_ftab"], 16)
            sp.dma_start(itab, cst["inv0"]).then_inc(S["ld_itab"], 16)
            for i in range(NI):
                s, q, o = ITEMS[i]
                if i + 1 < NI:
                    load_filter(i + 1)
                    load_signal(i + 1)
                if i >= 1:
                    sp.wait_ge(S["f_post"], 2 * i)
                c0 = KD * (1 + o) + 2 * q
                sp.dma_start(hx[:, :, 0:LENS[s]], uc_d[c0:c0 + 2, :, UC0[s]:UC0[s] + LENS[s]].rearrange("c p t -> p c t")
                             ).then_inc(S["ld_hx"], 16)
                if i + 1 < NI and ITEMS[i + 1][0] != s:
                    for u in range(uz[i] + npair(i) - 4, uz[i] + npair(i)):
                        wait_ready(sp, u)
                    sp.dma_start(ftab[:, 0:DFTS[1]["fwd"].shape[1]], cst["fwd1"]).then_inc(S["ld_ftab"], 16)
                    for u in range(ui[i] + 4, ui[i] + 8):
                        wait_ready(sp, u)
                    sp.dma_start(itab[:, 0:DFTS[1]["inv"].shape[1]], cst["inv1"]).then_inc(S["ld_itab"], 16)
            for u in range(f_units - 4, f_units):
                wait_ready(sp, u)
            sp.wait_ge(S["f_post"], 2 * NI)
            for sl in range(2):
                sp.wait_ge(hy_out[sl], 16 * zc_uses(NI - 1))
            M0 = NB_U + NB_A
            w_load(sp, M0)
            w_load(sp, M0 + 1)
            ends = (0, SPANS[1] // 2, COL_S // 2, HC // 2)
            for s in range(NSP):
                sp.dma_start(hn_words.rearrange("p (k c) -> p k c", k=2 * KD)[:, :, ends[s]:ends[s + 1]],
                             hn_d.rearrange("p (k c) -> p k c", k=2 * KD)[:, :, ends[s]:ends[s + 1]]).then_inc(ld_hm[s], 16)
            w_load(sp, M0 + 2)
            w_load(sp, M0 + 3)
            ahead = iter(((4, 5, 6), (7,), (8,), (9,), (10, 11, 12, 13, 14), (15,), (16,), (17,)))
            for kind in range(2):
                for q in range(4):
                    if kind or q:
                        m_all(sp, (MT_A, MT_H)[kind] + 4 * NSP * q if q else MT_GH)
                    w = (w_a, w_h)[kind]
                    sp.dma_start(wb[:, 0:w.shape[0] // P, :], w[:, WC * q:WC * q + WC].rearrange("(k p) c -> p k c", p=P)
                                 ).then_inc(S["ld_wb"], 16)
                    for b in next(ahead):
                        w_load(sp, M0 + b)
            m_all(sp, MT_O)
            sp.dma_start(gpost, ins["post_norm_g"].to_broadcast([P, D])).then_inc(S["ld_gain"], 16)
            for t in range(NT):
                if t >= 2:
                    sp.wait_ge(S["o_y"], t - 1)
                src = ins["x_prompt"][0, P * t:P * t + P, :] if t < SP // P else ins["x_sample"][0, P * t - SP:P * t - SP + P, :]
                sp.dma_start(xres[t % 2], src).then_inc(ld_xr[t % 2], 16)

        NSMALL, NTABS = 16 * 9, 16 * 7

        @block.gpsimd
        def _(pool):
            for c in (0, COL_P + SP, COL_S + SS):
                pool.memset(hn_words.rearrange("p (k c) -> p k c", k=2 * KD)[:, :, c // 2:(c + PADC) // 2], 0.0
                            ).then_inc(S["pads_ok"], 1)
            for b in range(2):
                for c in (0, 1 + SP, UC_W + 1):
                    pool.memset(ub[b][:, c:c + 1], 0.0).then_inc(S["pads_ok"], 1)
            pool.wait_ge(S["g_amax"], 1)
            pool.partition_all_reduce(gmax_all, gmax, P, bass.bass_isa.ReduceOp.max).then_inc(S["g_all"], 1)
            for b in range(3):
                w_allmax(pool, b)
            pool.wait_ge(S["n_evD"], 24)
            pool.wait_ge(S["pads_ok"], 3)
            pool.dma_start(hn_d, hn_words).then_inc(S["hn_saved"], 16)
            pool.wait_ge(S["b_rows"], 1)
            pool.dma_start(brow_d, mask[0:HEADS, :].unsqueeze(1).to_broadcast([HEADS, P, 3 * BANK])).then_inc(S["b_stored"], 16)
            for c in range(3 * KD):
                if c % 2 == 0 and c // 2 + 3 < PREPARED:
                    w_allmax(pool, c // 2 + 3)
                pool.wait_ge(S["u_conv"], c + 1)
                pool.dma_start(uc_d[c], ut[c % 3]).then_inc(uc_out[c % 3], 16)
            def skewed(g, q0, n, h0, width):
                return bass.AP(dram["brow"], BANK * g + q0 + h0 * P * 3 * BANK, [[3 * BANK - 1, n], [P * 3 * BANK, HH], [1, width]])

            for i in range(3):
                pool.wait_ge(uc_out[i], 16 * KD)
            pool.wait_ge(S["b_stored"], 16)
            pool.wait_ge(S["h_sin"], 3)
            pool.wait_ge(S["n_T"], 24)
            for b in range(2):
                for c in (0, COL_P + SP, COL_S + SS):
                    pool.memset(kt[b][:, :, c:c + PADC], 0.0).then_inc(S["pads_ok"], 1)

            def load_bias(H):
                g, h0 = H // 2, HH * (H % 2)
                if H >= 2:
                    pool.wait_ge(S["a_biased"], STEPS * (H - 1))
                if g < 2:
                    pool.dma_start(bwt[H % 2], skewed(g, P - 1, P, h0, BW)).then_inc(ld_bias[H % 2], 16)
                else:
                    for seq in range(2):
                        pool.dma_start(b2t[H % 2][:, :, P * seq:P * seq + P],
                                       skewed(2, P - 1 + seq * (2 * P - 1), P, h0, P)).then_inc(ld_bias[H % 2], 16)

            load_bias(0)
            load_bias(1)
            for m in range(NPT[0]):
                prepare(0, m, largest=lambda b: w_allmax(pool, b))
            for N in range(NSTEP + 2):
                if N % STEPS == 0 and 0 < N < NSTEP - STEPS:
                    load_bias(N // STEPS + 1)
                if 1 <= N <= NSTEP:
                    for H, m in MIX[N - 1]:
                        prepare(H, m, largest=lambda b: w_allmax(pool, b))
                if N >= 3 and N % 2 == 1:
                    H, g, t, _ = unit(N - 2)
                    n = (N - 3) // 2
                    pool.wait_ge(S["a_oevac"], n + 1)
                    seq = 0 if t < SP // P else 1
                    r, tt = stride(g, seq), t - TOK0[seq] // P
                    per = LENS[seq] // r
                    a = TOK0[seq] + P * tt // per + r * (P * tt % per)
                    pool.dma_start(og_d[g, a:a + r * (P - 1) + 1:r, H % 2, :], ot[n % 3]).then_inc(ot_out[n % 3], 16)
            def sums(i, j):
                n = GEN0[i] + j
                h = hfb[n % 2]
                pool.wait_ge(S["f_gen_used"], n + 1)
                if i >= 1:
                    pool.wait_ge(S["f_bf"], 3 * i - 1)
                nc.gpsimd.tensor_tensor(tge[:, j, :], h[:, 0:FQ], h[:, FQ:2 * FQ], ALU.add)
                nc.gpsimd.tensor_tensor(tgo[:, j, :], h[:, 0:FQ], h[:, FQ:2 * FQ], ALU.subtract).then_inc(S["f_ge"], 1)

            for j in range(ntile(0)):
                sums(0, j)
            for i in range(NI):
                for p in range(npair(i)):
                    n = PR0[i] + p
                    a = pq[n % 2]
                    wait_free(pool, uz[i] + p)
                    nc.gpsimd.tensor_tensor(yf[:, p, 0:FQ], a[:, 0:FQ], a[:, 3 * FQ:4 * FQ], ALU.subtract)
                    nc.gpsimd.tensor_tensor(yf[:, p, FQ:2 * FQ], a[:, FQ:2 * FQ], a[:, 2 * FQ:3 * FQ], ALU.add
                                            ).then_inc(S["f_y"], 1)
                    if i + 1 < NI and p < ntile(i + 1):
                        sums(i + 1, p)
                s, q, o = ITEMS[i]
                if o == 1:
                    pool.wait_ge(S["f_post"], 2 * (i + 1))
                    pool.dma_start(hy_d[2 * q:2 * q + 2, :, TOK0[s]:TOK0[s] + LENS[s]].rearrange("c p t -> p c t"),
                                   zc[q % 2][:, :, 0:LENS[s]]).then_inc(hy_out[q % 2], 16)
            M0 = NB_U + NB_A
            for b in range(3):
                w_allmax(pool, M0 + b)
            for t in range(NT):
                if t == 0:
                    w_allmax(pool, M0 + 3)
                if t == 0:
                    for u in range(f_units - 4, f_units):
                        wait_ready(pool, u)
                    pool.wait_ge(S["f_post"], 2 * NI)
                    for sl in range(2):
                        pool.wait_ge(hy_out[sl], 16 * zc_uses(NI - 1))
                    for sl in range(3):
                        pool.wait_ge(ot_out[sl], 16 * ot_count(6 * NT - 1))
                if t >= 2:
                    pool.wait_ge(S["g_cmb"], t - 1)
                pool.dma_start(ogt[t % 2], og_d[:, P * t:P * t + P, :, :].rearrange("g p a c -> p g a c")).then_inc(ld_og[t % 2], 16)
            for b in range(4, 9):
                w_allmax(pool, M0 + b)
            m_all(pool, MT_GH)
            m_allfree(pool, MT_GH)
            for j in range(KD):
                pool.dma_start(hg[:, j, :], hy_d[j]).then_inc(ld_hy[j], 16)
            for b in range(9, NB_M):
                w_allmax(pool, M0 + b)
            pool.wait_ge(mt_maxed, 1)
            pool.partition_all_reduce(m_all_max, m_max, P, bass.bass_isa.ReduceOp.max).then_inc(mt_all, 1)
            for t in range(NT):
                pool.wait_ge(S["o_y"], t + 1)
                dst = y_p[0, P * t:P * t + P, :] if t < SP // P else y_s[0, P * t - SP:P * t - SP + P, :]
                pool.dma_start(dst, yout[t % 2]).then_inc(y_out[t % 2], 16)
            for sl in range(2):
                pool.wait_ge(y_out[sl], 16 * (NT // 2))

        @block.tensor
        def _(pe):
            def split_product(out, ks, lhs, rhs):
                for k in ks:
                    for x, (a, b) in enumerate(((0, 0), (0, 1), (1, 0))):
                        mm = pe.matmul(out, lhs(a, k), rhs(b, k), start=(k == 0 and x == 0), stop=(k == KD - 1 and x == 2))
                return mm

            pe.wait_ge(S["ld_small"], NSMALL)
            pe.transpose(ps[:, 0, 0:NCOLS], rows[0:NCOLS, :], ident[0:NCOLS, 0:NCOLS])
            pe.transpose(ps[0:FHID, 0, P:P + 4], frows[0:4, :], ident[0:4, 0:4]).then_inc(S["rows_T"], 1)
            pe.wait_ge(S["fcols_ok"], 1)
            for G in range(3):
                for k in range(KD):
                    n = KD * G + k
                    if k == 0:
                        pe.wait_ge(S["n_scaled"], 4 * (G + 1))
                    if n >= 4:
                        pe.wait_ge(S["n_evD"], n - 3)
                    for j in range(4):
                        mm = pe.transpose(ps[:, n % 4, P * j:P * j + P], xt[:, 4 * G + j, P * k:P * k + P], ident)
                    mm.then_inc(S["n_T"], 1)
            pe.wait_ge(S["n_evD"], 24)
            pe.wait_ge(S["pads_ok"], 9)
            pe.wait_ge(S["ld_tabs"], NTABS)
            for g in range(3):
                mm = pe.matmul(ps[0:HEADS, g, :], relb[0:NBUCK, HEADS * g:HEADS * g + HEADS],
                               hot[0:NBUCK, BANK * g:BANK * g + BANK], start=True, stop=True)
            mm.then_inc(S["b_mm"], 1)

            def filter_layer(l):
                if l == 0:
                    pe.wait_ge(S["b_rows"], 1)
                else:
                    pe.wait_ge(S["h_sin"], l)
                kk = FEMB if l == 0 else FHID
                for s in range(3):
                    src = feat if l == 0 else hid
                    mm = pe.matmul(ps[0:FHID, s, :], fw[0:kk, FHID * l:FHID * l + FHID],
                                   src[0:kk, BANK * s:BANK * s + BANK], start=True, stop=True)
                mm.then_inc(S["h_mm"], 1)

            for c in range(3 * KD):
                b = c // 2
                if c % 2 == 0:
                    pe.wait_ge(S["w_lo"], b + 1)
                for s in range(NSP):
                    n = NSP * c + s
                    if n >= 4:
                        pe.wait_ge(S["u_evac"], n - 3)
                    split_product(ps[:, 4 + n % 4, :], range(KD),
                                  lambda a, k: ring[b % 3][:, a, k, P * (c % 2):P * (c % 2) + P],
                                  lambda a, k: hn[:, a, k, SPANS[s]:SPANS[s] + BANK]).then_inc(S["u_ready"], 1)
                if c in (2, 6, 10):
                    filter_layer((c - 2) // 4)
            pe.wait_ge(S["u_evac"], U_TILES)
            pe.wait_ge(S["h_arg"], 3)

            def project(H, m, u):
                kind, i, b = ptile(H, m)
                n = PT0[H] + m
                if i == 0 and u == 0:
                    pe.wait_ge(S["w_lo"], b + 1)
                if n >= 2 and u == 0:
                    pe.wait_ge(S["a_evac"], n - 1)
                w = ring[b % 3]
                if kind < 2:
                    j, s = i // NSP, i % NSP
                    mm = split_product(ps[:, n % 2, :], (u,), lambda a, k: w[:, a, k, P * j:P * j + P],
                                       lambda a, k: hn[:, a, k, SPANS[s]:SPANS[s] + BANK])
                else:
                    x = u // 4
                    c, r = value_tiles(H // 2)[2 * i + x]
                    mm = split_product(ps[:, n % 2, HW * x:HW * x + HW], (2 * (u % 4), 2 * (u % 4) + 1),
                                       lambda a, k: hn[:, a, k, c:c + r * (P - 1) + 1:r], lambda a, k: w[:, a, k, :])
                if u == KD - 1:
                    mm.then_inc(S["a_ready"], 1)

            def score(N):
                H, g, t, h = unit(N)
                if N % STEPS == 0:
                    pe.wait_ge(S["a_evac"], PT0[H] + 4 * NSP)
                    if N == 0:
                        pe.wait_ge(S["pads_ok"], 15)
                k0, kw = windows(g, t)[:2]
                if N >= 2:
                    pe.wait_ge(S["a_biased"], N - 1)
                for x in range(2):
                    r = slice(HD * h, HD * h + HD)
                    mm = pe.matmul(ps[:, 2 + N % 2, 2 * P * x:2 * P * x + kw], qt[H % 2][r, x, P * t:P * t + P],
                                   kt[H % 2][r, x, k0:k0 + kw], start=True, stop=True)
                mm.then_inc(S["a_score"], 1)

            def turn(N):
                H, g, t, h = unit(N)
                kw = windows(g, t)[1]
                pe.wait_ge(S["a_prob"], 2 * N + 2)
                if N >= 2:
                    pe.wait_ge(S["a_ptcopied"], N - 1)
                for x in range(2):
                    for b in range(kw // P):
                        mm = pe.transpose(ps[:, 4 + N % 2, 2 * P * x + P * b:2 * P * x + P * b + P],
                                          pr[N % 2][:, x, P * b:P * b + P], ident)
                mm.then_inc(S["a_pT"], 1)

            def value(N):
                H, g, t, h = unit(N)
                vs = windows(g, t)[3]
                if N % STEPS == 0:
                    pe.wait_ge(S["a_evac"], PT0[H + 1])
                pe.wait_ge(S["a_ptcopied"], N + 1)
                if h == 0 and N >= 4:
                    pe.wait_ge(S["a_oevac"], N // 2 - 1)
                for x in range(2):
                    for b, vi in enumerate(vs):
                        c = slice(HD * (h + 2 * x), HD * (h + 2 * x) + HD)
                        mm = pe.matmul(ps[:, 6 + t % 2, c], pt[N % 2][:, x, P * b:P * b + P], vt[H % 2][:, vi, c],
                                       start=(b == 0), stop=(b == len(vs) - 1))
                mm.then_inc(S["a_ov"], 1)

            for m in range(NPT[0]):
                for u in range(KD):
                    project(0, m, u)
            score(0)
            for N in range(NSTEP + 1):
                if N + 1 < NSTEP:
                    score(N + 1)
                if N < NSTEP:
                    turn(N)
                if N >= 1:
                    value(N - 1)
                if N < NSTEP:
                    for part in PARTS[N]:
                        project(*part)
            pe.wait_ge(S["a_ptcopied"], NSTEP)
            pe.wait_ge(S["a_oevac"], 6 * NT)

            def gen(i, j):
                s = ITEMS[i][0]
                if j == 0:
                    pe.wait_ge(ld_w4[i % 2], 16 * (i // 2 + 1))
                n = GEN0[i] + j
                if n >= 2:
                    pe.wait_ge(S["f_gen_used"], n - 1)
                pe.matmul(ps[:, n % 2, :], h3[0:FHID, TOK0[s] + P * j:TOK0[s] + P * j + P], w4[i % 2][0:FHID, :],
                          start=True, stop=True).then_inc(S["f_gen"], 1)

            def spectrum(out, terms, a):
                for x, (comp, c, tab) in enumerate(terms):
                    mm = pe.matmul(out, ftab[:, P * tab:P * tab + P], a[:, comp, FQ * c:FQ * c + FQ],
                                   start=(x == 0), stop=(x == len(terms) - 1))
                return mm

            def filter_dft(i):
                s = ITEMS[i][0]
                pe.wait_ge(S["ld_ftab"], 16 * (s + 1))
                pe.wait_ge(S["f_bf"], 3 * i + 1)
                ge, go = fa[3 * i % 2], fa[(3 * i + 1) % 2]
                pairs, half = DFTS[s]["pairs"], npair(i) // 2
                for n in range(npair(i) + 1):
                    u = uk[i] + n
                    if u >= 4:
                        wait_free(pe, u - 4)
                    if n == half + 1:
                        pe.wait_ge(S["f_bf"], 3 * i + 2)
                    if n == half:
                        mm = spectrum(ps[:, fbank(u), 0:FQ], pairs[0][3], ge)
                    else:
                        for x in range(2):
                            terms = pairs[2 * n + x][0] if n < half else pairs[2 * (n - half - 1) + x][2]
                            mm = spectrum(ps[:, fbank(u), FQ * x:FQ * x + FQ], terms, ge if n < half else go)
                    mm.then_inc(bank_ready[fbank(u)], 1)

            def signal_dft(i):
                s = ITEMS[i][0]
                pe.wait_ge(S["f_bf"], 3 * i + 3)
                a = fa[(3 * i + 2) % 2]
                for p in range(npair(i)):
                    u = uz[i] + p
                    wait_free(pe, u - 4)
                    spectrum(ps[:, fbank(u), 0:FQ], DFTS[s]["pairs"][p][0], a)
                    spectrum(ps[:, fbank(u), FQ:2 * FQ], DFTS[s]["pairs"][p][1], a
                             ).then_inc(bank_ready[fbank(u)], 1)
                    if i + 1 < NI and p < ntile(i + 1):
                        gen(i + 1, p)

            def inverse(i):
                s = ITEMS[i][0]
                pe.wait_ge(S["ld_itab"], 16 * (s + 1))
                for ct in range(2):
                    for x, blk in enumerate(ORDER):
                        u = ui[i] + 4 * ct + x
                        wait_free(pe, u - 4)
                        terms = DFTS[s]["units"][blk]
                        if ct == 0:
                            pe.wait_ge(S["f_y"], PR0[i] + max(term[0] for term in terms) + 1)
                        for n, (p, im, col, oc, w) in enumerate(terms):
                            starts = n == 0 or terms[n - 1][3] != oc
                            stops = n == len(terms) - 1 or terms[n + 1][3] != oc
                            mm = pe.matmul(ps[:, fbank(u), oc:oc + w],
                                           yf[:, p, FQ * im + P * ct:FQ * im + P * ct + P], itab[:, col:col + w],
                                           start=starts, stop=stops)
                        mm.then_inc(bank_ready[fbank(u)], 1)

            def to_time(i):
                s, q, o = ITEMS[i]
                if o == 0:
                    pe.wait_ge(ld_zc[q % 2], 16 * zc_uses(i))
                else:
                    pe.wait_ge(S["f_post"], 2 * (i - 1))
                for j in range(ntile(i) // 2):
                    n = TR0[i] + j
                    if n >= 2:
                        pe.wait_ge(S["f_tz"], n - 1)
                    for x in range(4):
                        a = P * (2 * j + x // 2)
                        mm = pe.transpose(ps[:, 6 + n % 2, P * x:P * x + P], zc[q % 2][:, x % 2, a:a + P], ident)
                    mm.then_inc(S["f_zT"], 1)

            for j in range(ntile(0)):
                gen(0, j)
            to_time(0)
            filter_dft(0)
            for i in range(NI):
                signal_dft(i)
                if i + 1 < NI:
                    to_time(i + 1)
                inverse(i)
                if i + 1 < NI:
                    filter_dft(i + 1)
            for u in range(f_units - 4, f_units):
                wait_free(pe, u)
            pe.wait_ge(S["f_gen_used"], GEN0[NI])
            pe.wait_ge(S["f_tz"], TR0[NI])

            def m_tile(n, kc, lhs, rhs):
                if n >= 8:
                    m_waitfree(pe, n - 8)
                for k in range(kc):
                    mm = pe.matmul(ps[:, n % 8, :], lhs(k), rhs(k), start=(k == 0), stop=(k == kc - 1))
                mm.then_inc(m_done[n % 8], 1)

            def gate_tile(n, i, d, s):
                b = NB_U + NB_A + i
                pe.wait_ge(S["w_lo"], b + 1)
                if n >= 8:
                    m_waitfree(pe, n - 8)
                split_product(ps[:, n % 8, :], range(KD), lambda a, k: mring[b % 3][:, a, k, P * (d % 2):P * (d % 2) + P],
                              lambda a, k: hn[:, a, k, SPANS[s]:SPANS[s] + BANK]).then_inc(m_done[n % 8], 1)

            for n, (kind, x, s) in enumerate(MSEQ):
                if kind != "T":
                    if kind == "ga" and x == 0:
                        pe.wait_ge(ld_hm[s], 16)
                    gate_tile(n, x // 2 if kind == "ga" else 2, x, s)
                    continue
                if n >= 8:
                    m_waitfree(pe, n - 8)
                pe.wait_ge(S["g_cmb"], x + 1)
                for j in range(4):
                    mm = pe.transpose(ps[:, n % 8, P * j:P * j + P], cmb[x % 2][:, 0, P * j:P * j + P], ident)
                mm.then_inc(m_done[n % 8], 1)
            for kind, n0, i0, kc, src in ((0, MT_A, 2, 4, at), (1, MT_H, 10, KD, hg)):
                if kind == 1:
                    for j in range(KD):
                        for s in range(NSP):
                            gate_tile(MT_GH + NSP * j + s, 6 + j // 2, j, s)
                for d in range(KD):
                    for s in range(NSP):
                        if kind or d:
                            gate_tile(n0 + 2 * NSP * d + s, i0 + d // 2, d, s)
                    if d == 0:
                        if kind == 0:
                            m_waitfree(pe, POS["T", NT - 1, 0])
                        else:
                            pe.wait_ge(S["m_mul"], KD * NSP)
                    pe.wait_ge(S["ld_wb"], 16 * (4 * kind + d // 2 + 1))
                    for s in range(NSP):
                        m_tile(n0 + 2 * NSP * d + NSP + s, kc, lambda k: wb[:, k, P * (d % 2):P * (d % 2) + P],
                               lambda k: src[:, k, BANK * s:BANK * s + BANK])
            m_allfree(pe, MT_O)
            for t in range(NT):
                pe.wait_ge(mt_lo, t + 1)
                for half in range(2):
                    n = MT_O + 2 * t + half
                    m_waitfree(pe, n - 8)
                    for x in range(2):
                        b = NB - 4 + 2 * half + x
                        if t == 0:
                            pe.wait_ge(S["w_lo"], b + 1)
                        mm = split_product(ps[:, n % 8, WC * x:WC * x + WC], range(KD),
                                           lambda a, k: m16[:, a, k, P * t:P * t + P], lambda a, k: w_place(b)[:, a, k, :])
                    mm.then_inc(m_done[n % 8], 1)

        @block.scalar
        def _(act):
            def root_mean_squares(G):
                act.wait_ge(ld_x[G], 16)
                for t in range(4 * G, 4 * G + 4):
                    if t >= 2:
                        act.wait_ge(S["n_sq"], t - 1)
                    act.activation(junk[t % 2], xt[:, t, :], ACT.Square, accum_out=ssq[:, t:t + 1]).then_inc(S["n_sq"], 1)
                act.wait_ge(S["n_mean"], G + 1)
                act.activation(rstd[:, 4 * G:4 * G + 4], rstd[:, 4 * G:4 * G + 4], ACT.Sqrt).then_inc(S["n_root"], 1)

            def normed_hi(G):
                for k in range(KD):
                    n = KD * G + k
                    act.wait_ge(S["n_T"], n + 1)
                    act.activation(hn[:, 0, k, SPANS[G]:SPANS[G] + BANK], ps[:, n % 4, :], ACT.Copy, scale=gscaled[:, k:k + 1]
                                   ).then_inc(S["n_evA"], 1)

            root_mean_squares(0)
            root_mean_squares(1)
            act.wait_ge(S["g_scale"], 1)
            normed_hi(0)
            root_mean_squares(2)
            normed_hi(1)
            w_hi(act, 0)
            normed_hi(2)
            w_hi(act, 1)

            def sine(l):
                act.wait_ge(S["h_arg"], l + 1)
                dst = hid if l < 2 else h3
                act.activation(dst[0:FHID, :], xt[0:FHID, 3:5, :].rearrange("p a c -> p (a c)")[:, 0:T], ACT.Sin
                               ).then_inc(S["h_sin"], 1)

            act.wait_ge(S["pads_ok"], 9)
            for c in range(3 * KD):
                u, o = ub[c % 2], ut[c % 3]
                if c % 2 == 0 and c // 2 + 2 < PREPARED:
                    w_hi(act, c // 2 + 2)
                for s in range(NSP):
                    n = NSP * c + s
                    act.wait_ge(S["u_ready"], n + 1)
                    if s == 0 and c >= 2:
                        act.wait_ge(S["u_conv"], c - 1)
                    at0 = 1 + BANK * s + (s == 2)
                    act.activation(u[:, at0:at0 + BANK], ps[:, 4 + n % 4, :], ACT.Copy, scale=descale[c // 2]
                                   ).then_inc(S["u_evac"], 1)
                act.wait_ge(S["u_evac"], NSP * (c + 1))
                if c >= 3:
                    act.wait_ge(uc_out[c % 3], 16 * (c // 3))
                act.activation(o, u[:, 1:1 + UC_W], ACT.Identity, scale=cols[:, CW + 3 * KD + c:CW + 3 * KD + c + 1],
                               bias=cols[:, CB + c:CB + c + 1]).then_inc(S["u_mid"], 1)
                if c in (4, 8, 12):
                    sine((c - 4) // 4)
            act.wait_ge(S["u_conv"], 3 * KD)
            for i in range(3):
                act.wait_ge(uc_out[i], 16 * KD)
            act.wait_ge(S["b_stored"], 16)

            def evacuate(H, m):
                prepare(H, m, scale=lambda b: w_hi(act, b))
                kind, i, b = ptile(H, m)
                n, g = PT0[H] + m, H // 2
                src = ps[:, n % 2, :]
                act.wait_ge(S["a_ready"], n + 1)
                if kind == 2:
                    dst = vt[H % 2][:, 2 * i:2 * i + 2, :]
                    src = src.rearrange("p (a c) -> p a c", a=2)
                else:
                    j, s = i // NSP, i % NSP
                    seq = 0 if s < 2 else 1
                    r = stride(g, seq)
                    if g == 0 and kind == 1:
                        dst = kt[H % 2][:, j, SPANS[s]:SPANS[s] + BANK]
                    else:
                        i0 = BANK * s // r if seq == 0 else 0
                        buf = (qt, kt)[kind][H % 2][:, j, TOK0[seq]:TOK0[seq] + LENS[seq]]
                        dst = buf.rearrange("p (r i) -> p r i", r=r)[:, :, i0:i0 + BANK // r]
                        src = src.rearrange("p (i r) -> p r i", r=r)
                act.activation(dst, src, ACT.Copy, scale=descale[b]).then_inc(S["a_evac"], 1)

            def prob(N):
                H, g, t, h = unit(N)
                kw = windows(g, t)[1]
                o = ot[N // 2 % 3]
                act.wait_ge(S["a_max"], N + 1)
                if N >= 2:
                    act.wait_ge(S["a_pT"], N - 1)
                for x in range(2):
                    c = HW + h + 2 * x
                    act.activation(pr[N % 2][:, x, 0:kw], lg[N % 2][:, x, 0:kw], ACT.Exp, bias=o[:, c:c + 1],
                                   accum_out=o[:, c + HH:c + HH + 1]).then_inc(S["a_prob"], 1)

            def copy(N):
                kw = windows(unit(N)[1], unit(N)[2])[1]
                act.wait_ge(S["a_pT"], N + 1)
                if N >= 2:
                    act.wait_ge(S["a_ov"], N - 1)
                act.activation(pt[N % 2][:, :, 0:kw], ps[:, 4 + N % 2, :].rearrange("p (x c) -> p x c", x=2)[:, :, 0:kw],
                               ACT.Copy).then_inc(S["a_ptcopied"], 1)

            def result(n):
                act.wait_ge(S["a_ov"], 2 * n + 2)
                if n >= 3:
                    act.wait_ge(ot_out[n % 3], 16 * ot_count(n - 3))
                act.activation(ot[n % 3][:, 0:HW], ps[:, 6 + n % 2, 0:HW], ACT.Copy).then_inc(S["a_oevac"], 1)

            for m in range(NPT[0]):
                evacuate(0, m)
            prob(0)
            for N in range(NSTEP + 2):
                if N < NSTEP:
                    copy(N)
                if 1 <= N <= NSTEP:
                    for H, m in MIX[N - 1]:
                        evacuate(H, m)
                if N + 1 < NSTEP:
                    prob(N + 1)
                if N >= 3 and N % 2 == 1:
                    result((N - 3) // 2)
            def filter_copy(i):
                if i >= 1:
                    for u in range(uz[i - 1] + npair(i - 1) - 4, uz[i - 1] + npair(i - 1)):
                        wait_free(act, u)
                half = npair(i) // 2
                for n in range(npair(i) + 1):
                    u = uk[i] + n
                    wait_ready(act, u)
                    src = ps[:, fbank(u), :].rearrange("p (a c) -> p a c", a=2)
                    if n == half:
                        src, dst = ps[:, fbank(u), 0:FQ], kfl
                    elif n < half:
                        dst = kf[:, 2 * n:2 * n + 2, 0:FQ]
                    else:
                        dst = kf[:, 2 * (n - half - 1):2 * (n - half), FQ:2 * FQ]
                    act.activation(dst, src, ACT.Copy).then_inc(bank_free[fbank(u)], 1)

            def time_copy(i):
                if i >= 1:
                    act.wait_ge(S["f_bf"], 3 * i)
                for j in range(ntile(i) // 2):
                    n = TR0[i] + j
                    act.wait_ge(S["f_zT"], n + 1)
                    act.activation(tz[:, 2 * j:2 * j + 2, :], ps[:, 6 + n % 2, :].rearrange("p (a c) -> p a c", a=2),
                                   ACT.Copy).then_inc(S["f_tz"], 1)

            time_copy(0)
            filter_copy(0)
            for i in range(NI):
                w2 = 2 * DFTS[ITEMS[i][0]]["w"]
                if i + 1 < NI:
                    time_copy(i + 1)
                for ct in range(2):
                    m = 2 * i + ct
                    for x, dst in ((0, iv0), (1, iv1)):
                        u = ui[i] + 4 * ct + x
                        if m >= 2:
                            act.wait_ge(S["f_post"], m - 1)
                        wait_ready(act, u)
                        act.activation(dst[m % 2][:, 0:w2], ps[:, fbank(u), 0:w2], ACT.Copy
                                       ).then_inc(bank_free[fbank(u)], 1)
                if i + 1 < NI:
                    filter_copy(i + 1)
            act.wait_ge(ld_hm[0], 16)

            def combine(t):
                act.wait_ge(S["g_sc"], 2 * t + 1)
                act.activation(wts[t % 2][:, 8:32], wts[t % 2][:, 8:32], ACT.Exp).then_inc(S["g_exp"], 1)

            M0 = NB_U + NB_A
            w_hi(act, M0)
            w_hi(act, M0 + 1)
            w_hi(act, M0 + 2)
            for n, (kind, x, s) in enumerate(MSEQ):
                if n in (1, 3):
                    combine(n // 2)
                if kind == "T":
                    if x + 2 < NT:
                        combine(x + 2)
                    continue
                m_wait(act, n)
                if kind == "ga":
                    act.activation(ga[:, x, BANK * s:BANK * s + BANK], ps[:, n % 8, :], ACT.Silu, scale=descale[M0 + x // 2]
                                   ).then_inc(m_free[n % 8], 1)
                else:
                    act.activation(sg[s], ps[:, n % 8, :], ACT.Sigmoid, scale=descale[M0 + 2]).then_inc(m_free[n % 8], 1)
            w_hi(act, M0 + 3)
            for ns, n in enumerate(GATES):
                i = 2 + ns // 6
                if ns < NSP:
                    continue
                if ns in SPLITS and i + 2 < NB_M:
                    w_hi(act, M0 + i + 2)
                m_wait(act, n)
                if ns >= 3:
                    gate_used(act, ns - 3)
                act.activation(sg[ns % 3], ps[:, n % 8, :], ACT.Silu if MT_GH <= n < MT_H else ACT.Sigmoid,
                               scale=descale[M0 + i]).then_inc(m_free[n % 8], 1)
            w_hi(act, NB - 2)
            w_hi(act, NB - 1)
            act.wait_ge(mt_scaled, 1)

            def merged_hi(t):
                act.activation(m16[:, 0, :, P * t:P * t + P], mt[:, :, P * t:P * t + P], ACT.Copy, scale=m_scale
                               ).then_inc(mt_hi, 1)

            for t in range(3):
                merged_hi(t)
            for t in range(NT):
                if t + 3 < NT:
                    merged_hi(t + 3)
                for half in range(2):
                    n = MT_O + 2 * t + half
                    m_wait(act, n)
                    for x in range(2):
                        j = 2 * half + x
                        act.activation(osq[:, WC * j:WC * j + WC], ps[:, n % 8, WC * x:WC * x + WC], ACT.Square,
                                       scale=o_descale[:, j:j + 1], accum_out=ssq2[:, 4 * (t % 2) + j:4 * (t % 2) + j + 1]
                                       ).then_inc(S["o_sq"], 1)
                act.wait_ge(S["o_r"], 2 * t + 1)
                act.activation(rstd2[:, t:t + 1], rstd2[:, t:t + 1], ACT.Sqrt).then_inc(S["o_root"], 1)

        @block.vector
        def _(dve):
            steps = [0]

            def chain(op):
                op.then_inc(S["dve_steps"], 1)
                steps[0] += 1

            def settle():
                dve.wait_ge(S["dve_steps"], steps[0])

            dve.wait_ge(S["rows_T"], 1)
            dve.tensor_copy(cols[:, 0:NCOLS], ps[:, 0, 0:NCOLS]).then_inc(S["cols_ok"], 1)
            dve.tensor_copy(fcol[0:FHID, 0:4], ps[0:FHID, 0, P:P + 4]).then_inc(S["fcols_ok"], 1)
            dve.wait_ge(S["cols_ok"], 1)

            def evac(n):
                G, k = n // KD, n % KD
                dve.wait_ge(S["n_evA"], n + 1)
                dst = hn[:, :, k, SPANS[G]:SPANS[G] + BANK]
                dve.scalar_tensor_tensor(dst[:, 1], ps[:, n % 4, :], gscaled[:, k:k + 1], dst[:, 0], ALU.mult, ALU.subtract
                                         ).then_inc(S["n_evD"], 1)

            dve.tensor_reduce(gmax, cols[:, CG:CG + KD], AX.X, ALU.max, apply_absolute_value=True).then_inc(S["g_amax"], 1)
            dve.wait_ge(S["g_all"], 1)
            power_of_two(dve, chain, settle, xdescale, gmax_all, 2.0 ** -15 * 2.0 ** math.ceil(math.log2(2 * math.sqrt(D))))
            chain(dve.reciprocal(xscale, xdescale))
            settle()
            dve.tensor_scalar(gscaled, cols[:, CG:CG + KD], xscale, None, ALU.mult).then_inc(S["g_scale"], 1)
            dve.wait_ge(S["g_scale"], 1)

            def normalise(G):
                a, b = 4 * G, 4 * G + 4
                dve.wait_ge(S["n_sq"], b)
                dve.tensor_scalar(rstd[:, a:b], ssq[:, a:b], 1.0 / D, EPS, ALU.mult, ALU.add).then_inc(S["n_mean"], 1)
                dve.wait_ge(S["n_root"], G + 1)
                dve.reciprocal(rstd[:, a:b], rstd[:, a:b]).then_inc(S["n_rstd"], 1)
                dve.wait_ge(S["n_rstd"], G + 1)
                for t in range(a, b):
                    dve.tensor_scalar(xt[:, t, :], xt[:, t, :], rstd[:, t:t + 1], None, ALU.mult).then_inc(S["n_scaled"], 1)

            def normed_lo(G):
                for k in range(KD):
                    evac(KD * G + k)

            normalise(0)
            normalise(1)
            normed_lo(0)
            w_max(dve, 0)
            w_max(dve, 1)
            normalise(2)
            w_power(dve, chain, settle, 0)
            w_power(dve, chain, settle, 1)
            normed_lo(1)
            normed_lo(2)
            w_low(dve, 0)
            w_low(dve, 1)
            w_max(dve, 2)
            dve.wait_ge(S["b_mm"], 1)
            m3 = mask[0:HEADS, :].rearrange("p (a c) -> p a c", a=3)
            dve.tensor_tensor(m3, ps[0:HEADS, 0:3, :], m3, ALU.add).then_inc(S["b_rows"], 1)

            TWO_PI = 2.0 * math.pi
            HI = float(np.float32(6.28125))
            LO = float(np.float32(TWO_PI - HI))
            ROUND = float(1.5 * 2 ** 23)
            LIM = float(np.float32(3.1415925))

            def argument(l):
                val = xt[0:FHID, 0:2, :].rearrange("p a c -> p (a c)")[:, 0:T]
                trn = xt[0:FHID, 6:8, :].rearrange("p a c -> p (a c)")[:, 0:T]
                arg = xt[0:FHID, 3:5, :].rearrange("p a c -> p (a c)")[:, 0:T]
                dve.wait_ge(S["h_mm"], l + 1)
                chain(dve.tensor_scalar(val.rearrange("p (a c) -> p a c", a=3), ps[0:FHID, 0:3, :], fcol[0:FHID, l:l + 1],
                                        fcol[0:FHID, 3:4], ALU.add, ALU.mult))
                settle()
                chain(dve.tensor_scalar(trn, val, 1.0 / TWO_PI, ROUND, ALU.mult, ALU.add))
                settle()
                chain(dve.tensor_scalar(trn, trn, -ROUND, None, ALU.add))
                settle()
                chain(dve.scalar_tensor_tensor(val, trn, -HI, val, ALU.mult, ALU.add))
                settle()
                chain(dve.scalar_tensor_tensor(val, trn, -LO, val, ALU.mult, ALU.add))
                settle()
                dve.tensor_scalar(arg, val, LIM, -LIM, ALU.min, ALU.max).then_inc(S["h_arg"], 1)

            for c in range(3 * KD):
                u, o = ub[c % 2], ut[c % 3]
                if c % 2 == 0 and c // 2 + 2 < PREPARED:
                    w_split(dve, chain, settle, c // 2 + 2)
                if c % 2 == 0 and c // 2 + 3 < PREPARED:
                    w_max(dve, c // 2 + 3)
                dve.wait_ge(S["u_mid"], c + 1)
                dve.scalar_tensor_tensor(o, u[:, 0:UC_W], cols[:, CW + c:CW + c + 1], o, ALU.mult, ALU.add
                                         ).then_inc(S["u_tap"], 1)
                dve.wait_ge(S["u_tap"], c + 1)
                dve.scalar_tensor_tensor(o, u[:, 2:2 + UC_W], cols[:, CW + 6 * KD + c:CW + 6 * KD + c + 1], o,
                                         ALU.mult, ALU.add).then_inc(S["u_conv"], 1)
                if c in (3, 7, 11):
                    argument((c - 3) // 4)
            def scored(N):
                H, g, t, h = unit(N)
                _, kw, b0, _, edge = windows(g, t)
                l = lg[N % 2]
                c0, c1 = 0, kw
                if edge is not None:
                    c0, c1 = (edge[1], kw) if edge[0] == 0 else (0, edge[0])
                if N % STEPS == 0:
                    dve.wait_ge(ld_bias[H % 2], 16 * (H // 2 + 1 if H < 4 else 4))
                dve.wait_ge(S["a_score"], N + 1)
                if N >= 2:
                    dve.wait_ge(S["a_prob"], 2 * N - 2)
                if edge is not None:
                    chain(dve.memset(l[:, :, edge[0]:edge[1]], NEG))
                    settle()
                bias = (bwt if g < 2 else b2t)[H % 2][:, h:h + 3:2, b0 + c0:b0 + c1]
                dve.tensor_tensor(l[:, :, c0:c1], ps[:, 2 + N % 2, :].rearrange("p (x c) -> p x c", x=2)[:, :, c0:c1], bias,
                                  ALU.add).then_inc(S["a_biased"], 1)
                dve.wait_ge(S["a_biased"], N + 1)
                n = N // 2
                if h == 0 and n >= 3:
                    dve.wait_ge(ot_out[n % 3], 16 * ot_count(n - 3))
                dve.tensor_reduce(ot[n % 3][:, HW + h:HW + h + 3:2], l[:, :, 0:kw], AX.X, ALU.max, negate=True
                                  ).then_inc(S["a_max"], 1)

            def look_ahead(H, m):
                prepare(H, m, lambda b: w_power(dve, chain, settle, b), lambda b: w_low(dve, b), lambda b: w_max(dve, b))

            for m in range(NPT[0]):
                look_ahead(0, m)
            scored(0)
            for N in range(NSTEP):
                if N + 1 < NSTEP:
                    scored(N + 1)
                if N >= 1:
                    for H, m in MIX[N - 1]:
                        look_ahead(H, m)
            RT = math.sqrt(0.5)

            def filt(i, j):
                if j == 0:
                    dve.wait_ge(ld_dec, 16 * (i + 1))
                n = GEN0[i] + j
                h = hfb[n % 2]
                dve.wait_ge(S["f_gen"], n + 1)
                if n >= 2:
                    dve.wait_ge(S["f_ge"], n - 1)
                if j == 0:
                    chain(dve.tensor_tensor(h[:, 0:FQ], ps[:, n % 2, 0:FQ], dec[:, 0, :], ALU.mult))
                    dve.tensor_tensor(h[:, FQ:2 * FQ], ps[:, n % 2, FQ:2 * FQ], dec[:, ntile(i), :], ALU.mult
                                      ).then_inc(S["f_gen_used"], 1)
                else:
                    dve.tensor_tensor(h.rearrange("p (e c) -> p e c", e=2),
                                      ps[:, n % 2, :].rearrange("p (e c) -> p e c", e=2),
                                      dec[:, j:j + 1, :].to_broadcast([P, 2, FQ]), ALU.mult).then_inc(S["f_gen_used"], 1)

            def butterfly(i, x, src):
                m = 3 * i + x
                if m >= 2:
                    if x == 0:
                        u = uk[i - 1] + npair(i - 1)
                    elif x == 1:
                        u = uz[i - 1] + npair(i - 1) - 1
                    else:
                        u = uk[i] + npair(i) // 2
                    wait_ready(dve, u)
                a = fa[m % 2]
                nc_ = DFTS[ITEMS[i][0]]["nc"]
                w = nc_ * FQ
                f = src.rearrange("p t c -> p (t c)")
                e = e01.rearrange("p a c -> p (a c)")

                def A(c):
                    return a[:, c, 0:w]

                settle()
                if m >= 1:
                    dve.wait_ge(S["f_bf"], m)
                chain(dve.tensor_tensor(e[:, 0:2 * w], f[:, 0:2 * w], f[:, 2 * w:4 * w], ALU.add))
                chain(dve.tensor_tensor(a[:, A2R:A2N + 1, 0:w], f[:, 0:2 * w].rearrange("p (a c) -> p a c", a=2),
                                        f[:, 2 * w:4 * w].rearrange("p (a c) -> p a c", a=2), ALU.subtract))
                settle()
                e0, e1 = e[:, 0:w], e[:, w:2 * w]
                chain(dve.tensor_tensor(A(A0), e0, e1, ALU.add))
                chain(dve.tensor_tensor(A(A4), e0, e1, ALU.subtract))
                chain(dve.scalar_tensor_tensor(A(A1R), A(A2N), RT, f[:, 0:w], ALU.mult, ALU.add))
                chain(dve.scalar_tensor_tensor(A(A3R), A(A2N), -RT, f[:, 0:w], ALU.mult, ALU.add))
                chain(dve.scalar_tensor_tensor(A(A1N), e1, RT, f[:, 2 * w:3 * w], ALU.mult, ALU.add))
                dve.scalar_tensor_tensor(A(A3I), e1, -RT, f[:, 2 * w:3 * w], ALU.mult, ALU.add).then_inc(S["f_bf"], 1)

            def filter_butterfly(i, x):
                dve.wait_ge(S["f_ge"], GEN0[i + 1])
                butterfly(i, x, (tge, tgo)[x])

            def product(i):
                settle()
                for u in range(uk[i] + npair(i) - 3, uk[i] + npair(i) + 1):
                    wait_free(dve, u)
                for p in range(npair(i)):
                    u = uz[i] + p
                    n = PR0[i] + p
                    a = pq[n % 2]
                    wait_ready(dve, u)
                    if n >= 2:
                        dve.wait_ge(S["f_y"], n - 1)
                    re, im = ps[:, fbank(u), 0:FQ], ps[:, fbank(u), FQ:2 * FQ]
                    k = kf[:, p, :].rearrange("p (a c) -> p a c", a=2)
                    chain(dve.tensor_tensor(a[:, 0:2 * FQ].rearrange("p (a c) -> p a c", a=2),
                                            re.unsqueeze(1).to_broadcast([P, 2, FQ]), k, ALU.mult))
                    if p == 0:
                        chain(dve.tensor_tensor(a[:, 2 * FQ:3 * FQ], im, kfl, ALU.mult))
                        dve.tensor_tensor(a[:, 3 * FQ:4 * FQ], im, kf[:, 0, FQ:2 * FQ], ALU.mult
                                          ).then_inc(bank_free[fbank(u)], 1)
                    else:
                        dve.tensor_tensor(a[:, 2 * FQ:4 * FQ].rearrange("p (a c) -> p a c", a=2),
                                          im.unsqueeze(1).to_broadcast([P, 2, FQ]), k, ALU.mult
                                          ).then_inc(bank_free[fbank(u)], 1)
                    if i + 1 < NI and p < ntile(i + 1):
                        filt(i + 1, p)

            def recombine(i, ct, combined):
                s, q, o = ITEMS[i]
                L, w = LENS[s], DFTS[s]["w"]
                m = 2 * i + ct
                b0, b1 = iv0[m % 2], iv1[m % 2]
                u0, u1, u3, u2 = (ui[i] + 4 * ct + x for x in range(4))
                U, V, E, X = iv_u[:, 0:2 * w], iv_v[:, 0:2 * w], iv_a[:, 0:2 * w], iv_b[:, 0:2 * w]
                G = e01.rearrange("p a c -> p (a c)")[:, 0:2 * w]
                settle()
                dve.wait_ge(S["f_y"], PR0[i + 1])
                if m >= 1:
                    dve.wait_ge(S["f_post"], m)
                dve.wait_ge(S["f_bf"], combined)
                wait_free(dve, u0)
                chain(dve.tensor_tensor(E[:, 0:w], b0[:, 0:w], b0[:, w:2 * w], ALU.add))
                chain(dve.tensor_tensor(E[:, w:2 * w], b0[:, 0:w], b0[:, w:2 * w], ALU.subtract))
                wait_free(dve, u1)
                wait_ready(dve, u3)
                chain(dve.tensor_tensor(U, ps[:, fbank(u3), 0:2 * w], b1[:, 0:2 * w], ALU.add))
                dve.scalar_tensor_tensor(V, ps[:, fbank(u3), 0:2 * w], -1.0, b1[:, 0:2 * w], ALU.mult, ALU.add
                                         ).then_inc(bank_free[fbank(u3)], 1)
                settle()
                wait_ready(dve, u2)
                chain(dve.tensor_tensor(X, ps[:, fbank(u2), 0:2 * w], E, ALU.add))
                settle()
                dve.scalar_tensor_tensor(E, ps[:, fbank(u2), 0:2 * w], -1.0, E, ALU.mult, ALU.add
                                         ).then_inc(bank_free[fbank(u2)], 1)
                wait_free(dve, u3)
                chain(dve.tensor_tensor(G[:, 0:w], V[:, 0:w], U[:, w:2 * w], ALU.subtract))
                chain(dve.tensor_tensor(G[:, w:2 * w], V[:, 0:w], U[:, w:2 * w], ALU.add))
                wait_free(dve, u2)
                settle()
                chain(dve.tensor_tensor(yo[:, 0:w], X[:, 0:w], U[:, 0:w], ALU.add))
                chain(dve.tensor_tensor(yo[:, 2 * w:3 * w], E[:, 0:w], V[:, w:2 * w], ALU.subtract))
                chain(dve.scalar_tensor_tensor(yo[:, w:2 * w], G[:, 0:w], RT, E[:, w:2 * w], ALU.mult, ALU.add))
                chain(dve.scalar_tensor_tensor(yo[:, 3 * w:4 * w], G[:, w:2 * w], -RT, X[:, w:2 * w], ALU.mult, ALU.add))
                settle()
                z = zc[q % 2][:, ct, 0:L]
                sk = CS + KD * o + 2 * q + ct
                chain(dve.scalar_tensor_tensor(yo[:, 0:L], z, cols[:, sk:sk + 1], yo[:, 0:L], ALU.mult, ALU.add))
                settle()
                dve.wait_ge(S["ld_hx"], 16 * (i + 1))
                dve.tensor_tensor(z, yo[:, 0:L], hx[:, ct, 0:L], ALU.mult).then_inc(S["f_post"], 1)

            for j in range(ntile(0)):
                filt(0, j)
            filter_butterfly(0, 0)
            filter_butterfly(0, 1)
            dve.wait_ge(S["f_tz"], TR0[1])
            butterfly(0, 2, tz)
            for i in range(NI):
                product(i)
                if i + 1 == NI:
                    recombine(i, 0, 3 * i + 3)
                    recombine(i, 1, 3 * i + 3)
                    break
                if ITEMS[i][0] == 0:
                    filter_butterfly(i + 1, 0)
                    filter_butterfly(i + 1, 1)
                    recombine(i, 0, 3 * i + 5)
                    recombine(i, 1, 3 * i + 5)
                else:
                    recombine(i, 0, 3 * i + 3)
                    filter_butterfly(i + 1, 0)
                    filter_butterfly(i + 1, 1)
                    recombine(i, 1, 3 * i + 5)
                dve.wait_ge(S["f_tz"], TR0[i + 2])
                butterfly(i + 1, 2, tz)
            M0 = NB_U + NB_A
            w_max(dve, M0)
            w_max(dve, M0 + 1)
            w_split(dve, chain, settle, M0)
            w_split(dve, chain, settle, M0 + 1)
            w_max(dve, M0 + 2)
            w_split(dve, chain, settle, M0 + 2)
            w_max(dve, M0 + 3)
            dve.wait_ge(ld_hm[0], 16)

            def gate(t):
                n = POS["T", t, 0]
                for j in range(4):
                    m_waitfree(dve, POS["ga", j, t // 4])
                m_wait(dve, n)
                c = slice(P * t, P * t + P)
                dve.tensor_tensor(at[:, :, c], ps[:, n % 8, :].rearrange("p (j c) -> p j c", j=4), ga[:, :, c], ALU.mult
                                  ).then_inc(m_free[n % 8], 1)

            for t in range(NT):
                o, w = ogt[t % 2], wts[t % 2]
                acc, tmp = cmb[t % 2][:, 0, :], cmb[t % 2][:, 1, :]
                nm, den = o[:, :, :, HW:HW + HH], o[:, :, :, HW + HH:OW]
                low, total = (w[:, c:c + 8].rearrange("p (a h) -> p a h", a=2) for c in (0, 56))
                e, ed = (w[:, c:c + 24].rearrange("p (g a h) -> p g a h", g=3, a=2) for c in (8, 32))
                dve.wait_ge(ld_og[t % 2], 16 * (t // 2 + 1))
                chain(dve.tensor_tensor(low, nm[:, 0], nm[:, 1], ALU.min))
                settle()
                chain(dve.tensor_tensor(low, low, nm[:, 2], ALU.min))
                settle()
                dve.tensor_tensor(e, low.unsqueeze(1).to_broadcast([P, 3, 2, HH]), nm, ALU.subtract).then_inc(S["g_sc"], 1)
                dve.wait_ge(S["g_exp"], t + 1)
                chain(dve.tensor_tensor(ed, e, den, ALU.mult))
                settle()
                chain(dve.tensor_tensor(total, ed[:, 0], ed[:, 1], ALU.add))
                settle()
                chain(dve.tensor_tensor(total, total, ed[:, 2], ALU.add))
                settle()
                chain(dve.reciprocal(total, total))
                settle()
                dve.tensor_tensor(e, e, total.unsqueeze(1).to_broadcast([P, 3, 2, HH]), ALU.mult).then_inc(S["g_sc"], 1)
                dve.wait_ge(S["g_sc"], 2 * t + 2)
                if t >= 2:
                    m_wait(dve, POS["T", t - 2, 0])

                def weighted(dst, g):
                    chain(dve.tensor_tensor(dst.rearrange("p (a h c) -> p a h c", a=2, h=HH),
                                            o[:, g, :, 0:HW].rearrange("p a (h c) -> p a h c", h=HH),
                                            e[:, g].unsqueeze(3).to_broadcast([P, 2, HH, HD]), ALU.mult))

                weighted(acc, 0)
                weighted(tmp, 1)
                settle()
                chain(dve.tensor_tensor(acc, acc, tmp, ALU.add))
                settle()
                weighted(tmp, 2)
                settle()
                dve.tensor_tensor(acc, acc, tmp, ALU.add).then_inc(S["g_cmb"], 1)
                if t >= 1:
                    gate(t - 1)
            gate(NT - 1)
            w_split(dve, chain, settle, M0 + 3)
            w_max(dve, M0 + 4)

            def m_prepare(i):
                if i + 2 < NB_M:
                    w_split(dve, chain, settle, M0 + i + 2)
                if i + 3 < NB_M:
                    w_max(dve, M0 + i + 3)

            for ns, n in enumerate(GATES):
                x = ns % (KD * NSP)
                d, s = x // NSP, x % NSP
                c = slice(BANK * s, BANK * s + BANK)
                if ns in SPLITS:
                    m_prepare(2 + ns // 6)
                if ns == len(GATES) - NSP:
                    w_power(dve, chain, settle, NB - 2)
                    w_max(dve, NB - 1)
                m_waitfree(dve, n)
                if MT_GH <= n < MT_H:
                    dve.wait_ge(ld_hy[d], 16)
                    dve.tensor_tensor(hg[:, d, c], hg[:, d, c], sg[ns % 3], ALU.mult).then_inc(S["m_mul"], 1)
                    continue
                b = BRANCH[ns]
                m_wait(dve, b)
                if n < MT_GH:
                    if x == 0:
                        dve.wait_ge(S["g_cmb"], NT)
                    dve.tensor_tensor(mt[:, d, c], ps[:, b % 8, :], sg[ns % 3], ALU.mult).then_inc(m_free[b % 8], 1)
                else:
                    if x >= 1:
                        dve.wait_ge(S["m_acc"], x)
                    dve.tensor_tensor(gated, ps[:, b % 8, :], sg[ns % 3], ALU.mult).then_inc(m_free[b % 8], 1)
                    m_waitfree(dve, b)
                    dve.tensor_tensor(mt[:, d, c], mt[:, d, c], gated, ALU.add).then_inc(S["m_acc"], 1)
                    dve.wait_ge(S["m_acc"], x + 1)
                    chain(dve.tensor_reduce(mt_max[:, x:x + 1], mt[:, d, c], AX.X, ALU.max, apply_absolute_value=True))
            w_power(dve, chain, settle, NB - 1)
            dve.tensor_reduce(m_max, mt_max, AX.X, ALU.max).then_inc(mt_maxed, 1)
            dve.wait_ge(mt_all, 1)
            power_of_two(dve, chain, settle, m_descale, m_all_max, 2.0 ** -14)
            chain(dve.reciprocal(m_scale, m_descale))
            settle()
            dve.tensor_scalar(o_descale, wsc[:, NB - 4:NB], m_descale, None, ALU.mult).then_inc(mt_scaled, 1)
            w_low(dve, NB - 2)

            def merged_lo(t):
                c = slice(P * t, P * t + P)
                dve.wait_ge(mt_hi, t + 1)
                dve.scalar_tensor_tensor(m16[:, 1, :, c], mt[:, :, c], m_scale, m16[:, 0, :, c], ALU.mult, ALU.subtract
                                         ).then_inc(mt_lo, 1)

            merged_lo(0)
            w_low(dve, NB - 1)
            merged_lo(1)
            merged_lo(2)
            dve.wait_ge(mt_scaled, 1)
            dve.wait_ge(S["ld_gain"], 16)
            for t in range(NT):
                a = 4 * (t % 2)
                r = rstd2[:, t:t + 1]
                if t + 3 < NT:
                    merged_lo(t + 3)
                dve.wait_ge(S["o_sq"], 4 * t + 4)
                chain(dve.tensor_reduce(r, ssq2[:, a:a + 4], AX.X, ALU.add))
                settle()
                dve.tensor_scalar(r, r, 1.0 / D, EPS, ALU.mult, ALU.add).then_inc(S["o_r"], 1)
                dve.wait_ge(S["o_root"], t + 1)
                dve.reciprocal(r, r).then_inc(S["o_r"], 1)
                dve.wait_ge(S["o_r"], 2 * t + 2)
                if t >= 2:
                    dve.wait_ge(y_out[t % 2], 16 * (t // 2))
                y = yout[t % 2]
                settle()
                chain(dve.tensor_scalar(o_scale, o_descale, r, None, ALU.mult))
                settle()
                for half in range(2):
                    n = MT_O + 2 * t + half
                    for x in range(2):
                        j = 2 * half + x
                        op = dve.scalar_tensor_tensor(y[:, WC * j:WC * j + WC], ps[:, n % 8, WC * x:WC * x + WC],
                                                      o_scale[:, j:j + 1], gpost[:, WC * j:WC * j + WC], ALU.mult, ALU.mult)
                        if x == 0:
                            chain(op)
                        else:
                            op.then_inc(m_free[n % 8], 1)
                    m_waitfree(dve, n)
                dve.wait_ge(ld_xr[t % 2], 16 * (t // 2 + 1))
                dve.tensor_tensor(y, y, xres[t % 2], ALU.add).then_inc(S["o_y"], 1)


INPUTS = ("x_prompt", "x_sample", "rel_bias", "pre_norm_g", "post_norm_g", "w_in", "conv_w", "conv_b", "filt_w1", "filt_b1",
          "filt_w2", "filt_b2", "filt_w3", "filt_b3", "filt_w4", "filt_freq", "hyena_skip", "w_branch_a", "w_branch_h", "w_out")


def kernel(**inputs):
    import concourse.bacc as bacc
    from concourse.bass_utils import run_bass_kernel_spmd

    nc = bacc.Bacc("TRN2", target_bir_lowering=False, num_devices=1)
    arrays, ins, cst = {}, {}, {}
    for name in INPUTS:
        arrays["in_" + name] = np.ascontiguousarray(inputs[name])
        ins[name] = nc.dram_tensor("in_" + name, arrays["in_" + name].shape, F32, kind="ExternalInput").ap()
    for name, a in constants().items():
        arrays["c_" + name] = a
        cst[name] = nc.dram_tensor("c_" + name, a.shape, F32, kind="ExternalInput").ap()
    y_p = nc.dram_tensor("y_prompt", (1, SP, D), F32, kind="ExternalOutput").ap()
    y_s = nc.dram_tensor("y_sample", (1, SS, D), F32, kind="ExternalOutput").ap()
    build(nc, ins, cst, y_p, y_s)
    r = run_bass_kernel_spmd(nc, [arrays], core_ids=[0])
    return r.results[0]["y_prompt"], r.results[0]["y_sample"]
```
